# Optimizing a Trainium2 kernel written in Bass

```python
import math
import jax, jax.numpy as jnp
from jax import lax
import numpy as np

D_MODEL = 1024
BATCH = 1
SEQ = 256
DEPTH = 1

CHUNK = 64
EPS = 1e-6
ATT_HEADS = 8
ATT_KV_HEADS = 2
ATT_HEAD_DIM = 64
IDX_HEADS = 8
IDX_HEAD_DIM = 64
TOPK_MAX = 256
Q_BLOCK = 128
MLSTM_HEADS = 4
MLSTM_QK_DIM = 64
MLSTM_V_DIM = 128
CONV_WIDTH = 4
MIX_A = ATT_HEADS * ATT_HEAD_DIM
MIX_B = MLSTM_HEADS * MLSTM_V_DIM
D_FF = 2816
SPLIT_WIDTHS = (
    ATT_HEADS * ATT_HEAD_DIM,
    ATT_KV_HEADS * ATT_HEAD_DIM,
    ATT_KV_HEADS * ATT_HEAD_DIM,
    IDX_HEADS * IDX_HEAD_DIM,
    IDX_HEAD_DIM,
    IDX_HEADS,
    MIX_B,
    MIX_B,
    MLSTM_HEADS,
    MLSTM_HEADS,
    MIX_B,
    D_MODEL,
    D_MODEL,
)
D_IN = sum(SPLIT_WIDTHS)


def rms_norm(x, g):
    xf = x.astype(jnp.float32)
    y = xf * lax.rsqrt(jnp.mean(xf * xf, axis=-1, keepdims=True) + EPS)
    return (y * g.astype(jnp.float32)).astype(x.dtype)

def swiglu_ffn(x, g, w_gate, w_up, w_down):
    h = rms_norm(x, g)
    return (jax.nn.silu(h @ w_gate) * (h @ w_up)) @ w_down

def split_columns(p):
    parts, off = [], 0
    for w in SPLIT_WIDTHS:
        parts.append(p[..., off:off + w])
        off += w
    return parts

def dsa_attention(q, k, v, iq, ik, iw):
    B, S = q.shape[0], q.shape[1]
    k_sel = min(TOPK_MAX, S // 4)
    nb = S // Q_BLOCK
    reps = ATT_HEADS // ATT_KV_HEADS
    idx_scale = (IDX_HEAD_DIM ** -0.5) * (IDX_HEADS ** -0.5)
    att_scale = ATT_HEAD_DIM ** -0.5
    key_pos = jnp.arange(S)

    qb = q.reshape(B, nb, Q_BLOCK, ATT_KV_HEADS, reps, ATT_HEAD_DIM).transpose(1, 0, 2, 3, 4, 5)
    iqb = iq.reshape(B, nb, Q_BLOCK, IDX_HEADS, IDX_HEAD_DIM).transpose(1, 0, 2, 3, 4)
    iwb = iw.reshape(B, nb, Q_BLOCK, IDX_HEADS).transpose(1, 0, 2, 3)
    ids = jnp.arange(nb, dtype=jnp.int32)

    def block(args):
        q_blk, iq_blk, iw_blk, bi = args
        t = bi * Q_BLOCK + jnp.arange(Q_BLOCK)
        logits = jnp.einsum('bqhd,bsd->bqhs', iq_blk, ik)
        score = jnp.einsum('bqhs,bqh->bqs', jax.nn.relu(logits), iw_blk).astype(jnp.float32) * idx_scale
        limit = (t // CHUNK + 1) * CHUNK
        allowed = key_pos[None, :] < limit[:, None]
        score = jnp.where(allowed[None], score, -jnp.inf)
        top_s, top_i = lax.top_k(score, k_sel)
        valid = jnp.isfinite(top_s)
        kg = jax.vmap(lambda kb, ib: kb[ib])(k, top_i)
        vg = jax.vmap(lambda vb, ib: vb[ib])(v, top_i)
        s = jnp.einsum('bqgrd,bqkgd->bqgrk', q_blk, kg).astype(jnp.float32) * att_scale
        s = jnp.where(valid[:, :, None, None, :], s, -jnp.inf)
        p = jax.nn.softmax(s, axis=-1).astype(vg.dtype)
        return jnp.einsum('bqgrk,bqkgd->bqgrd', p, vg)

    o = lax.map(block, (qb, iqb, iwb, ids))
    return o.transpose(1, 0, 2, 3, 4, 5).reshape(B, S, MIX_A)

def mlstm_branch(xm, vm, ig, fg, o_pre, conv_w, conv_b, w_mq, w_mk, b_i, b_f, head_g):
    B, S, _ = xm.shape
    H, L = MLSTM_HEADS, CHUNK
    nc = S // L
    xpad = jnp.pad(xm, ((0, 0), (CONV_WIDTH - 1, 0), (0, 0)))
    xc = conv_b + xpad[:, 0:S] * conv_w[0]
    for j in range(1, CONV_WIDTH):
        xc = xc + xpad[:, j:j + S] * conv_w[j]
    xc = jax.nn.silu(xc).reshape(B, S, H, MLSTM_V_DIM)
    q = jnp.einsum('bshc,hcd->bshd', xc, w_mq).astype(jnp.float32) * (MLSTM_QK_DIM ** -0.5)
    k = jnp.einsum('bshc,hcd->bshd', xc, w_mk).astype(jnp.float32)
    v = vm.reshape(B, S, H, MLSTM_V_DIM).astype(jnp.float32)
    log_i = (ig + b_i).astype(jnp.float32)
    log_f = jax.nn.log_sigmoid((fg + b_f).astype(jnp.float32))

    def to_chunks(a):
        a = a.reshape((B, nc, L) + a.shape[2:])
        perm = (1, 0, 3, 2) + tuple(range(4, a.ndim))
        return a.transpose(perm)

    tril = jnp.tril(jnp.ones((L, L), dtype=bool))

    def step(carry, inp):
        C, n, m = carry
        qc, kc, vc, ic, fc = inp
        b = jnp.cumsum(fc, axis=-1)
        D = b[..., :, None] - b[..., None, :] + ic[..., None, :]
        D = jnp.where(tril, D, -jnp.inf)
        inter = b + m[..., None]
        m_t = jnp.maximum(jnp.max(D, axis=-1), inter)
        W = jnp.einsum('bhtd,bhsd->bhts', qc, kc) * jnp.exp(D - m_t[..., None])
        w_int = jnp.exp(inter - m_t)
        num = jnp.einsum('bhts,bhsv->bhtv', W, vc) + w_int[..., None] * jnp.einsum('bhtd,bhdv->bhtv', qc, C)
        den = jnp.sum(W, axis=-1) + w_int * jnp.einsum('bhtd,bhd->bht', qc, n)
        h = num / jnp.maximum(jnp.abs(den), jnp.exp(-m_t))[..., None]
        bL = b[..., -1]
        wk = bL[..., None] - b + ic
        m_new = jnp.maximum(bL + m, jnp.max(wk, axis=-1))
        ws = jnp.exp(wk - m_new[..., None])
        wc = jnp.exp(bL + m - m_new)
        C_new = wc[..., None, None] * C + jnp.einsum('bhs,bhsd,bhsv->bhdv', ws, kc, vc)
        n_new = wc[..., None] * n + jnp.einsum('bhs,bhsd->bhd', ws, kc)
        return (C_new, n_new, m_new), h

    init = (jnp.zeros((B, H, MLSTM_QK_DIM, MLSTM_V_DIM), jnp.float32),
            jnp.zeros((B, H, MLSTM_QK_DIM), jnp.float32),
            jnp.zeros((B, H), jnp.float32))
    _, hs = lax.scan(step, init, (to_chunks(q), to_chunks(k), to_chunks(v), to_chunks(log_i), to_chunks(log_f)))
    h = hs.transpose(1, 0, 3, 2, 4).reshape(B, S, H, MLSTM_V_DIM)
    h = rms_norm(h, head_g.reshape(H, MLSTM_V_DIM)).reshape(B, S, MIX_B).astype(xm.dtype)
    return h * jax.nn.sigmoid(o_pre)

def first_inputs(seed: int = 0) -> dict:
    key = jax.random.key(seed)
    ks = jax.random.split(key, 32)
    f32 = jnp.float32

    def nrm(k, shape, fan_in):
        return jax.random.normal(k, shape, f32) * (fan_in ** -0.5)

    def gain(k, shape):
        return 1.0 + 0.02 * jax.random.normal(k, shape, f32)

    Ld = DEPTH
    return {
        "x": jax.random.normal(ks[0], (BATCH, SEQ, D_MODEL), f32),
        "ffn1_norm": gain(ks[1], (Ld, D_MODEL)),
        "ffn1_w_gate": nrm(ks[2], (Ld, D_MODEL, D_FF), D_MODEL),
        "ffn1_w_up": nrm(ks[3], (Ld, D_MODEL, D_FF), D_MODEL),
        "ffn1_w_down": nrm(ks[4], (Ld, D_FF, D_MODEL), D_FF),
        "mix_norm": gain(ks[5], (Ld, D_MODEL)),
        "w_in": nrm(ks[6], (Ld, D_MODEL, D_IN), D_MODEL),
        "q_norm": gain(ks[7], (Ld, ATT_HEAD_DIM)),
        "k_norm": gain(ks[8], (Ld, ATT_HEAD_DIM)),
        "idx_k_norm": gain(ks[9], (Ld, IDX_HEAD_DIM)),
        "conv_w": nrm(ks[10], (Ld, CONV_WIDTH, MIX_B), CONV_WIDTH),
        "conv_b": 0.02 * jax.random.normal(ks[11], (Ld, MIX_B), f32),
        "w_mq": nrm(ks[12], (Ld, MLSTM_HEADS, MLSTM_V_DIM, MLSTM_QK_DIM), MLSTM_V_DIM),
        "w_mk": nrm(ks[13], (Ld, MLSTM_HEADS, MLSTM_V_DIM, MLSTM_QK_DIM), MLSTM_V_DIM),
        "b_i": 0.1 * jax.random.normal(ks[14], (Ld, MLSTM_HEADS), f32),
        "b_f": 3.0 + 0.1 * jax.random.normal(ks[15], (Ld, MLSTM_HEADS), f32),
        "m_head_norm": gain(ks[16], (Ld, MIX_B)),
        "w_proj_a": nrm(ks[17], (Ld, MIX_A, D_MODEL), MIX_A),
        "w_proj_b": nrm(ks[18], (Ld, MIX_B, D_MODEL), MIX_B),
        "w_out": nrm(ks[19], (Ld, D_MODEL, D_MODEL), D_MODEL),
        "ffn2_norm": gain(ks[20], (Ld, D_MODEL)),
        "ffn2_w_gate": nrm(ks[21], (Ld, D_MODEL, D_FF), D_MODEL),
        "ffn2_w_up": nrm(ks[22], (Ld, D_MODEL, D_FF), D_MODEL),
        "ffn2_w_down": nrm(ks[23], (Ld, D_FF, D_MODEL), D_FF),
    }

def first_block(x, ffn1_norm, ffn1_w_gate, ffn1_w_up, ffn1_w_down, mix_norm, w_in,
              q_norm, k_norm, idx_k_norm, conv_w, conv_b, w_mq, w_mk, b_i, b_f,
              m_head_norm, w_proj_a, w_proj_b, w_out, ffn2_norm, ffn2_w_gate,
              ffn2_w_up, ffn2_w_down):
    B, S, _ = x.shape
    for l in range(DEPTH):
        x = x + 0.5 * swiglu_ffn(x, ffn1_norm[l], ffn1_w_gate[l], ffn1_w_up[l], ffn1_w_down[l])
        h = rms_norm(x, mix_norm[l])
        (aq, ak, av, iq, ik, iw, mx, mv, mi, mf, mo, ga, gb) = split_columns(h @ w_in[l])
        q = rms_norm(aq.reshape(B, S, ATT_HEADS, ATT_HEAD_DIM), q_norm[l])
        k = rms_norm(ak.reshape(B, S, ATT_KV_HEADS, ATT_HEAD_DIM), k_norm[l])
        v = av.reshape(B, S, ATT_KV_HEADS, ATT_HEAD_DIM)
        iq = iq.reshape(B, S, IDX_HEADS, IDX_HEAD_DIM)
        ik = rms_norm(ik, idx_k_norm[l])
        ya = dsa_attention(q, k, v, iq, ik, iw)
        yb = mlstm_branch(mx, mv, mi, mf, mo, conv_w[l], conv_b[l], w_mq[l], w_mk[l],
                          b_i[l], b_f[l], m_head_norm[l])
        merged = jax.nn.sigmoid(ga) * (ya @ w_proj_a[l]) + jax.nn.sigmoid(gb) * (yb @ w_proj_b[l])
        x = x + merged @ w_out[l]
        x = x + 0.5 * swiglu_ffn(x, ffn2_norm[l], ffn2_w_gate[l], ffn2_w_up[l], ffn2_w_down[l])
    return x


D_MIX = D_MODEL
N_ATTN_HEADS = 8
ATTN_HEAD_DIM = 64
D_ATTN = N_ATTN_HEADS * ATTN_HEAD_DIM
D_POOL = D_MIX - D_ATTN
POOL_WINDOWS = (2, 4, 8, 16)
N_POOL_GROUPS = len(POOL_WINDOWS)
POOL_GROUP_DIM = D_POOL // N_POOL_GROUPS
D_IN_2 = 3 * D_ATTN + D_POOL
MOBA_BLOCK = 256
MOBA_TOPK = 3
Q_CHUNK = 32
N_MEM = 256
XA_HEADS = 4
XA_HEAD_DIM = D_MODEL // XA_HEADS
MACARON_WEIGHT = 0.5
RMS_EPS = 1e-6


def rmsnorm(x, g):
    xf = x.astype(jnp.float32)
    r = lax.rsqrt(jnp.mean(xf * xf, axis=-1, keepdims=True) + RMS_EPS)
    return (xf * r).astype(x.dtype) * g

def swiglu(h, w_gate, w_up, w_down):
    return (jax.nn.silu(h @ w_gate) * (h @ w_up)) @ w_down

def alibi_slopes(n_heads):
    s = 2.0 ** (-8.0 * np.arange(1, n_heads + 1) / n_heads)
    return jnp.asarray(s, dtype=jnp.float32)

def moba_attention(q, k, v, slopes):
    B, H, S, dh = q.shape
    L = MOBA_BLOCK
    s_pad = ((S + L - 1) // L) * L
    pad = s_pad - S
    kp = jnp.pad(k, ((0, 0), (0, 0), (0, pad), (0, 0)))
    vp = jnp.pad(v, ((0, 0), (0, 0), (0, pad), (0, 0)))
    nb = s_pad // L
    n_sel = min(MOBA_TOPK, nb)
    kb = kp.reshape(B, H, nb, L, dh)
    vb = vp.reshape(B, H, nb, L, dh)
    k_mean = jnp.mean(kb, axis=3)
    qs = q * (dh ** -0.5)
    bi = jnp.arange(B)[:, None, None, None]
    hi = jnp.arange(H)[None, :, None, None]
    lpos = jnp.arange(L)
    slot = jnp.arange(n_sel)
    blk_ids = jnp.arange(nb)
    n_chunks = S // Q_CHUNK

    def chunk(c):
        start = c * Q_CHUNK
        qc = lax.dynamic_slice_in_dim(qs, start, Q_CHUNK, axis=2)
        qpos = start + jnp.arange(Q_CHUNK)
        qpos_f = qpos.astype(jnp.float32)
        own = start // L
        gate = jnp.einsum('bhqd,bhnd->bhqn', qc, k_mean).astype(jnp.float32)
        gate = jnp.where(blk_ids < own, gate, -jnp.inf)
        _, idx = lax.top_k(gate, n_sel)
        slot_ok = slot < own
        k_sel = kb[bi, hi, idx]
        v_sel = vb[bi, hi, idx]
        kpos_sel = (idx[..., None] * L + lpos).astype(jnp.float32)
        s_sel = (jnp.einsum('bhqd,bhqrld->bhqrl', qc, k_sel).astype(jnp.float32)
                 - slopes[:, None, None, None] * (qpos_f[:, None, None] - kpos_sel))
        s_sel = jnp.where(slot_ok[:, None], s_sel, -jnp.inf)
        k_own = lax.dynamic_index_in_dim(kb, own, axis=2, keepdims=False)
        v_own = lax.dynamic_index_in_dim(vb, own, axis=2, keepdims=False)
        kpos_own = own * L + lpos
        s_own = (jnp.einsum('bhqd,bhld->bhql', qc, k_own).astype(jnp.float32)
                 - slopes[:, None, None] * (qpos_f[:, None] - kpos_own.astype(jnp.float32)[None, :]))
        s_own = jnp.where(kpos_own[None, :] <= qpos[:, None], s_own, -jnp.inf)
        scores = jnp.concatenate([s_sel.reshape(B, H, Q_CHUNK, n_sel * L), s_own], axis=-1)
        p = jax.nn.softmax(scores, axis=-1)
        p_sel = p[..., :n_sel * L].reshape(B, H, Q_CHUNK, n_sel, L).astype(v.dtype)
        p_own = p[..., n_sel * L:].astype(v.dtype)
        return (jnp.einsum('bhqrl,bhqrld->bhqd', p_sel, v_sel)
                + jnp.einsum('bhql,bhld->bhqd', p_own, v_own))

    outs = lax.map(chunk, jnp.arange(n_chunks))
    return outs.transpose(1, 2, 0, 3, 4).reshape(B, H, S, dh)

def multiscale_pool(p, pool_w, pool_scale):
    B, S, C = p.shape
    pf = p.reshape(B, S, N_POOL_GROUPS, POOL_GROUP_DIM).astype(jnp.float32)
    cs = jnp.concatenate([jnp.zeros((B, 1, N_POOL_GROUPS, POOL_GROUP_DIM), jnp.float32),
                          lax.cumsum(pf, axis=1)], axis=1)
    t = jnp.arange(S)
    outs = []
    for g, w in enumerate(POOL_WINDOWS):
        lo = jnp.maximum(t + 1 - w, 0)
        cnt = (t + 1 - lo).astype(jnp.float32)
        mean = (cs[:, 1:, g] - cs[:, lo, g]) / cnt[None, :, None]
        outs.append(mean - pf[:, :, g])
    d = jnp.stack(outs, axis=2).astype(p.dtype)
    y = jnp.einsum('bsgc,gcd->bsgd', d, pool_w)
    return y.reshape(B, S, C) * pool_scale

def memory_cross_attention(h, mem_n, wq, wkv, wo):
    B, S, _ = h.shape
    M = mem_n.shape[1]
    q = (h @ wq).reshape(B, S, XA_HEADS, XA_HEAD_DIM)
    kv = mem_n @ wkv
    k = kv[..., :D_MODEL].reshape(B, M, XA_HEADS, XA_HEAD_DIM)
    v = kv[..., D_MODEL:].reshape(B, M, XA_HEADS, XA_HEAD_DIM)
    s = jnp.einsum('bshd,bmhd->bhsm', q, k).astype(jnp.float32) * (XA_HEAD_DIM ** -0.5)
    p = jax.nn.softmax(s, axis=-1).astype(v.dtype)
    o = jnp.einsum('bhsm,bmhd->bshd', p, v).reshape(B, S, XA_HEADS * XA_HEAD_DIM)
    return o @ wo

def second_inputs(seed: int = 0) -> dict:
    key = jax.random.key(seed)
    ks = jax.random.split(key, 24)

    def nrm(k, shape, fan_in):
        return jax.random.normal(k, shape, jnp.float32) * fan_in ** -0.5

    def gain(k, shape):
        return 1.0 + 0.1 * jax.random.normal(k, shape, jnp.float32)

    L = DEPTH
    return {
        "x": jax.random.normal(ks[0], (BATCH, SEQ, D_MODEL), jnp.float32),
        "mem": jax.random.normal(ks[1], (BATCH, N_MEM, D_MODEL), jnp.float32),
        "ffn1_pre_g": gain(ks[2], (L, D_MODEL)),
        "ffn1_w_gate": nrm(ks[3], (L, D_MODEL, D_FF), D_MODEL),
        "ffn1_w_up": nrm(ks[4], (L, D_MODEL, D_FF), D_MODEL),
        "ffn1_w_down": nrm(ks[5], (L, D_FF, D_MODEL), D_FF),
        "ffn1_post_g": gain(ks[6], (L, D_MODEL)),
        "mix_pre_g": gain(ks[7], (L, D_MODEL)),
        "w_in": nrm(ks[8], (L, D_MODEL, D_IN_2), D_MODEL),
        "pool_w": nrm(ks[9], (L, N_POOL_GROUPS, POOL_GROUP_DIM, POOL_GROUP_DIM), POOL_GROUP_DIM),
        "pool_scale": gain(ks[10], (L, D_POOL)),
        "w_out": nrm(ks[11], (L, D_MIX, D_MODEL), D_MIX),
        "mix_post_g": gain(ks[12], (L, D_MODEL)),
        "xa_pre_g": gain(ks[13], (L, D_MODEL)),
        "mem_g": gain(ks[14], (L, D_MODEL)),
        "xa_wq": nrm(ks[15], (L, D_MODEL, XA_HEADS * XA_HEAD_DIM), D_MODEL),
        "xa_wkv": nrm(ks[16], (L, D_MODEL, 2 * XA_HEADS * XA_HEAD_DIM), D_MODEL),
        "xa_wo": nrm(ks[17], (L, XA_HEADS * XA_HEAD_DIM, D_MODEL), XA_HEADS * XA_HEAD_DIM),
        "xa_post_g": gain(ks[18], (L, D_MODEL)),
        "ffn2_pre_g": gain(ks[19], (L, D_MODEL)),
        "ffn2_w_gate": nrm(ks[20], (L, D_MODEL, D_FF), D_MODEL),
        "ffn2_w_up": nrm(ks[21], (L, D_MODEL, D_FF), D_MODEL),
        "ffn2_w_down": nrm(ks[22], (L, D_FF, D_MODEL), D_FF),
        "ffn2_post_g": gain(ks[23], (L, D_MODEL)),
    }

def second_block(x, mem, ffn1_pre_g, ffn1_w_gate, ffn1_w_up, ffn1_w_down, ffn1_post_g,
              mix_pre_g, w_in, pool_w, pool_scale, w_out, mix_post_g,
              xa_pre_g, mem_g, xa_wq, xa_wkv, xa_wo, xa_post_g,
              ffn2_pre_g, ffn2_w_gate, ffn2_w_up, ffn2_w_down, ffn2_post_g):
    B, S, _ = x.shape
    slopes = alibi_slopes(N_ATTN_HEADS)
    for l in range(DEPTH):
        h = rmsnorm(x, ffn1_pre_g[l])
        f = swiglu(h, ffn1_w_gate[l], ffn1_w_up[l], ffn1_w_down[l])
        x = x + MACARON_WEIGHT * rmsnorm(f, ffn1_post_g[l])

        h = rmsnorm(x, mix_pre_g[l])
        proj = h @ w_in[l]
        q = proj[..., :D_ATTN]
        k = proj[..., D_ATTN:2 * D_ATTN]
        v = proj[..., 2 * D_ATTN:3 * D_ATTN]
        p_in = proj[..., 3 * D_ATTN:]
        to_heads = lambda t: t.reshape(B, S, N_ATTN_HEADS, ATTN_HEAD_DIM).transpose(0, 2, 1, 3)
        attn = moba_attention(to_heads(q), to_heads(k), to_heads(v), slopes)
        attn = attn.transpose(0, 2, 1, 3).reshape(B, S, D_ATTN)
        pool = multiscale_pool(p_in, pool_w[l], pool_scale[l])
        y = jnp.concatenate([attn, pool], axis=-1) @ w_out[l]
        x = x + rmsnorm(y, mix_post_g[l])

        h = rmsnorm(x, xa_pre_g[l])
        mem_n = rmsnorm(mem, mem_g[l])
        c = memory_cross_attention(h, mem_n, xa_wq[l], xa_wkv[l], xa_wo[l])
        x = x + rmsnorm(c, xa_post_g[l])

        h = rmsnorm(x, ffn2_pre_g[l])
        f = swiglu(h, ffn2_w_gate[l], ffn2_w_up[l], ffn2_w_down[l])
        x = x + MACARON_WEIGHT * rmsnorm(f, ffn2_post_g[l])
    return x


def setup_inputs(seed=0):
    out = dict(first_inputs(seed))
    for name, value in second_inputs(seed + 1).items():
        if name != "x":
            out[name + "_2"] = value
    return out


def reference(
    x, ffn1_norm, ffn1_w_gate, ffn1_w_up, ffn1_w_down, mix_norm, w_in, q_norm, k_norm,
    idx_k_norm, conv_w, conv_b, w_mq, w_mk, b_i, b_f, m_head_norm, w_proj_a, w_proj_b, w_out,
    ffn2_norm, ffn2_w_gate, ffn2_w_up, ffn2_w_down, mem_2, ffn1_pre_g_2, ffn1_w_gate_2,
    ffn1_w_up_2, ffn1_w_down_2, ffn1_post_g_2, mix_pre_g_2, w_in_2, pool_w_2, pool_scale_2,
    w_out_2, mix_post_g_2, xa_pre_g_2, mem_g_2, xa_wq_2, xa_wkv_2, xa_wo_2, xa_post_g_2,
    ffn2_pre_g_2, ffn2_w_gate_2, ffn2_w_up_2, ffn2_w_down_2, ffn2_post_g_2,
):
    x = first_block(
        x, ffn1_norm, ffn1_w_gate, ffn1_w_up, ffn1_w_down, mix_norm, w_in, q_norm, k_norm,
        idx_k_norm, conv_w, conv_b, w_mq, w_mk, b_i, b_f, m_head_norm, w_proj_a, w_proj_b,
        w_out, ffn2_norm, ffn2_w_gate, ffn2_w_up, ffn2_w_down,
    )
    return second_block(
        x, mem_2, ffn1_pre_g_2, ffn1_w_gate_2, ffn1_w_up_2, ffn1_w_down_2, ffn1_post_g_2,
        mix_pre_g_2, w_in_2, pool_w_2, pool_scale_2, w_out_2, mix_post_g_2, xa_pre_g_2, mem_g_2,
        xa_wq_2, xa_wkv_2, xa_wo_2, xa_post_g_2, ffn2_pre_g_2, ffn2_w_gate_2, ffn2_w_up_2,
        ffn2_w_down_2, ffn2_post_g_2,
    )


_drawn_inputs = setup_inputs


def setup_inputs(seed=0):
    import zlib

    import numpy as np

    out = dict(_drawn_inputs(seed))
    spreads = {}
    factors = {'ffn1_norm': 3.558,
     'q_norm': 24.701,
     'k_norm': 23.897,
     'idx_k_norm': 4.32,
     'conv_b': 4.662,
     'b_i': 64.0,
     'b_f': 64.0,
     'm_head_norm': 35.251,
     'ffn2_norm': 6.78,
     'ffn1_pre_g_2': 8.0,
     'ffn1_post_g_2': 8.0,
     'mix_pre_g_2': 8.0,
     'pool_scale_2': 8.0,
     'mix_post_g_2': 8.0,
     'xa_pre_g_2': 8.0,
     'mem_g_2': 6.81,
     'xa_post_g_2': 8.0,
     'ffn2_pre_g_2': 8.0,
     'ffn2_post_g_2': 26.138}
    for name, (base, spread) in spreads.items():
        noise = np.random.default_rng([zlib.crc32(name.encode()), seed]).standard_normal(out[name].shape)
        drawn = base * np.exp(spread * noise) if base else spread * noise
        out[name] = __import__('jax').numpy.asarray(drawn.astype(out[name].dtype))
    for name, factor in factors.items():
        out[name] = (out[name] * factor).astype(out[name].dtype)
    return out
```

```python
from contextlib import ExitStack

import concourse.bass as bass
import concourse.mybir as mybir
import numpy as np

F32 = mybir.dt.float32
F32R = mybir.dt.float32r
ACT = mybir.ActivationFunctionType
ALU = mybir.AluOpType
AX_X = mybir.AxisListType.X

P = 128
S = 256
T = S // P
D = 1024
DC = D // P
EPS = 1e-6
MASKED = -1e30
UNPICKED = -3e38
PICKED = -3.4e38
TOPK = S // 4
UNIT = 2048
STAGES = 3
SPLITS = 3
DEBUG = False


class Engine:

    def __init__(self, sem):
        self.sem, self.count, self.items, self.known = sem, 0, [], {}

    def wait(self, *marks):
        for m in marks:
            if m is None:
                continue
            if isinstance(m, list):
                self.wait(*m)
                continue
            sem, value = m
            if self.known.get(id(sem), 0) < value:
                self.known[id(sem)] = value
                self.items.append(lambda e, sem=sem, value=value: e.wait_ge(sem, value))

    def do(self, emit, *waits, signal=True):
        self.wait(*waits)
        if not signal:
            self.items.append(emit)
            return None
        self.count += 1
        self.items.append(lambda e: emit(e).then_inc(self.sem, 1))
        return (self.sem, self.count)

    def dma(self, out, in_, sem, used, *waits):
        self.wait(*waits)
        used[id(sem)] = used.get(id(sem), 0) + 16
        self.items.append(lambda e: e.dma_start(out, in_).then_inc(sem, 16))
        return (sem, used[id(sem)])

    def run(self, e):
        for item in self.items:
            item(e)


def bcast(ap, axis, n):
    a = ap.unsqueeze(axis)
    shape = list(a.shape)
    shape[axis] = n
    return a.to_broadcast(shape)


PARAM_COLS = {}


def param_columns():
    at = 0
    for name, n in (("ffn1_norm", 8), ("mix_norm", 8), ("ffn2_norm", 8), ("ffn1_pre_g_2", 8), ("mix_pre_g_2", 8),
                    ("xa_pre_g_2", 8), ("mem_g_2", 8), ("ffn2_pre_g_2", 8), ("q_norm", 1), ("k_norm", 1),
                    ("idx_k_norm", 1), ("conv_w", 16), ("conv_b", 4), ("pool_scale_2", 4), ("b_i", 1), ("b_f", 1)):
        PARAM_COLS[name] = (at, at + n)
        at += n
    return at


N_PARAMS = param_columns()
CONST_COLS = {"ident": (0, 128), "causal": (128, 384), "chunked": (384, 640), "alibi": (640, 2688),
              "inv_count": (2688, 3712), "head_rows": (3712, 4224)}
N_CONSTS = 4224


def shape_constants():
    c = np.zeros((P, N_CONSTS), np.float32)
    r = np.arange(P)[:, None]
    col = np.arange(P)[None, :]
    c[:, 0:128] = np.eye(P)
    causal = np.concatenate([np.zeros((P, P)), np.where(col <= r, 0.0, MASKED)], 1)
    c[:, 128:384] = causal
    c[:, 512:640] = np.where(col < (r // 64 + 1) * 64, 0.0, UNPICKED)
    dist = np.arange(S)[None, :] - (r + P)
    for group in range(2):
        for half in range(2):
            for jj in range(2):
                head = 2 * (2 * group + jj) + half
                at = 640 + ((group * 2 + half) * 2 + jj) * S
                slope = np.float32(2.0 ** (-8.0 * (head + 1) / 8))
                c[:, at:at + S] = np.where(dist <= 0, slope * dist, MASKED)
    for g, w in enumerate((2, 4, 8, 16)):
        c[:, 2688 + g * S:2688 + (g + 1) * S] = 1.0 / np.minimum(np.arange(S) + 1, w)
    for h in range(4):
        c[h, 3712 + h * P:3712 + (h + 1) * P] = 1.0
    return c


def build(nc, d, out, dbg):
    ctx = ExitStack()
    with ctx:
        def sb(scope, name, shape, dt=F32):
            return scope.enter_context(nc.sbuf_tensor(name, shape, dt))

        def sem(name):
            return ctx.enter_context(nc.semaphore(name))

        pe, act, dve, pool, sp = (Engine(sem("s_" + n)) for n in ("pe", "act", "dve", "pool", "sp"))
        used = {}
        s_stage = [sem(f"s_stage{i}") for i in range(STAGES)]
        s_x, s_par, s_out = sem("s_x"), sem("s_par"), sem("s_out")
        s_small = {n: sem("s_" + n) for n in ("mix1", "mix2", "mem", "post0", "post1", "post2", "post3")}

        x = sb(ctx, "x", [P, T, D])
        xr = sb(ctx, "xr", [P, T, D])
        h_hi = sb(ctx, "h_hi", [P, DC, S], F32R)
        h_lo = sb(ctx, "h_lo", [P, DC, S], F32R)
        stage = [sb(ctx, f"stage{i}", [P, UNIT]) for i in range(STAGES)]
        w_hi = [sb(ctx, f"w_hi{i}", [P, UNIT], F32R) for i in range(SPLITS)]
        w_lo = [sb(ctx, f"w_lo{i}", [P, UNIT], F32R) for i in range(SPLITS)]
        par = sb(ctx, "par", [P, N_PARAMS])
        ident = sb(ctx, "ident", [P, P])
        causal = sb(ctx, "causal", [P, 2 * P])
        stat = sb(ctx, "stat", [P, 8])
        half_pow = sb(ctx, "half_pow", [P, 32])
        pairs = [ctx.enter_context(nc.psum_tensor(f"pair{i}", [P, 1024], F32)) for i in range(4)]
        pair_free = [(i, []) for i in range(4)]

        def take_pair():
            i, waits = pair_free.pop(0)
            return i, pairs[i], waits

        def give_pair(i, *marks):
            pair_free.append((i, list(marks)))

        def col(name, c=0, rows=P):
            a = PARAM_COLS[name][0] + c
            return par[0:rows, a:a + 1]

        m_x = [sp.dma(x[:, t, :], d["x"][t * P:(t + 1) * P, :], s_x, used) for t in range(T)]
        m_x = [m_x[-1]] * T
        pool.dma(par[:], d["params"], s_par, used)
        pool.dma(ident[:], d["consts"][:, 0:128], s_par, used)
        m_par = pool.dma(causal[:], d["consts"][:, 128:384], s_par, used)
        m_pow = pool.do(lambda e: e.memset(half_pow[:], -0.5))

        plan = []

        def plan_block(w, K, n0, nw, rows=None):
            kc = min(K, UNIT // nw)
            for k0 in range(0, K, kc):
                k1 = min(K, k0 + kc)
                if rows:
                    srcs = rows(k0, k1, n0, nw)
                else:
                    v = w.rearrange("(k p) n -> p k n", p=P)
                    srcs = [(slice(0, P), slice(0, nw), v[:, k0:k1, n0:n0 + nw])]
                plan.append((w, k0, k1, n0, nw, srcs))

        state = {"next": 0, "split": 0, "loaded": 0}
        m_load, m_hi, m_lo, m_used = {}, {}, {}, {}

        def load_unit(u):
            _, k0, k1, _, nw, srcs = plan[u]
            dst = stage[u % STAGES][:, 0:(k1 - k0) * nw].rearrange("p (k n) -> p k n", n=nw)
            held = [m_hi[u - STAGES], m_lo[u - STAGES]] if u >= STAGES else []
            for parts, cols, src in srcs:
                m_load[u] = sp.dma(dst[parts, :, cols], src, s_stage[u % STAGES], used, *held)

        def split_unit(u):
            _, k0, k1, _, nw, _ = plan[u]
            n = (k1 - k0) * nw
            src, hi, lo = stage[u % STAGES][:, 0:n], w_hi[u % SPLITS][:, 0:n], w_lo[u % SPLITS][:, 0:n]
            held = m_used[u - SPLITS] if u >= SPLITS else None
            m_hi[u] = act.do(lambda e: e.copy(hi, src), m_load[u], held)
            m_lo[u] = dve.do(lambda e: e.tensor_tensor(lo, src, hi.bitcast(F32), ALU.subtract), m_hi[u], held)
            if state["loaded"] < len(plan):
                load_unit(state["loaded"])
                state["loaded"] += 1

        def take_unit(w, k0, n0):
            u = state["next"]
            assert plan[u][0] is w and plan[u][1] == k0 and plan[u][3] == n0, (u, k0, n0)
            state["next"] += 1
            while state["split"] < min(len(plan), u + SPLITS):
                split_unit(state["split"])
                state["split"] += 1
            return u

        def block(w, K, n0, nw, a_hi, a_lo, ready, form):
            i, ps, free = take_pair()
            kc = min(K, UNIT // nw)
            done = None
            begun = set()
            for k0 in range(0, K, kc):
                k1 = min(K, k0 + kc)
                u = take_unit(w, k0, n0)
                hi = w_hi[u % SPLITS][:, 0:(k1 - k0) * nw].rearrange("p (k n) -> p k n", n=nw)
                lo = w_lo[u % SPLITS][:, 0:(k1 - k0) * nw].rearrange("p (k n) -> p k n", n=nw)
                pe.wait(free, m_hi[u], m_lo[u])
                for k in range(k0, k1):
                    pe.wait(ready[k])
                    for g in range(T if form == "rows" else nw // P):
                        if form == "rows":
                            o = ps[:, g * 512:g * 512 + nw]
                            bank = g
                            ops = [(a_hi[:, k, g * P:(g + 1) * P], hi[:, k - k0, :]),
                                   (a_lo[:, k, g * P:(g + 1) * P], hi[:, k - k0, :]),
                                   (a_hi[:, k, g * P:(g + 1) * P], lo[:, k - k0, :])]
                        else:
                            o = ps[:, g * S:(g + 1) * S]
                            bank = g // 2
                            ops = [(hi[:, k - k0, g * P:(g + 1) * P], a_hi[:, k, :]),
                                   (hi[:, k - k0, g * P:(g + 1) * P], a_lo[:, k, :]),
                                   (lo[:, k - k0, g * P:(g + 1) * P], a_hi[:, k, :])]
                        for j, (l, r) in enumerate(ops):
                            first = bank not in begun
                            begun.add(bank)
                            last_in_unit = k == k1 - 1 and g == (T if form == "rows" else nw // P) - 1 and j == 2
                            done = pe.do(lambda e, o=o, l=l, r=r, first=first, stop=(k == K - 1 and j == 2):
                                         e.matmul(o, l, r, start=first, stop=stop, skip_group_check=True),
                                         signal=last_in_unit)
                m_used[u] = done
            return i, ps, done

        def mm(o, l, r, start, stop, *waits, signal=False):
            return pe.do(lambda e: e.matmul(o, l, r, start=start, stop=stop, skip_group_check=True), *waits, signal=signal)

        def turn(o, i_, *waits, signal=False):
            n = i_.shape[0]
            return pe.do(lambda e: e.transpose(o, i_, ident[0:n, 0:n]), *waits, signal=signal)

        def inverse_root(r, ss, n, width, *waits):
            a = pool.do(lambda e: e.tensor_scalar(r, ss, 1.0 / width, EPS, ALU.mult, ALU.add), *waits)
            return pool.do(lambda e: e.tensor_tensor(r, r, half_pow[:, 0:n], ALU.pow), a, m_pow)

        def split_whole(hi, lo, src, *waits):
            a = act.do(lambda e: e.copy(hi, src), *waits)
            b = dve.do(lambda e: e.tensor_tensor(lo, src, hi.bitcast(F32), ALU.subtract), a, *waits)
            return [a, b]

        def split_gained(hi, lo, ps, gains, done, *waits):
            marks = []
            for bank in range(2):
                cs = (2 * bank, 2 * bank + 1)
                for c in cs:
                    a = act.do(lambda e, c=c: e.activation(hi[:, c, :], ps[:, c * S:(c + 1) * S], ACT.Copy, scale=gains[c]), done[bank], *waits)
                for c in cs:
                    b = dve.do(lambda e, c=c: e.scalar_tensor_tensor(
                        lo[:, c, :], ps[:, c * S:(c + 1) * S], gains[c], hi[:, c, :].bitcast(F32), ALU.mult, ALU.subtract), a, *waits)
                    marks.append([a, b])
            return marks

        gain_buf = []
        norm_free = [[]]

        def norm_cols(src, gain, hi, lo, m_src, m_free=()):
            m_r = []
            for t in range(T):
                ss, r, row, o = stat[:, 2 * t:2 * t + 1], stat[:, 2 * t + 1:2 * t + 2], src[:, t, :], xr[:, t, :]
                if t == 0:
                    a = act.do(lambda e, row=row, o=o, ss=ss: e.activation(o, row, ACT.Square, accum_out=ss), m_src[t], norm_free[0])
                else:
                    a = dve.do(lambda e, row=row, o=o, ss=ss: e.tensor_tensor_reduce(o, row, row, 1.0, 0.0, ALU.mult, ALU.add, ss),
                               m_src[t], norm_free[0])
                m_r.append(inverse_root(r, ss, 1, D, a, m_src[t]))
            m_xr = []
            for t in range(T):
                r, row, o = stat[:, 2 * t + 1:2 * t + 2], src[:, t, :], xr[:, t, :]
                m_xr.append(dve.do(lambda e, row=row, o=o, r=r: e.tensor_scalar(o, row, r, None, ALU.mult), m_r[t]))
            marks = []
            for half in range(2):
                i, ps, free = take_pair()
                turned = []
                for bank in range(2):
                    for c in (2 * bank, 2 * bank + 1):
                        k = half * 4 + c
                        for t in range(T):
                            m = turn(ps[:, c * S + t * P:c * S + (t + 1) * P], xr[:, t, k * P:(k + 1) * P],
                                     free, m_xr[t], m_par, signal=c % 2 == 1 and t == 1)
                    turned.append(m)
                marks += split_gained(hi[:, half * 4:half * 4 + 4, :], lo[:, half * 4:half * 4 + 4, :], ps,
                                      [col(gain, half * 4 + c) for c in range(4)], turned, m_par, *m_free)
                give_pair(i, *marks[-4:])
            norm_free[0] = [m_xr, turned]
            return marks

        def debug(k, m):
            if dbg is not None:
                for t in range(T):
                    sp.dma(dbg[k, t * P:(t + 1) * P, :], x[:, t, :], s_out, used, m)

        FF = d["ffn1_w_gate"].shape[1]
        FC = FF // P
        ff_blocks = [(n, min(512, FF - n)) for n in range(0, FF, 512)]
        IN = {"q": 0, "kv": 512, "iq": 768, "ik_iw": 1280, "mx": 1352, "mv": 1864, "mi_mf": 2376, "mo": 2384,
              "ga": 2896, "gb": 3920}
        w_in, w_in2 = d["w_in"], d["w_in_2"]

        def ffn_plan(gate, up, down):
            for n, nw in ff_blocks:
                plan_block(gate, DC, n, nw)
                plan_block(up, DC, n, nw)
            for n in range(0, D, 512):
                plan_block(down, FC, n, 512)

        def narrow_rows(k0, k1, n0, nw):
            v = w_in.rearrange("(k p) n -> p k n", p=P)
            return [(slice(0, P), slice(0, 72), v[:, :, IN["ik_iw"]:IN["ik_iw"] + 72]),
                    (slice(0, P), slice(72, 80), v[:, :, IN["mi_mf"]:IN["mi_mf"] + 8])]

        def proj_a_rows(k0, k1, n0, nw):
            v = d["w_proj_a"].rearrange("(g j q) n -> g q j n", g=2, j=4)
            return [(slice(64 * g, 64 * g + 64), slice(0, nw), v[g, :, k0:k1, n0:n0 + nw]) for g in range(2)]

        ffn_plan(d["ffn1_w_gate"], d["ffn1_w_up"], d["ffn1_w_down"])
        plan_block(w_in, DC, IN["q"], 512)
        plan_block(w_in, DC, IN["kv"], 256)
        plan_block(w_in, DC, 1280, 80, narrow_rows)
        plan_block(w_in, DC, IN["iq"], 512)
        for n in ("mx", "mv", "mo"):
            plan_block(w_in, DC, IN[n], 512)
        for n in ("ga", "gb"):
            for b in range(2):
                plan_block(w_in, DC, IN[n] + 512 * b, 512)
        for b in range(2):
            plan_block(d["w_proj_a"], 4, 512 * b, 512, proj_a_rows)
            plan_block(d["w_proj_b"], 4, 512 * b, 512)
        for b in range(2):
            plan_block(d["w_out"], DC, 512 * b, 512)
        ffn_plan(d["ffn2_w_gate"], d["ffn2_w_up"], d["ffn2_w_down"])
        ffn_plan(d["ffn1_w_gate_2"], d["ffn1_w_up_2"], d["ffn1_w_down_2"])
        for b in range(4):
            plan_block(w_in2, DC, 512 * b, 512)
        for b in range(4):
            plan_block(d["xa_wkv_2"], DC, 512 * b, 512)
        for b in range(2):
            plan_block(d["w_out_2"], DC, 512 * b, 512)
        for b in range(2):
            plan_block(d["xa_wq_2"], DC, 512 * b, 512)
        for b in range(2):
            plan_block(d["xa_wo_2"], DC, 512 * b, 512)
        ffn_plan(d["ffn2_w_gate_2"], d["ffn2_w_up_2"], d["ffn2_w_down_2"])
        for u in range(STAGES):
            load_unit(u)
        state["loaded"] = STAGES

        def post_norm_add(y, gain_name, s_gain, weight, m_y, m_x):
            gb = gain_buf[0]
            m_gb = pool.dma(gb[:], d[gain_name].partition_broadcast(P), s_gain, used, m_x)
            marks = []
            m_r = []
            for t in range(T):
                ss, r, row, o = stat[:, 4 + 2 * t:5 + 2 * t], stat[:, 5 + 2 * t:6 + 2 * t], y[:, t, :], xr[:, t, :]
                a = act.do(lambda e, row=row, o=o, ss=ss: e.activation(o, row, ACT.Square, accum_out=ss), m_y[t], norm_free[0])
                m_r.append(inverse_root(r, ss, 1, D, a))
            for t in range(T):
                r, row, xt = stat[:, 5 + 2 * t:6 + 2 * t], y[:, t, :], x[:, t, :]
                b = dve.do(lambda e, row=row, r=r: e.scalar_tensor_tensor(row, row, r, gb[:], ALU.mult, ALU.mult), m_r[t], m_gb)
                marks.append(dve.do(lambda e, row=row, xt=xt: e.scalar_tensor_tensor(xt, row, weight, xt, ALU.mult, ALU.add), b))
            return marks

        def rows_to_y(w, K, a_hi, a_lo, ready, y):
            m = [[], []]
            for b in range(2):
                i, ps, done = block(w, K, 512 * b, 512, a_hi, a_lo, ready, "rows")
                for t in range(T):
                    m[t].append(act.do(lambda e, b=b, t=t, ps=ps: e.copy(y[:, t, 512 * b:512 * b + 512], ps[:, t * 512:(t + 1) * 512]), done))
                give_pair(i, m[1][-1])
            return m

        def ffn(n_ffn, gate, up, down, gain, m_x, y=None, post=None, s_post=None):
            scope = ExitStack()
            with scope:
                f_hi = sb(scope, f"f_hi{n_ffn}", [P, FC, S], F32R)
                f_lo = sb(scope, f"f_lo{n_ffn}", [P, FC, S], F32R)
                act_buf = [sb(scope, f"act_buf{n_ffn}_{i}", [P, 1024]) for i in range(2)]
                buf_free = [None, None]
                m_h = norm_cols(x, gain, h_hi, h_lo, m_x)
                m_f = {}
                for b, (n, nw) in enumerate(ff_blocks):
                    ig, pg, dg = block(gate, DC, n, nw, h_hi, h_lo, m_h, "cols")
                    w = nw // P * S
                    s_ = act_buf[b % 2][:, 0:w]
                    a = act.do(lambda e, s_=s_, pg=pg, w=w: e.activation(s_, pg[:, 0:w], ACT.Sigmoid), dg, buf_free[b % 2])
                    a = dve.do(lambda e, s_=s_, pg=pg, w=w: e.tensor_tensor(s_, s_, pg[:, 0:w], ALU.mult), a)
                    give_pair(ig, a)
                    iu, pu, du = block(up, DC, n, nw, h_hi, h_lo, m_h, "cols")
                    a = dve.do(lambda e, s_=s_, pu=pu, w=w: e.tensor_tensor(s_, s_, pu[:, 0:w], ALU.mult), a, du)
                    give_pair(iu, a)
                    k = n // P
                    hi = f_hi[:, k:k + nw // P, :].rearrange("p k s -> p (k s)")
                    lo = f_lo[:, k:k + nw // P, :].rearrange("p k s -> p (k s)")
                    m1 = act.do(lambda e, s_=s_, hi=hi: e.copy(hi, s_), a)
                    m2 = dve.do(lambda e, s_=s_, hi=hi, lo=lo: e.tensor_tensor(lo, s_, hi.bitcast(F32), ALU.subtract), m1)
                    buf_free[b % 2] = [m1, m2]
                    for c in range(nw // P):
                        m_f[k + c] = [m1, m2]
                if y is not None:
                    m_y = rows_to_y(down, FC, f_hi, f_lo, m_f, y)
                    return post_norm_add(y, post, s_post, 0.5, m_y, list(m_h))
                marks = [[], []]
                for b in range(2):
                    i, ps, done = block(down, FC, 512 * b, 512, f_hi, f_lo, m_f, "rows")
                    for t in range(T):
                        xt = x[:, t, 512 * b:512 * b + 512]
                        marks[t].append(dve.do(lambda e, xt=xt, t=t, ps=ps: e.scalar_tensor_tensor(
                            xt, ps[:, t * 512:(t + 1) * 512], 0.5, xt, ALU.mult, ALU.add), done))
                    give_pair(i, marks[1][-1])
                return marks

        def attention(name, scope, qT, kT_of, v_of, mask_ops, m_q, m_k, m_v, m_mask, o_hi, o_lo, filler=lambda: None):
            sc = [sb(scope, f"scores{t}_{name}", [P, 8, P * (t + 1)]) for t in range(T)]
            nmax = sb(scope, f"nmax_{name}", [P, T, 8])
            tot = sb(scope, f"tot_{name}", [P, T, 8])
            m_p = []
            for t in range(T):
                w = P * (t + 1)
                groups = [range(4)] if t == 0 else [range(0, 2), range(2, 4)]
                for g, js in enumerate(groups):
                    n = len(js)
                    i, ps, free = take_pair()
                    for half in range(2):
                        for jj, j in enumerate(js):
                            o = ps[:, half * 512 + jj * w:half * 512 + (jj + 1) * w]
                            r = slice(64 * half, 64 * half + 64)
                            done = mm(o, qT[r, j, t * P:(t + 1) * P], kT_of(half, j)[:, 0:w], jj == 0, jj == n - 1,
                                      free, m_q, m_k, signal=half == 1 and jj == n - 1)
                    dst = sc[t][:, g * 4:g * 4 + 2 * n, :]
                    src = ps[:, :].rearrange("p (h w) -> p h w", w=w)
                    m_s = []
                    for lo_, hi_, mask in mask_ops(t, g):
                        m_s.append(dve.do(lambda e, dst=dst, src=src, lo_=lo_, hi_=hi_, mask=mask: e.scalar_tensor_tensor(
                            dst[:, lo_:hi_, :], src[:, lo_:hi_, :], 0.125, mask, ALU.mult, ALU.add), done, m_mask))
                    give_pair(i, *m_s)
                    h0 = g * 4
                    nm = nmax[:, t, h0:h0 + 2 * n]
                    a = dve.do(lambda e, nm=nm, dst=dst: e.tensor_reduce(nm, dst, AX_X, ALU.max, negate=True), m_s)
                    for h in range(2 * n):
                        b = act.do(lambda e, h=h, dst=dst, t=t, h0=h0: e.activation(
                            dst[:, h, :], dst[:, h, :], ACT.Exp, bias=nmax[:, t, h0 + h:h0 + h + 1],
                            accum_out=tot[:, t, h0 + h:h0 + h + 1]), a)
                    tt = tot[:, t, h0:h0 + 2 * n]
                    b = dve.do(lambda e, tt=tt: e.reciprocal(tt, tt), b)
                    m_p.append(dve.do(lambda e, dst=dst, tt=tt, n=n, w=w: e.tensor_tensor(dst, dst, bcast(tt, 2, w), ALU.mult), b))
                    filler()
            pt = [sb(scope, f"pt{i}_{name}", [P, 384]) for i in range(2)]
            pt_free = [None, None]
            io, po, ofree = take_pair()
            begun = set()
            n_head = 0
            for j in range(4):
                for half in range(2):
                    at0 = half * 4 + j
                    at1 = (j // 2) * 4 + half * 2 + j % 2
                    i, ps, free = take_pair()
                    turn(ps[:, 0:P], sc[0][:, at0, :], free, m_p)
                    turn(ps[:, P:2 * P], sc[1][:, at1, 0:P])
                    done = turn(ps[:, 2 * P:3 * P], sc[1][:, at1, P:2 * P], signal=True)
                    b = n_head % 2
                    eng = act if n_head % 2 else dve
                    if eng is act:
                        c = act.do(lambda e, b=b, ps=ps: e.copy(pt[b][:], ps[:, 0:384]), done, pt_free[b])
                    else:
                        c = dve.do(lambda e, b=b, ps=ps: e.tensor_copy(pt[b][:], ps[:, 0:384]), done, pt_free[b])
                    give_pair(i, c)
                    o = po[64 * half:64 * half + 64, j * S:(j + 1) * S]
                    key = (j // 2, half)
                    mm(o, v_of(0, half, j), pt[b][:, 0:S], key not in begun, False, c, ofree, m_v)
                    begun.add(key)
                    pt_free[b] = mm(o[:, P:S], v_of(1, half, j), pt[b][:, S:384], False, True, signal=True)
                    n_head += 1
                    if n_head % 4 == 0:
                        filler()
            a = act.do(lambda e: e.copy(o_hi, po[:, :]), pt_free)
            b = dve.do(lambda e: e.tensor_tensor(o_lo, po[:, :], o_hi.bitcast(F32), ALU.subtract), a)
            give_pair(io, a, b)
            return [a, b]

        def mixer1(m_x):
            outer = ExitStack()
            with outer:
                ya_hi, ya_lo = sb(outer, "ya_hi", [P, 4, S], F32R), sb(outer, "ya_lo", [P, 4, S], F32R)
                yb_hi, yb_lo = sb(outer, "yb_hi", [P, 4, S], F32R), sb(outer, "yb_lo", [P, 4, S], F32R)
                xpad = sb(outer, "xpad", [P, 4, S + 3])
                mv = sb(outer, "mv", [P, T, 512])
                mo = sb(outer, "mo", [P, T, 512])
                nar = sb(outer, "nar", [P, T, 80])
                ga, gb = sb(outer, "ga", [P, DC, S]), sb(outer, "gb", [P, DC, S])
                w_mq, w_mk = sb(outer, "w_mq", [P, 4, 64]), sb(outer, "w_mk", [P, 4, 64])
                head_g = sb(outer, "head_g", [P, 512])
                chunked = sb(outer, "chunked", [P, 2 * P])
                head_rows = sb(outer, "head_rows", [4, 512])
                s_m = s_small["mix1"]
                pool.dma(w_mq[:], d["w_mq"].rearrange("h c q -> c h q"), s_m, used, m_x)
                pool.dma(w_mk[:], d["w_mk"].rearrange("h c q -> c h q"), s_m, used)
                pool.dma(head_g[:], d["m_head_norm"].partition_broadcast(P), s_m, used)
                pool.dma(chunked[:], d["consts"][:, 384:640], s_m, used)
                m_const = pool.dma(head_rows[:], d["consts"][0:4, 3712:4224], s_m, used)
                m_zero = pool.do(lambda e: e.memset(xpad[:, :, 0:3], 0.0))
                m_h = norm_cols(x, "mix_norm", h_hi, h_lo, m_x)

                inner = ExitStack()
                with inner:
                    qk = sb(inner, "qk", [P, T, 704])
                    sq = sb(inner, "sq", [P, T, 704])
                    rr = sb(inner, "rr", [P, T * 11])
                    v = sb(inner, "v", [P, T, P])
                    ikk = sb(inner, "ikk", [P, T, 2, 64])
                    qT, kT, ikT = sb(inner, "qT", [P, 4, S]), sb(inner, "kT", [P, S]), sb(inner, "ikT", [P, S])
                    iqT = sb(inner, "iqT", [P, 4, S])
                    i, ps, done = block(w_in, DC, IN["q"], 512, h_hi, h_lo, m_h, "rows")
                    a1 = act.do(lambda e, ps=ps: e.copy(qk[:, :, 0:512], ps[:, :].rearrange("p (t n) -> p t n", t=T)), done)
                    give_pair(i, a1)
                    i, ps, done = block(w_in, DC, IN["kv"], 256, h_hi, h_lo, m_h, "rows")
                    pv_ = ps[:, :].rearrange("p (t n) -> p t n", t=T)
                    a2 = act.do(lambda e, pv_=pv_: e.copy(qk[:, :, 512:640], pv_[:, :, 0:128]), done)
                    m_v = act.do(lambda e, pv_=pv_: e.copy(v[:], pv_[:, :, 128:256]), done)
                    give_pair(i, a2, m_v)
                    i, ps, done = block(w_in, DC, 1280, 80, h_hi, h_lo, m_h, "rows")
                    pn = ps[:, :].rearrange("p (t n) -> p t n", t=T)
                    a3 = act.do(lambda e, pn=pn: e.copy(qk[:, :, 640:704], pn[:, :, 0:64]), done)
                    m_nar = act.do(lambda e, pn=pn: e.copy(nar[:], pn[:, :, 0:80]), done)
                    give_pair(i, a3, m_nar)
                    flat = lambda ap: ap.rearrange("p t n -> p (t n)")
                    b = dve.do(lambda e: e.tensor_tensor(flat(sq[:]), flat(qk[:]), flat(qk[:]), ALU.mult), a1, a2, a3)
                    b = dve.do(lambda e: e.tensor_reduce(rr[:], flat(sq[:]).rearrange("p (g q) -> p g q", q=64), AX_X, ALU.add), b)
                    m_rr = inverse_root(rr[:], rr[:], T * 11, 64, b)
                    m_n = []
                    for t in range(T):
                        src = qk[:, t, 0:512].rearrange("p (g j q) -> p g j q", g=2, j=4)
                        dst = sq[:, t, 0:512].rearrange("p (j g q) -> p g j q", g=2, j=4)
                        r = rr[:, t * 11:t * 11 + 8].rearrange("p (g j) -> p g j", g=2)
                        m_n.append(dve.do(lambda e, src=src, dst=dst, r=r: e.tensor_tensor(dst, src, bcast(r, 3, 64), ALU.mult), m_rr))
                        src = qk[:, t, 512:640].rearrange("p (g q) -> p g q", q=64)
                        dst = sq[:, t, 512:640].rearrange("p (g q) -> p g q", q=64)
                        r = rr[:, t * 11 + 8:t * 11 + 10]
                        m_n.append(dve.do(lambda e, src=src, dst=dst, r=r: e.tensor_tensor(dst, src, bcast(r, 2, 64), ALU.mult)))
                        src, r = qk[:, t, 640:704], rr[:, t * 11 + 10:t * 11 + 11]
                        for c in range(2):
                            m_n.append(dve.do(lambda e, src=src, r=r, t=t, c=c: e.tensor_scalar(ikk[:, t, c, :], src, r, None, ALU.mult)))
                    i, ps, free = take_pair()
                    for j in range(4):
                        for t in range(T):
                            done = turn(ps[:, j * S + t * P:j * S + (t + 1) * P], sq[:, t, j * P:(j + 1) * P], free, m_n, signal=j == 3 and t == 1)
                    m_q = dve.do(lambda e, ps=ps: e.tensor_scalar(qT[:].rearrange("p j s -> p (j s)"), ps[:, :], col("q_norm"), None, ALU.mult), done)
                    give_pair(i, m_q)
                    i, ps, free = take_pair()
                    for t in range(T):
                        turn(ps[:, t * P:(t + 1) * P], sq[:, t, 512:640], free)
                        done = turn(ps[:, 512 + t * P:512 + (t + 1) * P], ikk[:, t, :, :].rearrange("p c q -> p (c q)"), signal=t == 1)
                    m_k = dve.do(lambda e, ps=ps: e.tensor_scalar(kT[:], ps[:, 0:S], col("k_norm"), None, ALU.mult), done)
                    m_ik = dve.do(lambda e, ps=ps: e.tensor_scalar(ikT[:], ps[:, 512:512 + S], col("idx_k_norm"), None, ALU.mult), done)
                    give_pair(i, m_k, m_ik)
                    i, ps, done = block(w_in, DC, IN["iq"], 512, h_hi, h_lo, m_h, "cols")
                    m_iq = act.do(lambda e, ps=ps: e.copy(iqT[:].rearrange("p j s -> p (j s)"), ps[:, :]), done)
                    give_pair(i, m_iq)

                    iscope = ExitStack()
                    sel = [sb(inner, f"sel{t}", [P, P * (t + 1)]) for t in range(T)]
                    with iscope:
                        relu = [sb(iscope, f"relu{i}", [P, 1024]) for i in range(2)]
                        relu_free = [None, None]
                        work = [sb(iscope, f"work{t}", [P, P * (t + 1)]) for t in range(T)]
                        top = sb(iscope, "top", [P, 8])
                        n_relu = 0
                        m_top = None
                        m_sel = []
                        for t in range(T):
                            w = P * (t + 1)
                            a = None
                            for js in ([range(4)] if t == 0 else [range(0, 2), range(2, 4)]):
                                i, ps, free = take_pair()
                                for half in range(2):
                                    for jj, j in enumerate(js):
                                        r = slice(64 * half, 64 * half + 64)
                                        done = mm(ps[:, half * 512 + jj * w:half * 512 + (jj + 1) * w], iqT[r, j, t * P:(t + 1) * P],
                                                  ikT[r, 0:w], jj == 0, jj == len(js) - 1, free, m_iq, m_ik,
                                                  signal=half == 1 and jj == len(js) - 1)
                                rb = relu[n_relu % 2]
                                m_r = act.do(lambda e, rb=rb, ps=ps: e.activation(rb[:], ps[:, :], ACT.Relu), done, relu_free[n_relu % 2])
                                give_pair(i, m_r)
                                for half in range(2):
                                    for jj, j in enumerate(js):
                                        head = 2 * j + half
                                        src = rb[:, half * 512 + jj * w:half * 512 + (jj + 1) * w]
                                        iw = nar[:, t, 64 + head:65 + head]
                                        if a is None:
                                            a = dve.do(lambda e, src=src, iw=iw, t=t: e.tensor_scalar(work[t][:], src, iw, None, ALU.mult), m_r, m_nar)
                                        else:
                                            a = dve.do(lambda e, src=src, iw=iw, t=t: e.scalar_tensor_tensor(
                                                work[t][:], src, iw, work[t][:], ALU.mult, ALU.add), m_r, a)
                                relu_free[n_relu % 2] = a
                                n_relu += 1
                            mask = chunked[:, P:2 * P] if t == 0 else chunked[:, :]
                            a = dve.do(lambda e, t=t, mask=mask: e.scalar_tensor_tensor(
                                work[t][:], work[t][:], (64 ** -0.5) * (8 ** -0.5), mask, ALU.mult, ALU.add), a, m_const)
                            for _ in range(TOPK // 8):
                                a = dve.do(lambda e, t=t: e.max(top[:], work[t][:]), a, m_top)
                                a = m_top = dve.do(lambda e, t=t: e.match_replace(work[t][:], top[:], work[t][:], PICKED), a)
                            m_sel.append(dve.do(lambda e, t=t: e.tensor_scalar(
                                sel[t][:], work[t][:], (PICKED + UNPICKED) / 2, MASKED, ALU.is_gt, ALU.mult), a))

                    i, ps, done = block(w_in, DC, IN["mx"], 512, h_hi, h_lo, m_h, "cols")
                    m_mx = act.do(lambda e, ps=ps: e.copy(xpad[:, :, 3:3 + S], ps[:, :].rearrange("p (c s) -> p c s", c=4)), done)
                    give_pair(i, m_mx)
                    i, ps, done = block(w_in, DC, IN["mv"], 512, h_hi, h_lo, m_h, "rows")
                    m_mv = act.do(lambda e, ps=ps: e.copy(flat(mv[:]), ps[:, :]), done)
                    give_pair(i, m_mv)
                    i, ps, done = block(w_in, DC, IN["mo"], 512, h_hi, h_lo, m_h, "rows")
                    m_mo = act.do(lambda e, ps=ps: e.activation(flat(mo[:]), ps[:, :], ACT.Sigmoid), done)
                    give_pair(i, m_mo)
                    m_mog = pool.do(lambda e: e.tensor_tensor(mo[:], mo[:], bcast(head_g[:], 1, T), ALU.mult), m_mo, m_const)
                    m_g = {}
                    pending = [("ga", ga, 0), ("ga", ga, 1), ("gb", gb, 0), ("gb", gb, 1)]

                    def gate_block():
                        if not pending:
                            return
                        n, dst, b = pending.pop(0)
                        i, ps, done = block(w_in, DC, IN[n] + 512 * b, 512, h_hi, h_lo, m_h, "cols")
                        o = dst[:, 4 * b:4 * b + 4, :].rearrange("p c s -> p (c s)")
                        m_g[n, b] = act.do(lambda e, o=o, ps=ps: e.activation(o, ps[:, :], ACT.Sigmoid), done)
                        give_pair(i, m_g[n, b])

                    def mask_ops(t, g):
                        return [(0, 8 if t == 0 else 4, bcast(sel[t][:], 1, 8 if t == 0 else 4))]
                    m_ya = attention("a", inner, qT, lambda half, j: kT[64 * half:64 * half + 64, :],
                                     lambda st, half, j: v[:, st, 64 * half:64 * half + 64], mask_ops, m_q, m_k, m_v, m_sel,
                                     ya_hi[:].rearrange("p c s -> p (c s)"), ya_lo[:].rearrange("p c s -> p (c s)"))

                ml = ExitStack()
                with ml:
                    xc = sb(ml, "xc", [P, 4, S])
                    sg = sb(ml, "sg", [P, 4, S])
                    mq, mk = sb(ml, "mq", [64, 4, S]), sb(ml, "mk", [64, 4, S])
                    gi, gf, gt, ones = (sb(ml, n, [4, S]) for n in ("gi", "gf", "gt", "ones"))
                    dm = [sb(ml, f"dm{t}", [P, 4, P * (t + 1)]) for t in range(T)]
                    mt = sb(ml, "mt", [P, T, 4])
                    nmt = sb(ml, "nmt", [P, T, 4])
                    ft = sb(ml, "ft", [P, T, 4])
                    den = sb(ml, "den", [P, T, 4])
                    wt = [sb(ml, f"wt{i}", [P, 384]) for i in range(2)]
                    rh = sb(ml, "rh", [P, T * 4])
                    after = [m_ya]

                    m_c = []
                    for c in range(4):
                        a = dve.do(lambda e, c=c: e.tensor_scalar(xc[:, c, :], xpad[:, c, 0:S], col("conv_w", c), col("conv_b", c), ALU.mult, ALU.add),
                                   m_mx, m_zero, after)
                        for j in range(1, 4):
                            a = dve.do(lambda e, c=c, j=j: e.scalar_tensor_tensor(
                                xc[:, c, :], xpad[:, c, j:j + S], col("conv_w", 4 * j + c), xc[:, c, :], ALU.mult, ALU.add), a)
                        m_c.append(a)
                    a = act.do(lambda e: e.activation(sg[:], xc[:], ACT.Sigmoid), m_c, after)
                    m_xc = dve.do(lambda e: e.tensor_tensor(xc[:], xc[:], sg[:], ALU.mult), a)

                    i, ps, free = take_pair()
                    for t in range(T):
                        turn(ps[0:4, t * P:(t + 1) * P], nar[:, t, 72:76], free, m_nar)
                        done = turn(ps[0:4, 512 + t * P:512 + (t + 1) * P], nar[:, t, 76:80], signal=t == 1)
                    m_gi = dve.do(lambda e, ps=ps: e.tensor_scalar(gi[:], ps[0:4, 0:S], col("b_i", 0, 4), None, ALU.add), done)
                    a0 = dve.do(lambda e, ps=ps: e.tensor_scalar(gf[:], ps[0:4, 512:512 + S], col("b_f", 0, 4), None, ALU.add), done)
                    give_pair(i, m_gi, a0)
                    a = act.do(lambda e: e.activation(gt[:], gf[:], ACT.Abs), a0)
                    a = act.do(lambda e: e.activation(gt[:], gt[:], ACT.Exp, scale=-1.0), a)
                    a = act.do(lambda e: e.activation(gt[:], gt[:], ACT.Ln, bias=1.0), a)
                    a = dve.do(lambda e: e.scalar_tensor_tensor(gt[:], gf[:], 0.0, gt[:], ALU.min, ALU.subtract), a)
                    b = dve.do(lambda e: e.memset(ones[:], 1.0))
                    m_F = dve.do(lambda e: e.tensor_tensor_scan(gf[:], ones[:], gt[:], 0.0, ALU.mult, ALU.add), a, b)
                    m_G = dve.do(lambda e: e.tensor_tensor(gi[:], gi[:], gf[:], ALU.subtract), m_F, m_gi)
                    i, ps, free = take_pair()
                    for t in range(T):
                        done = turn(ps[:, 4 * t:4 * t + 4], gf[:, t * P:(t + 1) * P], free, m_F, signal=t == 1)
                    m_ft = act.do(lambda e, ps=ps: e.copy(ft[:].rearrange("p t h -> p (t h)"), ps[:, 0:8]), done, after)
                    give_pair(i, m_ft)
                    i, ps, free = take_pair()
                    for h in range(4):
                        done = mm(ps[:, h * S:(h + 1) * S], head_rows[:, h * P:(h + 1) * P], gi[:], h % 2 == 0, h % 2 == 1,
                                  free, m_G, m_const, signal=h == 3)
                    gps = ps[:, :].rearrange("p (h s) -> p h s", h=4)
                    m_d = []
                    for t in range(T):
                        w = P * (t + 1)
                        mask = causal[:, P:2 * P] if t == 0 else causal[:, :]
                        m_d.append(dve.do(lambda e, t=t, w=w, mask=mask, gps=gps: e.tensor_tensor(dm[t][:], gps[:, :, 0:w], bcast(mask, 1, 4), ALU.add), done, m_par))
                    give_pair(i, m_d)
                    m_e = []
                    for t in range(T):
                        a = dve.do(lambda e, t=t: e.tensor_reduce(mt[:, t, :], dm[t][:], AX_X, ALU.max), m_d)
                        m_m = dve.do(lambda e, t=t: e.tensor_scalar(mt[:, t, :], mt[:, t, :], 0.0, None, ALU.max), a)
                        a = dve.do(lambda e, t=t: e.tensor_scalar(nmt[:, t, :], mt[:, t, :], -1.0, None, ALU.mult), m_m)
                        for h in range(4):
                            b = act.do(lambda e, t=t, h=h: e.activation(dm[t][:, h, :], dm[t][:, h, :], ACT.Exp, bias=nmt[:, t, h:h + 1]), a)
                        m_e.append(b)
                    a = dve.do(lambda e: e.tensor_tensor(ft[:], ft[:], mt[:], ALU.add), m_ft, m_m)
                    m_floor = act.do(lambda e: e.activation(ft[:], ft[:], ACT.Exp, scale=-1.0), a)

                    for w_m, dst, scale in ((w_mq, mq, 0.125), (w_mk, mk, 1.0)):
                        i, ps, free = take_pair()
                        for h in range(4):
                            done = mm(ps[0:64, h * S:(h + 1) * S], w_m[:, h, :], xc[:, h, :], h % 2 == 0, h % 2 == 1, free, m_xc, m_const, signal=h == 3)
                        m_qk = act.do(lambda e, dst=dst, ps=ps, scale=scale: e.activation(
                            dst[:].rearrange("p h s -> p (h s)"), ps[0:64, :], ACT.Copy, scale=scale), done)
                        give_pair(i, m_qk)
                    m_w = []
                    for t in range(T):
                        w = P * (t + 1)
                        i, ps, free = take_pair()
                        for h in range(4):
                            done = mm(ps[:, h * w:(h + 1) * w], mq[:, h, t * P:(t + 1) * P], mk[:, h, 0:w], h * w % 512 == 0,
                                      (h + 1) * w % 512 == 0, free, m_qk, signal=h == 3)
                        src = ps[:, 0:4 * w].rearrange("p (h s) -> p h s", h=4)
                        a = dve.do(lambda e, t=t, src=src: e.tensor_tensor(dm[t][:], dm[t][:], src, ALU.mult), done, m_e[t])
                        give_pair(i, a)
                        m_w.append(a)
                        m_den = dve.do(lambda e, t=t: e.tensor_reduce(den[:, t, :], dm[t][:], AX_X, ALU.add), a)
                    a = act.do(lambda e: e.activation(den[:], den[:], ACT.Abs), m_den)
                    a = dve.do(lambda e: e.tensor_tensor(den[:], den[:], ft[:], ALU.max), a, m_floor)
                    m_den = dve.do(lambda e: e.reciprocal(den[:], den[:]), a)
                    ih, ph, hfree = take_pair()
                    begun = set()
                    wt_free = [None, None]
                    for h in range(4):
                        i, ps, free = take_pair()
                        turn(ps[:, 0:P], dm[0][:, h, :], free, m_w)
                        turn(ps[:, P:2 * P], dm[1][:, h, 0:P])
                        done = turn(ps[:, 2 * P:3 * P], dm[1][:, h, P:2 * P], signal=True)
                        b = h % 2
                        if b:
                            c = act.do(lambda e, b=b, ps=ps: e.copy(wt[b][:], ps[:, 0:384]), done, wt_free[b])
                        else:
                            c = dve.do(lambda e, b=b, ps=ps: e.tensor_copy(wt[b][:], ps[:, 0:384]), done, wt_free[b])
                        give_pair(i, c)
                        mm(ph[:, h * P:(h + 1) * P], wt[b][:, 0:P], mv[:, 0, h * P:(h + 1) * P], h == 0, h == 3, c, hfree, m_mv)
                        mm(ph[:, 512 + h * P:512 + (h + 1) * P], wt[b][:, P:2 * P], mv[:, 0, h * P:(h + 1) * P], h == 0, False)
                        wt_free[b] = mm(ph[:, 512 + h * P:512 + (h + 1) * P], wt[b][:, 2 * P:3 * P], mv[:, 1, h * P:(h + 1) * P], False, h == 3, signal=True)
                    while pending:
                        gate_block()
                    hm = xc[:].rearrange("p c s -> p (c s)")
                    hv = hm.rearrange("p (g q) -> p g q", q=P)
                    sv = sg[:].rearrange("p c s -> p (c s)")
                    dn = den[:].rearrange("p t h -> p (t h)")
                    a = dve.do(lambda e: e.tensor_tensor(hv, ph[:, :].rearrange("p (g q) -> p g q", q=P), bcast(dn, 2, P), ALU.mult),
                               wt_free, m_den, m_qk)
                    give_pair(ih, a)
                    a = dve.do(lambda e: e.tensor_tensor(sv, hm, hm, ALU.mult), a)
                    a = dve.do(lambda e: e.tensor_reduce(rh[:], sv.rearrange("p (g q) -> p g q", q=P), AX_X, ALU.add), a)
                    a = inverse_root(rh[:], rh[:], T * 4, P, a)
                    a = dve.do(lambda e: e.tensor_tensor(hv, hv, bcast(rh[:], 2, P), ALU.mult), a)
                    a = dve.do(lambda e: e.tensor_tensor(hm, hm, flat(mo[:]), ALU.mult), a, m_mog)
                    i, ps, free = take_pair()
                    for h in range(4):
                        for t in range(T):
                            done = turn(ps[:, h * S + t * P:h * S + (t + 1) * P], hm[:, t * 512 + h * P:t * 512 + (h + 1) * P], free, a, signal=h == 3 and t == 1)
                    m_yb = split_whole(yb_hi[:].rearrange("p c s -> p (c s)"), yb_lo[:].rearrange("p c s -> p (c s)"), ps[:, :], done)
                    give_pair(i, m_yb)

                m_merged = {}
                for b in range(2):
                    ia, pa, da = block(d["w_proj_a"], 4, 512 * b, 512, ya_hi, ya_lo, [m_ya] * 4, "cols")
                    av = ga[:, 4 * b:4 * b + 4, :].rearrange("p c s -> p (c s)")
                    bv = gb[:, 4 * b:4 * b + 4, :].rearrange("p c s -> p (c s)")
                    a1 = dve.do(lambda e, av=av, pa=pa: e.tensor_tensor(av, av, pa[:, :], ALU.mult), da, m_g["ga", b])
                    give_pair(ia, a1)
                    ib, pb, db = block(d["w_proj_b"], 4, 512 * b, 512, yb_hi, yb_lo, [m_yb] * 4, "cols")
                    a2 = dve.do(lambda e, bv=bv, pb=pb: e.tensor_tensor(bv, bv, pb[:, :], ALU.mult), db, m_g["gb", b])
                    give_pair(ib, a2)
                    a = dve.do(lambda e, av=av, bv=bv: e.tensor_tensor(av, av, bv, ALU.add), a1, a2)
                    hi = h_hi[:, 4 * b:4 * b + 4, :].rearrange("p c s -> p (c s)")
                    lo = h_lo[:, 4 * b:4 * b + 4, :].rearrange("p c s -> p (c s)")
                    m = split_whole(hi, lo, av, a, m_g["gb", 1])
                    for c in range(4):
                        m_merged[4 * b + c] = m
                marks = [[], []]
                for b in range(2):
                    i, ps, done = block(d["w_out"], DC, 512 * b, 512, h_hi, h_lo, m_merged, "rows")
                    for t in range(T):
                        xt = x[:, t, 512 * b:512 * b + 512]
                        marks[t].append(dve.do(lambda e, xt=xt, t=t, ps=ps: e.tensor_tensor(xt, xt, ps[:, t * 512:(t + 1) * 512], ALU.add), done))
                    give_pair(i, marks[1][-1])
                return marks

        def mixer2(m_x, y, xk, xv):
            scope = ExitStack()
            with scope:
                alibi = sb(scope, "alibi", [P, 2, 2, 2, S])
                mem_hi, mem_lo = sb(scope, "mem_hi", [P, DC, S], F32R), sb(scope, "mem_lo", [P, DC, S], F32R)
                qT, kT = sb(scope, "qT2", [P, 4, S]), sb(scope, "kT2", [P, 4, S])
                v = sb(scope, "v2", [P, T, 512])
                m_alibi = pool.dma(alibi[:].rearrange("p a b c s -> p (a b c s)"), d["consts"][:, 640:2688], s_small["mix2"], used, m_x)
                for t in range(T):
                    m_mem = pool.dma(y[:, t, :], d["mem_2"][t * P:(t + 1) * P, :], s_small["mem"], used, m_x)
                m_h = norm_cols(x, "mix_pre_g_2", h_hi, h_lo, m_x)

                for b, dst in ((0, qT), (1, kT)):
                    i, ps, done = block(w_in2, DC, 512 * b, 512, h_hi, h_lo, m_h, "cols")
                    m = act.do(lambda e, dst=dst, ps=ps: e.copy(dst[:].rearrange("p j s -> p (j s)"), ps[:, :]), done)
                    give_pair(i, m)
                m_qk = m
                m_memT = norm_cols(y, "mem_g_2", mem_hi, mem_lo, [m_mem] * T)
                i, ps, done = block(w_in2, DC, 1024, 512, h_hi, h_lo, m_h, "rows")
                m_v = act.do(lambda e, ps=ps: e.copy(v[:].rearrange("p t n -> p (t n)"), ps[:, :]), done)
                give_pair(i, m_v)

                L = 16 + S
                ps_scope = ExitStack()
                with ps_scope:
                    win = [sb(ps_scope, f"win{i}", [P, 4, L]) for i in range(2)]
                    pin = sb(ps_scope, "pin", [P, 4, S])
                    inv = sb(ps_scope, "inv", [P, 4, S])
                    pw = sb(ps_scope, "pw", [P, 4, P])
                    m_zero = pool.do(lambda e: e.memset(win[0][:, :, 0:16], 0.0), m_x)
                    pool.dma(inv[:].rearrange("p g s -> p (g s)"), d["consts"][:, 2688:3712], s_small["mix2"], used)
                    m_pw = pool.dma(pw[:], d["pool_w_2"].rearrange("g c n -> c g n"), s_small["mix2"], used)
                    i, ps, done = block(w_in2, DC, 1536, 512, h_hi, h_lo, m_h, "cols")
                    pv_ = ps[:, :].rearrange("p (g s) -> p g s", g=4)
                    a = act.do(lambda e, pv_=pv_: e.copy(win[0][:, :, 16:L], pv_), done)
                    b = act.do(lambda e, pv_=pv_: e.copy(pin[:], pv_), done)
                    give_pair(i, a, b)
                    m_pin = [a, b]
                    last = [a, m_zero]
                    for g in range(4):
                        src, dst = win[g % 2], win[(g + 1) % 2]
                        sh = 2 ** g
                        first = (1, 4, 8, 16)[g]
                        m_sum = dve.do(lambda e, src=src, dst=dst, sh=sh, first=first, g=g: e.tensor_tensor(
                            dst[:, g:4, first:L], src[:, g:4, first:L], src[:, g:4, first - sh:L - sh], ALU.add), *last)
                        a = dve.do(lambda e, dst=dst, g=g: e.tensor_tensor(inv[:, g, :], dst[:, g, 16:L], inv[:, g, :], ALU.mult), m_sum, m_pw)
                        m_dev = dve.do(lambda e, g=g: e.tensor_tensor(pin[:, g, :], inv[:, g, :], pin[:, g, :], ALU.subtract), a, m_pin)
                        last = [m_sum, a]
                    i, ps, free = take_pair()
                    for g in range(4):
                        done = mm(ps[:, g * S:(g + 1) * S], pw[:, g, :], pin[:, g, :], g % 2 == 0, g % 2 == 1, free, m_dev, m_pw, signal=g == 3)
                    m_cat = {}
                    ms = split_gained(h_hi[:, 4:8, :], h_lo[:, 4:8, :], ps, [col("pool_scale_2", g) for g in range(4)], [done, done])
                    for g in range(4):
                        m_cat[4 + g] = ms[g]
                    give_pair(i, *[m_cat[4 + g] for g in range(4)])
                after_pool = [m_cat[7]]

                kv_pending = list(range(4))
                m_kv = []

                def kv_block():
                    if not kv_pending:
                        return
                    b = kv_pending.pop(0)
                    form = "cols" if b < 2 else "rows"
                    i, ps, done = block(d["xa_wkv_2"], DC, 512 * b, 512, mem_hi, mem_lo, m_memT, form)
                    if b < 2:
                        o = xk[:, 4 * b:4 * b + 4, :].rearrange("p c s -> p (c s)")
                        m = act.do(lambda e, o=o, ps=ps: e.copy(o, ps[:, :]), done)
                    else:
                        o = xv[:, :, 512 * (b - 2):512 * (b - 1)]
                        m = act.do(lambda e, o=o, ps=ps: e.copy(o, ps[:, :].rearrange("p (t n) -> p t n", t=T)), done)
                    give_pair(i, m)
                    m_kv.append(m)

                def mask_ops(t, g):
                    if t == 1:
                        return [(0, 4, alibi[:, g].rearrange("p b c s -> p (b c) s"))]
                    return [(half * 4 + gg * 2, half * 4 + gg * 2 + 2, alibi[:, gg, half, :, P:2 * P]) for half in range(2) for gg in range(2)]
                m_att = attention("m", scope, qT, lambda half, j: kT[64 * half:64 * half + 64, j, :],
                                  lambda st, half, j: v[:, st, (2 * j + half) * 64:(2 * j + half) * 64 + 64], mask_ops,
                                  m_qk, [m_qk, after_pool], m_v, [m_alibi, after_pool],
                                  h_hi[:, 0:4, :].rearrange("p c s -> p (c s)"), h_lo[:, 0:4, :].rearrange("p c s -> p (c s)"), kv_block)
                while kv_pending:
                    kv_block()
                for c in range(4):
                    m_cat[c] = m_att
                m_y = rows_to_y(d["w_out_2"], DC, h_hi, h_lo, m_cat, y)
                return post_norm_add(y, "mix_post_g_2", s_small["post1"], 1.0, m_y, m_y[1]), m_kv

        def cross(m_x, y, xk, xv, m_kv):
            scope = ExitStack()
            with scope:
                xq = sb(scope, "xq", [P, DC, S])
                pr = sb(scope, "pr", [P, T, 4, S])
                nmax = sb(scope, "nmax_x", [P, T, 4])
                tot = sb(scope, "tot_x", [P, T, 4])
                pt = [sb(scope, f"ptx{i}", [P, 512]) for i in range(2)]
                m_h = norm_cols(x, "xa_pre_g_2", h_hi, h_lo, m_x)
                m_q = []
                for b in range(2):
                    i, ps, done = block(d["xa_wq_2"], DC, 512 * b, 512, h_hi, h_lo, m_h, "cols")
                    o = xq[:, 4 * b:4 * b + 4, :].rearrange("p c s -> p (c s)")
                    m_q.append(act.do(lambda e, o=o, ps=ps: e.copy(o, ps[:, :]), done))
                    give_pair(i, m_q[-1])
                m_p = []
                for t in range(T):
                    i, ps, free = take_pair()
                    for h in range(4):
                        for c in range(2):
                            done = mm(ps[:, h * S:(h + 1) * S], xq[:, 2 * h + c, t * P:(t + 1) * P], xk[:, 2 * h + c, :],
                                      h % 2 == 0 and c == 0, h % 2 == 1 and c == 1, free, m_q, m_kv, signal=h == 3 and c == 1)
                    pv_ = ps[:, :].rearrange("p (h s) -> p h s", h=4)
                    a = dve.do(lambda e, t=t, pv_=pv_: e.tensor_reduce(nmax[:, t, :], pv_, AX_X, ALU.max, negate=True), done)
                    a = dve.do(lambda e, t=t: e.tensor_scalar(nmax[:, t, :], nmax[:, t, :], 1.0 / 16, None, ALU.mult), a)
                    for h in range(4):
                        b = act.do(lambda e, t=t, h=h, pv_=pv_: e.activation(pr[:, t, h, :], pv_[:, h, :], ACT.Exp, bias=nmax[:, t, h:h + 1],
                                   scale=1.0 / 16, accum_out=tot[:, t, h:h + 1]), a)
                    give_pair(i, b)
                    b = dve.do(lambda e, t=t: e.reciprocal(tot[:, t, :], tot[:, t, :]), b)
                    m_p.append(dve.do(lambda e, t=t: e.tensor_tensor(pr[:, t], pr[:, t], bcast(tot[:, t, :], 2, S), ALU.mult), b))
                pt_free = [None, None]
                m_o = {}
                for h2 in range(2):
                    io, po, ofree = take_pair()
                    for hh in range(2):
                        h = 2 * h2 + hh
                        i, ps, free = take_pair()
                        for mt_ in range(2):
                            for t in range(T):
                                done = turn(ps[:, mt_ * S + t * P:mt_ * S + (t + 1) * P], pr[:, t, h, mt_ * P:(mt_ + 1) * P], free, m_p, signal=mt_ == 1 and t == 1)
                        b = h % 2
                        if b:
                            c = act.do(lambda e, b=b, ps=ps: e.copy(pt[b][:], ps[:, 0:512]), done, pt_free[b])
                        else:
                            c = dve.do(lambda e, b=b, ps=ps: e.tensor_copy(pt[b][:], ps[:, 0:512]), done, pt_free[b])
                        give_pair(i, c)
                        for dd in range(2):
                            o = po[:, (2 * hh + dd) * S:(2 * hh + dd + 1) * S]
                            for mt_ in range(2):
                                pt_free[b] = mm(o, xv[:, mt_, (2 * h + dd) * P:(2 * h + dd + 1) * P], pt[b][:, mt_ * S:(mt_ + 1) * S],
                                                dd == 0 and mt_ == 0, dd == 1 and mt_ == 1, c, ofree, signal=dd == 1 and mt_ == 1)
                    m = split_whole(h_hi[:, 4 * h2:4 * h2 + 4, :].rearrange("p c s -> p (c s)"),
                                    h_lo[:, 4 * h2:4 * h2 + 4, :].rearrange("p c s -> p (c s)"), po[:, :], pt_free)
                    give_pair(io, m)
                    for c in range(4):
                        m_o[4 * h2 + c] = m
                m_y = rows_to_y(d["xa_wo_2"], DC, h_hi, h_lo, m_o, y)
                return post_norm_add(y, "xa_post_g_2", s_small["post2"], 1.0, m_y, m_y[1])

        m = ffn(0, d["ffn1_w_gate"], d["ffn1_w_up"], d["ffn1_w_down"], "ffn1_norm", m_x)
        debug(0, m)
        m = mixer1(m)
        debug(1, m)
        m = ffn(1, d["ffn2_w_gate"], d["ffn2_w_up"], d["ffn2_w_down"], "ffn2_norm", m)
        debug(2, m)
        second = ExitStack()
        with second:
            y = sb(second, "y", [P, T, D])
            xk, xv = sb(second, "xk", [P, DC, S]), sb(second, "xv", [P, T, D])
            gain_buf.append(sb(second, "gain", [P, D]))
            m = ffn(2, d["ffn1_w_gate_2"], d["ffn1_w_up_2"], d["ffn1_w_down_2"], "ffn1_pre_g_2", m, y, "ffn1_post_g_2", s_small["post0"])
            debug(3, m)
            m, m_kv = mixer2(m, y, xk, xv)
            debug(4, m)
            m = cross(m, y, xk, xv, m_kv)
            debug(5, m)
            m = ffn(3, d["ffn2_w_gate_2"], d["ffn2_w_up_2"], d["ffn2_w_down_2"], "ffn2_pre_g_2", m, y, "ffn2_post_g_2", s_small["post3"])
        for t in range(T):
            last = sp.dma(out[t * P:(t + 1) * P, :], x[:, t, :], s_out, used, m[t])
        sp.wait(last)
        assert state["next"] == len(plan)

        blk = ctx.enter_context(nc.Block())
        blk.tensor(pe.run)
        blk.scalar(act.run)
        blk.vector(dve.run)
        blk.gpsimd(pool.run)
        blk.sync(sp.run)


_MATS = ["ffn1_w_gate", "ffn1_w_up", "ffn1_w_down", "w_in", "w_mq", "w_mk", "w_proj_a", "w_proj_b", "w_out",
         "ffn2_w_gate", "ffn2_w_up", "ffn2_w_down", "ffn1_w_gate_2", "ffn1_w_up_2", "ffn1_w_down_2", "w_in_2",
         "pool_w_2", "w_out_2", "xa_wq_2", "xa_wkv_2", "xa_wo_2", "ffn2_w_gate_2", "ffn2_w_up_2", "ffn2_w_down_2",
         "x", "mem_2"]
_ROWS = ["m_head_norm", "ffn1_post_g_2", "mix_post_g_2", "xa_post_g_2", "ffn2_post_g_2"]


def kernel(**inputs):
    import concourse.bacc as bacc
    from concourse.bass_utils import run_bass_kernel_spmd

    nc = bacc.Bacc("TRN2", target_bir_lowering=False, num_devices=1)
    arrays, d = {}, {}

    def declare(name, a):
        a = np.ascontiguousarray(a)
        arrays["in_" + name] = a
        d[name] = nc.dram_tensor("in_" + name, a.shape, mybir.dt.from_np(a.dtype), kind="ExternalInput").ap()

    for name in _MATS:
        declare(name, np.asarray(inputs[name])[0])
    for name in _ROWS:
        declare(name, np.asarray(inputs[name])[0])
    par = np.zeros((P, N_PARAMS), np.float32)
    for name, (a, b) in PARAM_COLS.items():
        v = np.asarray(inputs[name])[0]
        if name in ("q_norm", "k_norm", "idx_k_norm"):
            par[0:64, a], par[64:128, a] = v, v
        elif name in ("b_i", "b_f"):
            par[0:4, a] = v
        else:
            par[:, a:b] = v.reshape(b - a, P).T
    declare("params", par)
    declare("consts", shape_constants())
    out = nc.dram_tensor("out", (S, D), F32, kind="ExternalOutput").ap()
    dbg = nc.dram_tensor("dbg", (6, S, D), F32, kind="ExternalOutput").ap() if DEBUG else None
    build(nc, d, out, dbg)
    r = run_bass_kernel_spmd(nc, [arrays], core_ids=[0])
    got = r.results[0]["out"].reshape(1, S, D)
    if DEBUG:
        return (got, r.results[0]["dbg"])
    return got
```

```python
from contextlib import ExitStack

import concourse.bass as bass
import concourse.mybir as mybir
import numpy as np

F32 = mybir.dt.float32
F32R = mybir.dt.float32r
ACT = mybir.ActivationFunctionType
ALU = mybir.AluOpType
AX_X = mybir.AxisListType.X

P = 128
S = 256
T = S // P
D = 1024
DC = D // P
EPS = 1e-6
MASKED = -1e30
UNPICKED = -3e38
PICKED = -3.4e38
TOPK = S // 4
UNIT = 2048
STAGES = 3
SPLITS = 3
DEBUG = False


class Engine:

    def __init__(self, sem):
        self.sem, self.count, self.items, self.known = sem, 0, [], {}

    def wait(self, *marks):
        for m in marks:
            if m is None:
                continue
            if isinstance(m, list):
                self.wait(*m)
                continue
            sem, value = m
            if self.known.get(id(sem), 0) < value:
                self.known[id(sem)] = value
                self.items.append(lambda e, sem=sem, value=value: e.wait_ge(sem, value))

    def do(self, emit, *waits, signal=True):
        self.wait(*waits)
        if not signal:
            self.items.append(emit)
            return None
        self.count += 1
        self.items.append(lambda e: emit(e).then_inc(self.sem, 1))
        return (self.sem, self.count)

    def dma(self, out, in_, sem, used, *waits):
        self.wait(*waits)
        used[id(sem)] = used.get(id(sem), 0) + 16
        self.items.append(lambda e: e.dma_start(out, in_).then_inc(sem, 16))
        return (sem, used[id(sem)])

    def run(self, e):
        for item in self.items:
            item(e)


def bcast(ap, axis, n):
    a = ap.unsqueeze(axis)
    shape = list(a.shape)
    shape[axis] = n
    return a.to_broadcast(shape)


PARAM_COLS = {}


def param_columns():
    at = 0
    for name, n in (("q_norm", 1), ("k_norm", 1),
                    ("idx_k_norm", 1), ("conv_w", 16), ("conv_b", 4), ("pool_scale_2", 4), ("b_i", 1), ("b_f", 1)):
        PARAM_COLS[name] = (at, at + n)
        at += n
    return at


N_PARAMS = param_columns()
CONST_COLS = {"ident": (0, 128), "causal": (128, 384), "chunked": (384, 640), "alibi": (640, 2688),
              "inv_count": (2688, 3712), "head_rows": (3712, 4224)}
N_CONSTS = 4224


def shape_constants():
    c = np.zeros((P, N_CONSTS), np.float32)
    r = np.arange(P)[:, None]
    col = np.arange(P)[None, :]
    c[:, 0:128] = np.eye(P)
    causal = np.concatenate([np.zeros((P, P)), np.where(col <= r, 0.0, MASKED)], 1)
    c[:, 128:384] = causal
    c[:, 512:640] = np.where(col < (r // 64 + 1) * 64, 0.0, UNPICKED)
    dist = np.arange(S)[None, :] - (r + P)
    for group in range(2):
        for half in range(2):
            for jj in range(2):
                head = 2 * (2 * group + jj) + half
                at = 640 + ((group * 2 + half) * 2 + jj) * S
                slope = np.float32(2.0 ** (-8.0 * (head + 1) / 8))
                c[:, at:at + S] = np.where(dist <= 0, slope * dist, MASKED)
    for g, w in enumerate((2, 4, 8, 16)):
        c[:, 2688 + g * S:2688 + (g + 1) * S] = 1.0 / np.minimum(np.arange(S) + 1, w)
    for h in range(4):
        c[h, 3712 + h * P:3712 + (h + 1) * P] = 1.0
    return c


def build(nc, d, out, dbg):
    ctx = ExitStack()
    with ctx:
        def sb(scope, name, shape, dt=F32):
            return scope.enter_context(nc.sbuf_tensor(name, shape, dt))

        def sem(name):
            return ctx.enter_context(nc.semaphore(name))

        pe, act, dve, pool, sp = (Engine(sem("s_" + n)) for n in ("pe", "act", "dve", "pool", "sp"))
        used = {}
        s_stage = [sem(f"s_stage{i}") for i in range(STAGES)]
        s_x, s_par, s_out = [sem("s_x0"), sem("s_x1")], sem("s_par"), sem("s_out")
        s_small = {n: sem("s_" + n) for n in ("mix1", "mix2", "alibi", "mem", "post0", "post1", "post2", "post3")}
        s_gain, s_ident = sem("s_gain"), sem("s_ident")

        x = sb(ctx, "x", [P, T, D])
        xr = sb(ctx, "xr", [P, T, D])
        h_hi = sb(ctx, "h_hi", [P, DC, S], F32R)
        h_lo = sb(ctx, "h_lo", [P, DC, S], F32R)
        stage = [sb(ctx, f"stage{i}", [P, UNIT]) for i in range(STAGES)]
        w_hi = [sb(ctx, f"w_hi{i}", [P, UNIT], F32R) for i in range(SPLITS)]
        w_lo = [sb(ctx, f"w_lo{i}", [P, UNIT], F32R) for i in range(SPLITS)]
        par = sb(ctx, "par", [P, N_PARAMS])
        ident = sb(ctx, "ident", [P, P])
        causal = sb(ctx, "causal", [P, 2 * P])
        stat = sb(ctx, "stat", [P, T, 4])
        post_stat = sb(ctx, "post_stat", [P, T, 4])
        pre_gain = sb(ctx, "pre_gain", [P, D])
        half_pow = sb(ctx, "half_pow", [P, 32])
        pairs = [ctx.enter_context(nc.psum_tensor(f"pair{i}", [P, 1024], F32)) for i in range(4)]
        pair_free = [(i, []) for i in range(4)]

        def take_pair():
            i, waits = pair_free.pop(0)
            return i, pairs[i], waits

        def give_pair(i, *marks):
            pair_free.append((i, list(marks)))

        def col(name, c=0, rows=P):
            a = PARAM_COLS[name][0] + c
            return par[0:rows, a:a + 1]

        m_x = [sp.dma(x[:, 0, :], d["x"][0:P, :], s_x[0], used)]
        m_ident = sp.dma(ident[:], d["consts"][:, 0:128], s_ident, used)
        m_pow = pool.do(lambda e: e.memset(half_pow[:], -0.5))
        m_first_gain = pool.dma(pre_gain[:], d["ffn1_norm"].partition_broadcast(P), s_gain, used)
        pool.dma(par[:], d["params"], s_par, used)
        m_par = pool.dma(causal[:], d["consts"][:, 128:384], s_par, used)

        plan = []

        def unit_chunks(K, nw):
            fit = min(K, UNIT // nw)
            return 4 if K == DC and 4 <= fit < 8 else fit

        def plan_block(w, K, n0, nw, rows=None, share=False, ks=None):
            kc = unit_chunks(K, nw)
            for k0 in range(0, K, kc) if ks is None else [ks]:
                k1 = min(K, k0 + kc)
                if rows:
                    srcs = rows(k0, k1, n0, nw)
                else:
                    v = w.rearrange("(k p) n -> p k n", p=P)
                    srcs = [(slice(0, P), slice(0, nw), v[:, k0:k1, n0:n0 + nw])]
                plan.append((w, k0, k1, n0, nw, srcs, share and k0 == 0))

        state = {"next": 0, "hi": 0, "lo": 0, "loaded": 0}
        m_load, m_hi, m_lo, m_used = {}, {}, {}, {}

        def load_unit(u):
            _, k0, k1, _, nw, srcs, _ = plan[u]
            dst = stage[u % STAGES][:, 0:(k1 - k0) * nw].rearrange("p (k n) -> p k n", n=nw)
            held = [m_hi[u - STAGES], m_lo[u - STAGES]] if u >= STAGES else []
            for parts, cols, src in srcs:
                m_load[u] = sp.dma(dst[parts, :, cols], src, s_stage[u % STAGES], used, *held)

        def split_parts(u):
            _, k0, k1, _, nw, _, _ = plan[u]
            n = (k1 - k0) * nw
            held = m_used[u - SPLITS] if u >= SPLITS else None
            return stage[u % STAGES][:, 0:n], w_hi[u % SPLITS][:, 0:n], w_lo[u % SPLITS][:, 0:n], held

        def queue_hi(end=None):
            while state["hi"] < (end or len(plan)) and (state["hi"] < SPLITS or state["hi"] - SPLITS in m_used):
                u = state["hi"]
                src, hi, _, held = split_parts(u)
                m_hi[u] = act.do(lambda e, hi=hi, src=src: e.copy(hi, src), m_load[u], held)
                if plan[u][6]:
                    queue_lo(pool)
                state["hi"] += 1

        def queue_lo(engine=None):
            while state["lo"] < state["hi"] + (engine is pool):
                u = state["lo"]
                src, hi, lo, held = split_parts(u)
                on = pool if plan[u][6] else dve
                m_lo[u] = on.do(lambda e, hi=hi, src=src, lo=lo: e.tensor_tensor(lo, src, hi.bitcast(F32), ALU.subtract), m_hi[u], held)
                state["lo"] += 1
                if state["loaded"] < len(plan):
                    load_unit(state["loaded"])
                    state["loaded"] += 1

        def queue_splits(end=None):
            queue_hi(end)
            queue_lo()

        def take_unit(w, k0, n0):
            u = state["next"]
            assert plan[u][0] is w and plan[u][1] == k0 and plan[u][3] == n0, (u, k0, n0)
            assert u < state["lo"]
            state["next"] += 1
            return u

        class Block:

            def __init__(self, w, K, n0, nw, hi, lo, ready, form, evac):
                self.w, self.K, self.n0, self.nw, self.hi, self.lo, self.form, self.evac = w, K, n0, nw, hi, lo, form, evac
                self.ready = ready if callable(ready) else (lambda k, t: ready[k])
                self.begun, self.ps, self.left = set(), None, [K] * T
                self.kc = unit_chunks(K, nw)
                self.units = [(k0, min(K, k0 + self.kc)) for k0 in range(0, K, self.kc)]

            def complete(self, t):
                return self.left[t] == 0

            def take(self, k0):
                if self.ps is None:
                    self.i, self.ps, free = take_pair()
                    pe.wait(free)
                return take_unit(self.w, k0, self.n0)

            def multiply(self, u, k0, k1, ts):
                nw, form = self.nw, self.form
                w_h = w_hi[u % SPLITS][:, 0:(k1 - k0) * nw].rearrange("p (k n) -> p k n", n=nw)
                w_l = w_lo[u % SPLITS][:, 0:(k1 - k0) * nw].rearrange("p (k n) -> p k n", n=nw)
                pe.wait(m_hi[u], m_lo[u])
                c0, c1 = ts[0] * P, (ts[-1] + 1) * P
                groups = list(ts) if form == "rows" else list(range(nw // P))
                for t in ts:
                    self.left[t] -= k1 - k0
                for k in range(k0, k1):
                    for t in ts:
                        pe.wait(self.ready(k, t))
                    for g in groups:
                        if form == "rows":
                            o, bank = self.ps[:, g * 512:g * 512 + nw], g
                            a_h, a_l = self.hi[:, k, g * P:(g + 1) * P], self.lo[:, k, g * P:(g + 1) * P]
                            ops = [(a_h, w_h[:, k - k0, :]), (a_l, w_h[:, k - k0, :]), (a_h, w_l[:, k - k0, :])]
                        else:
                            o, bank = self.ps[:, g * S + c0:g * S + c1], g // 2
                            b_h, b_l = w_h[:, k - k0, g * P:(g + 1) * P], w_l[:, k - k0, g * P:(g + 1) * P]
                            ops = [(b_h, self.hi[:, k, c0:c1]), (b_h, self.lo[:, k, c0:c1]), (b_l, self.hi[:, k, c0:c1])]
                        for j, (l, r) in enumerate(ops):
                            first = bank not in self.begun
                            self.begun.add(bank)
                            done = pe.do(lambda e, o=o, l=l, r=r, first=first, stop=(self.left[ts[-1]] == 0 and k == k1 - 1 and j == 2):
                                         e.matmul(o, l, r, start=first, stop=stop, skip_group_check=True),
                                         signal=k == k1 - 1 and g == groups[-1] and j == 2)
                return done

        side = []

        def tick():
            for g in list(side):
                try:
                    next(g)
                except StopIteration:
                    side.remove(g)

        def after_unit(lo=True):
            queue_hi()
            tick()
            if lo:
                queue_lo()

        def drain(*gens):
            while any(g in side for g in gens) if gens else side:
                tick()

        def by_chunks(blocks, ks):
            return [(b, k0, k1) for k in ks for b in blocks for k0, k1 in b.units if k0 == k]

        def products(blocks, head=None, tail=None, then=None, steps=None):
            steps = steps or [(b, k0, k1) for b in blocks for k0, k1 in b.units]
            n_head = min(SPLITS, len(steps)) if head else 0
            n_tail = min(SPLITS, len(steps)) if tail else 0
            assert n_head + n_tail <= len(steps)
            queue_splits()
            taken = []
            for n, (b, k0, k1) in enumerate(steps[:n_head]):
                taken.append(b.take(k0))
                b.multiply(taken[n], k0, k1, [0])
                if n == min(1, n_head - 1):
                    head()
            for n, (b, k0, k1) in enumerate(steps[:n_head]):
                m_used[taken[n]] = done = b.multiply(taken[n], k0, k1, [1])
                if b.complete(1):
                    b.evac(b, done, None)
                after_unit()
            for b, k0, k1 in steps[n_head:len(steps) - n_tail]:
                u = b.take(k0)
                m_used[u] = done = b.multiply(u, k0, k1, [0, 1])
                if then and (b, k0) == steps[-1][:2]:
                    then()
                if b.complete(0):
                    b.evac(b, done, None)
                after_unit(lo=not (then and len(steps) > 1 and (b, k0) == steps[-2][:2]))
            if not tail:
                return
            drain()
            last = steps[len(steps) - n_tail:]
            taken = []
            for n, (b, k0, k1) in enumerate(last):
                taken.append(b.take(k0))
                done = b.multiply(taken[n], k0, k1, [0])
                if b.complete(0):
                    b.evac(b, done, 0)
            tail.stats(0)
            for n, (b, k0, k1) in enumerate(last):
                if n == n_tail - 1:
                    tail.turn(0)
                    queue_splits()
                m_used[taken[n]] = done = b.multiply(taken[n], k0, k1, [1])
                if b.complete(1):
                    b.evac(b, done, 1)
                if n < n_tail - 2:
                    queue_splits()
            tail.stats(1)
            queue_splits()

        def mm(o, l, r, start, stop, *waits, signal=False):
            return pe.do(lambda e: e.matmul(o, l, r, start=start, stop=stop, skip_group_check=True), *waits, signal=signal)

        def turn(o, i_, *waits, signal=False):
            n = i_.shape[0]
            return pe.do(lambda e: e.transpose(o, i_, ident[0:n, 0:n]), *waits, signal=signal)

        def inverse_root(r, ss, n, width, *waits):
            a = pool.do(lambda e: e.tensor_scalar(r, ss, 1.0 / width, EPS, ALU.mult, ALU.add), *waits)
            return pool.do(lambda e: e.tensor_tensor(r, r, half_pow[:, 0:n], ALU.pow), a, m_pow)

        def split_whole(hi, lo, src, *waits):
            a = act.do(lambda e: e.copy(hi, src), *waits)
            b = dve.do(lambda e: e.tensor_tensor(lo, src, hi.bitcast(F32), ALU.subtract), a, *waits)
            return [a, b]

        def split_gained(hi, lo, ps, gains, done, *waits):
            marks = []
            for bank in range(2):
                cs = (2 * bank, 2 * bank + 1)
                for c in cs:
                    a = act.do(lambda e, c=c: e.activation(hi[:, c, :], ps[:, c * S:(c + 1) * S], ACT.Copy, scale=gains[c]), done[bank], *waits)
                for c in cs:
                    b = dve.do(lambda e, c=c: e.scalar_tensor_tensor(
                        lo[:, c, :], ps[:, c * S:(c + 1) * S], gains[c], hi[:, c, :].bitcast(F32), ALU.mult, ALU.subtract), a, *waits)
                    marks.append([a, b])
            return marks

        gain_buf = []
        xr_free = [[], []]
        gain_free = [[]]

        class Norm:

            def __init__(self, src, gain, hi, lo, m_gain=None):
                self.src, self.hi, self.lo = src, hi, lo
                self.m_src = [[None, None], [None, None]]
                self.m_part = [[None, None], [None, None]]
                self.m_xr, self.marks = [None] * T, {}
                self.m_gain = m_gain or pool.dma(pre_gain[:], d[gain].partition_broadcast(P), s_gain, used, gain_free[0])

            def part(self, t, half, *marks):
                cols = slice(512 * half, 512 * half + 512)
                self.m_src[t][half] = list(marks)
                self.m_part[t][half] = act.do(lambda e: e.activation(
                    xr[:, t, cols], self.src[:, t, cols], ACT.Square, accum_out=stat[:, t, half:half + 1]), list(marks), xr_free[t])

            def stats(self, t):
                ss0, ss1, ms, r = (stat[:, t, n:n + 1] for n in range(4))
                a = dve.do(lambda e: e.tensor_scalar(ms, ss0, 1.0 / D, EPS, ALU.mult, ALU.add), self.m_part[t][0])
                a = dve.do(lambda e: e.scalar_tensor_tensor(ms, ss1, 1.0 / D, ms, ALU.mult, ALU.add), self.m_part[t][1], a)
                a = pool.do(lambda e: e.tensor_tensor(r, ms, half_pow[:, 0:1], ALU.pow), a, m_pow)
                self.m_xr[t] = []
                for half in range(2):
                    cols = slice(512 * half, 512 * half + 512)
                    self.m_xr[t].append(dve.do(lambda e, cols=cols: e.scalar_tensor_tensor(
                        xr[:, t, cols], self.src[:, t, cols], r, pre_gain[:, cols], ALU.mult, ALU.mult),
                        a, self.m_gain, self.m_src[t][half]))
                if t == T - 1:
                    gain_free[0] = self.m_xr[t]

            def turn(self, t):
                i, ps, free = take_pair()
                for bank in range(2):
                    for c in range(4):
                        k = 4 * bank + c
                        done = turn(ps[:, k * P:(k + 1) * P], xr[:, t, k * P:(k + 1) * P], free, self.m_xr[t][bank], m_ident, signal=c == 3)
                    ks, cols = slice(4 * bank, 4 * bank + 4), slice(t * P, (t + 1) * P)
                    src = ps[:, bank * 512:(bank + 1) * 512].rearrange("p (k s) -> p k s", k=4)
                    m = split_whole(self.hi[:, ks, cols], self.lo[:, ks, cols], src, done)
                    for c in range(4):
                        self.marks[4 * bank + c, t] = m
                xr_free[t] = done
                give_pair(i, m, self.marks[0, t])

            def ready(self, k, t):
                return self.marks[k, t]

        class Finish:

            def __init__(self):
                self.m_src = [[], []]

            def part(self, t, half, *marks):
                self.m_src[t].append(list(marks))

            def stats(self, t):
                sp.dma(out[t * P:(t + 1) * P, :], x[:, t, :], s_out, used, self.m_src[t])

            def turn(self, t):
                pass

        def debug(k, n):
            if dbg is not None:
                m = n.m_xr[1]
                for t in range(T):
                    sp.dma(dbg[k, t * P:(t + 1) * P, :], x[:, t, :], s_out, used, m)

        FF = d["ffn1_w_gate"].shape[1]
        FC = FF // P
        ff_blocks = [(n, min(512, FF - n)) for n in range(0, FF, 512)]
        IN = {"q": 0, "kv": 512, "iq": 768, "ik_iw": 1280, "mx": 1352, "mv": 1864, "mi_mf": 2376, "mo": 2384,
              "ga": 2896, "gb": 3920}
        w_in, w_in2 = d["w_in"], d["w_in_2"]

        def ffn_plan(gate, up, down):
            for n, nw in ff_blocks:
                plan_block(gate, DC, n, nw)
                plan_block(up, DC, n, nw)
            for n in range(0, D, 512):
                plan_block(down, FC, n, 512)

        def narrow_rows(k0, k1, n0, nw):
            v = w_in.rearrange("(k p) n -> p k n", p=P)
            return [(slice(0, P), slice(0, 256), v[:, k0:k1, IN["kv"]:IN["kv"] + 256]),
                    (slice(0, P), slice(256, 328), v[:, k0:k1, IN["ik_iw"]:IN["ik_iw"] + 72]),
                    (slice(0, P), slice(328, 336), v[:, k0:k1, IN["mi_mf"]:IN["mi_mf"] + 8])]

        def proj_a_rows(k0, k1, n0, nw):
            v = d["w_proj_a"].rearrange("(g j q) n -> g q j n", g=2, j=4)
            return [(slice(64 * g, 64 * g + 64), slice(0, nw), v[g, :, k0:k1, n0:n0 + nw]) for g in range(2)]

        ffn_plan(d["ffn1_w_gate"], d["ffn1_w_up"], d["ffn1_w_down"])
        plan_block(w_in, DC, IN["q"], 512)
        plan_block(w_in, DC, IN["kv"], 336, narrow_rows)
        plan_block(w_in, DC, IN["iq"], 512)
        for n in ("mx", "mv", "mo"):
            plan_block(w_in, DC, IN[n], 512, share=True)
        for n in ("ga", "gb"):
            for b in range(2):
                plan_block(w_in, DC, IN[n] + 512 * b, 512, share=True)
        for b in range(2):
            plan_block(d["w_proj_a"], 4, 512 * b, 512, proj_a_rows)
        for b in range(2):
            plan_block(d["w_proj_b"], 4, 512 * b, 512)
        for b in range(2):
            plan_block(d["w_out"], DC, 512 * b, 512)
        ffn_plan(d["ffn2_w_gate"], d["ffn2_w_up"], d["ffn2_w_down"])
        ffn_plan(d["ffn1_w_gate_2"], d["ffn1_w_up_2"], d["ffn1_w_down_2"])
        plan_block(d["xa_wkv_2"], DC, 0, 512)
        for b in (2, 0, 1, 3):
            plan_block(w_in2, DC, 512 * b, 512, share=b not in (0, 2))
        plan_block(d["xa_wkv_2"], DC, 512, 512)
        for k in (4, 0):
            for b in range(2):
                plan_block(d["w_out_2"], DC, 512 * b, 512, ks=k)
        plan_block(d["xa_wkv_2"], DC, 1024, 512)
        for b in range(2):
            plan_block(d["xa_wq_2"], DC, 512 * b, 512)
        plan_block(d["xa_wkv_2"], DC, 1536, 512)
        for k in (0, 4):
            for b in range(2):
                plan_block(d["xa_wo_2"], DC, 512 * b, 512, ks=k)
        ffn_plan(d["ffn2_w_gate_2"], d["ffn2_w_up_2"], d["ffn2_w_down_2"])
        for u in range(STAGES):
            load_unit(u)
            if u == 0:
                m_x.append(sp.dma(x[:, 1, :], d["x"][P:2 * P, :], s_x[1], used))
        state["loaded"] = STAGES

        def post_blocks(w, K, a_hi, a_lo, ready, y, gain_name, s_g, weight, nxt, m_gain_free):
            gb = gain_buf[0]
            m_gb = pool.dma(gb[:], d[gain_name].partition_broadcast(P), s_g, used, m_gain_free)
            m_y, m_ss = {}, {}

            def evac(half):
                def run(b, done, t_only):
                    cols = slice(512 * half, 512 * half + 512)
                    for t in ([t_only] if t_only is not None else range(T)):
                        src = b.ps[:, t * 512:(t + 1) * 512]
                        ss0, ss1, ms, r = (post_stat[:, t, n:n + 1] for n in range(4))
                        m_ss[t, half] = act.do(lambda e, src=src, t=t: e.activation(
                            xr[:, t, cols], src, ACT.Square, accum_out=post_stat[:, t, half:half + 1]), done, xr_free[t])
                        m_y[t, half] = act.do(lambda e, src=src, t=t: e.copy(y[:, t, cols], src), done)
                        if half == 0:
                            continue
                        a = dve.do(lambda e, ms=ms, ss0=ss0: e.tensor_scalar(ms, ss0, 1.0 / D, EPS, ALU.mult, ALU.add), m_ss[t, 0])
                        a = dve.do(lambda e, ms=ms, ss1=ss1: e.scalar_tensor_tensor(ms, ss1, 1.0 / D, ms, ALU.mult, ALU.add), m_ss[t, 1], a)
                        a = pool.do(lambda e, ms=ms, r=r: e.tensor_tensor(r, ms, half_pow[:, 0:1], ALU.pow), a, m_pow)
                        if t_only == 1:
                            queue_hi()
                        for h in range(2):
                            c2 = slice(512 * h, 512 * h + 512)
                            m = dve.do(lambda e, t=t, r=r, c2=c2: e.scalar_tensor_tensor(
                                y[:, t, c2], y[:, t, c2], r, gb[:, c2], ALU.mult, ALU.mult), a, m_gb, m_y[t, h])
                            m = dve.do(lambda e, t=t, c2=c2: e.scalar_tensor_tensor(
                                x[:, t, c2], y[:, t, c2], weight, x[:, t, c2], ALU.mult, ALU.add), m)
                            nxt.part(t, h, m)
                    if t_only != 0:
                        give_pair(b.i, m_y[1, half], m_y[0, half])
                return run
            return [Block(w, K, 512 * h, 512, a_hi, a_lo, ready, "rows", evac(h)) for h in range(2)]

        def add_blocks(w, K, a_hi, a_lo, ready, weight, nxt):
            def evac(half):
                def run(b, done, t_only):
                    for t in ([t_only] if t_only is not None else range(T)):
                        xt, src = x[:, t, 512 * half:512 * half + 512], b.ps[:, t * 512:(t + 1) * 512]
                        m = dve.do(lambda e, xt=xt, src=src: e.scalar_tensor_tensor(xt, src, weight, xt, ALU.mult, ALU.add), done)
                        nxt.part(t, half, m)
                    if t_only != 0:
                        give_pair(b.i, m)
                return run
            return [Block(w, K, 512 * h, 512, a_hi, a_lo, ready, "rows", evac(h)) for h in range(2)]

        def ffn(n_ffn, gate, up, down, norm, make_next, post=None):
            scope = ExitStack()
            with scope:
                f_hi = sb(scope, f"f_hi{n_ffn}", [P, FC, S], F32R)
                f_lo = sb(scope, f"f_lo{n_ffn}", [P, FC, S], F32R)
                act_buf = [sb(scope, f"act_buf{n_ffn}_{i}", [P, 1024]) for i in range(2)]
                buf_free = [None, None]
                m_silu, m_f = {}, {}

                def turn_rows(s_, k, a):
                    yield
                    i, ps, free = take_pair()
                    for c in range(4):
                        for t in range(T):
                            done = turn(ps[:, c * S + t * P:c * S + (t + 1) * P], s_[:, t * 512 + c * P:t * 512 + (c + 1) * P],
                                        free, a, signal=c == 3 and t == 1)
                    m = split_whole(f_hi[:, k:k + 4, :].rearrange("p k s -> p (k s)"), f_lo[:, k:k + 4, :].rearrange("p k s -> p (k s)"),
                                    ps[:, :], done)
                    give_pair(i, m)
                    buf_free[0] = done
                    for c in range(4):
                        m_f[k + c] = m

                def evac_gate(b, done, _):
                    n = b.n0 // 512
                    w = b.nw // P * S
                    s_, ps = act_buf[n % 2][:, 0:w], b.ps[:, 0:w]
                    a = act.do(lambda e: e.activation(s_, ps, ACT.Sigmoid), done, buf_free[n % 2])
                    m_silu[n] = dve.do(lambda e: e.tensor_tensor(s_, s_, ps, ALU.mult), a)
                    give_pair(b.i, m_silu[n])

                def evac_up(b, done, _):
                    n, k = b.n0 // 512, b.n0 // P
                    w = b.nw // P * S
                    s_, ps = act_buf[n % 2][:, 0:w], b.ps[:, 0:w]
                    a = dve.do(lambda e: e.tensor_tensor(s_, s_, ps, ALU.mult), m_silu[n], done)
                    give_pair(b.i, a)
                    if b.form == "rows":
                        side.append(turn_rows(s_, k, a))
                        return
                    hi = f_hi[:, k:k + b.nw // P, :].rearrange("p k s -> p (k s)")
                    lo = f_lo[:, k:k + b.nw // P, :].rearrange("p k s -> p (k s)")
                    buf_free[n % 2] = split_whole(hi, lo, s_, a)
                    for c in range(b.nw // P):
                        m_f[k + c] = buf_free[n % 2]

                up_blocks = []
                for n, nw in ff_blocks:
                    form = "rows" if n == 0 else "cols"
                    up_blocks.append(Block(gate, DC, n, nw, h_hi, h_lo, norm.ready, form, evac_gate))
                    up_blocks.append(Block(up, DC, n, nw, h_hi, h_lo, norm.ready, form, evac_up))
                products(up_blocks, head=lambda: norm.turn(1))
                nxt = make_next()
                if post:
                    down_blocks = post_blocks(down, FC, f_hi, f_lo, m_f, post[0], post[1], post[2], 0.5, nxt, norm.marks[7, 1])
                else:
                    down_blocks = add_blocks(down, FC, f_hi, f_lo, m_f, 0.5, nxt)
                products(down_blocks, tail=nxt)
                return nxt

        def attention(name, scope, qT, kT_of, v_of, mask_ops, marks, o_hi, o_lo, sc, pt):
            nmax = sb(scope, f"nmax_{name}", [P, T, 8])
            tot = sb(scope, f"tot_{name}", [P, T, 8])
            m_p = []
            for t in range(T):
                w = P * (t + 1)
                groups = [range(4)] if t == 0 else [range(0, 2), range(2, 4)]
                for g, js in enumerate(groups):
                    n = len(js)
                    i, ps, free = take_pair()
                    for half in range(2):
                        for jj, j in enumerate(js):
                            o = ps[:, half * 512 + jj * w:half * 512 + (jj + 1) * w]
                            r = slice(64 * half, 64 * half + 64)
                            done = mm(o, qT[r, j, t * P:(t + 1) * P], kT_of(half, j)[:, 0:w], jj == 0, jj == n - 1,
                                      free, marks["q"], marks["k"], signal=half == 1 and jj == n - 1)
                    dst = sc[t][:, g * 4:g * 4 + 2 * n, :]
                    src = ps[:, :].rearrange("p (h w) -> p h w", w=w)
                    m_s = []
                    for lo_, hi_, mask in mask_ops(t, g):
                        m_s.append(dve.do(lambda e, dst=dst, src=src, lo_=lo_, hi_=hi_, mask=mask: e.scalar_tensor_tensor(
                            dst[:, lo_:hi_, :], src[:, lo_:hi_, :], 0.125, mask, ALU.mult, ALU.add), done, marks[f"mask{t}"]))
                    give_pair(i, *m_s)
                    h0 = g * 4
                    nm = nmax[:, t, h0:h0 + 2 * n]
                    a = dve.do(lambda e, nm=nm, dst=dst: e.tensor_reduce(nm, dst, AX_X, ALU.max, negate=True), m_s)
                    for h in range(2 * n):
                        b = act.do(lambda e, h=h, dst=dst, t=t, h0=h0: e.activation(
                            dst[:, h, :], dst[:, h, :], ACT.Exp, bias=nmax[:, t, h0 + h:h0 + h + 1],
                            accum_out=tot[:, t, h0 + h:h0 + h + 1]), a)
                    tt = tot[:, t, h0:h0 + 2 * n]
                    b = dve.do(lambda e, tt=tt: e.reciprocal(tt, tt), b)
                    m_p.append(dve.do(lambda e, dst=dst, tt=tt, n=n, w=w: e.tensor_tensor(dst, dst, bcast(tt, 2, w), ALU.mult), b))
                    yield
            pt_free, turned = [None] * 4, {}
            io, po, ofree = take_pair()
            begun = set()
            for j in range(5):
                if j < 4:
                    i, ps, free = take_pair()
                    at0, at1 = (j, 4 + j), ((j // 2) * 4 + j % 2, (j // 2) * 4 + 2 + j % 2)
                    for half in range(2):
                        o = half * 512
                        turn(ps[:, o:o + P], sc[0][:, at0[half], :], free, m_p[0], m_p[1 + j // 2])
                        turn(ps[:, o + P:o + 2 * P], sc[1][:, at1[half], 0:P])
                        done = turn(ps[:, o + 2 * P:o + 3 * P], sc[1][:, at1[half], P:2 * P], signal=True)
                        b, src = 2 * (j % 2) + half, ps[:, o:o + 384]
                        turned[j, half] = act.do(lambda e, b=b, src=src: e.copy(pt[b], src), done, pt_free[b])
                    give_pair(i, turned[j, 0], turned[j, 1])
                for half in range(2 if j else 0):
                    q, b = j - 1, 2 * ((j - 1) % 2) + half
                    o = po[64 * half:64 * half + 64, q * S:(q + 1) * S]
                    key = (q // 2, half)
                    mm(o, v_of(0, half, q), pt[b][:, 0:S], key not in begun, False, turned[q, half], ofree, marks["v"])
                    begun.add(key)
                    pt_free[b] = mm(o[:, P:S], v_of(1, half, q), pt[b][:, S:384], False, True, signal=True)
                if j < 4:
                    yield
            a = act.do(lambda e: e.copy(o_hi, po[:, :]), pt_free)
            b = dve.do(lambda e: e.tensor_tensor(o_lo, po[:, :], o_hi.bitcast(F32), ALU.subtract), a)
            give_pair(io, a, b)
            marks["out"] = [a, b]

        def mixer1(norm, make_next):
            m_x = norm.m_xr[1]
            scope = ExitStack()
            with scope:
                ya_hi, ya_lo = sb(scope, "ya_hi", [P, 4, S], F32R), sb(scope, "ya_lo", [P, 4, S], F32R)
                yb_hi, yb_lo = sb(scope, "yb_hi", [P, 4, S], F32R), sb(scope, "yb_lo", [P, 4, S], F32R)
                xpad = sb(scope, "xpad", [P, 4, S + 3])
                mv, mo = sb(scope, "mv", [P, T, 512]), sb(scope, "mo", [P, T, 512])
                kvn = sb(scope, "kvn", [P, T, 336])
                ga, gb = sb(scope, "ga", [P, DC, S]), sb(scope, "gb", [P, DC, S])
                w_mq, w_mk = sb(scope, "w_mq", [P, 4, 64]), sb(scope, "w_mk", [P, 4, 64])
                head_g = sb(scope, "head_g", [P, 512])
                chunked = sb(scope, "chunked", [P, 2 * P])
                q_raw = sb(scope, "q_raw", [P, T, 512])
                q_nrm = sb(scope, "q_nrm", [P, T, 640])
                rr = sb(scope, "rr", [P, 22])
                ikk = sb(scope, "ikk", [P, T, 2, 64])
                qT, kT, ikT = sb(scope, "qT", [P, 4, S]), sb(scope, "kT", [P, S]), sb(scope, "ikT", [P, S])
                iqT = sb(scope, "iqT", [P, 4, S])
                work = [sb(scope, f"work{t}", [P, P * (t + 1)]) for t in range(T)]
                top = sb(scope, "top", [P, 8])
                big = sb(scope, "big", [P, 2 * 1024])
                mq, mk = sb(scope, "mq", [P, 2, S]), sb(scope, "mk", [P, 2, S])
                dm = [sb(scope, f"dm{t}", [P, 4, P * (t + 1)]) for t in range(T)]
                mt, nmt, ft, den = (sb(scope, n_, [P, T, 4]) for n_ in ("mt", "nmt", "ft", "den"))
                wt = [sb(scope, f"wt{i}", [P, 384]) for i in range(2)]
                rh = sb(scope, "rh", [P, T * 4])
                xc, sg = xr[:, 0, :].rearrange("p (c s) -> p c s", c=4), xr[:, 1, :].rearrange("p (c s) -> p c s", c=4)
                gi, gf, gt, ones = (xr[0:4, 1, n_ * S:(n_ + 1) * S] for n_ in range(4))
                s_m = s_small["mix1"]
                pool.dma(chunked[:], d["consts"][:, 384:640], s_m, used, m_x)
                pool.dma(head_g[:], d["m_head_norm"].partition_broadcast(P), s_m, used)
                pool.dma(w_mq[:], d["w_mq"].rearrange("h c q -> c h q"), s_m, used)
                m_const = pool.dma(w_mk[:], d["w_mk"].rearrange("h c q -> c h q"), s_m, used)
                m_zero = pool.do(lambda e: e.memset(xpad[:, :, 0:3], 0.0))
                m = {}
                flat = lambda ap: ap.rearrange("p t n -> p (t n)")

                def evac(name, out_ap, func=ACT.Copy, view=lambda ps: ps[:, :]):
                    def run(b, done, _):
                        m[name] = act.do(lambda e: e.activation(out_ap, view(b.ps), func), done, m_x)
                        give_pair(b.i, m[name])
                    return run

                def attention_chain():
                    while "kvn" not in m:
                        yield
                    rik, sq_ik, ik = rr[:, 20:22], ikk[:, :, 0, :], kvn[:, :, 256:320]
                    a = dve.do(lambda e: e.tensor_tensor(sq_ik, ik, ik, ALU.mult), m["kvn"])
                    a = dve.do(lambda e: e.tensor_reduce(rik, sq_ik, AX_X, ALU.add), a)
                    a = inverse_root(rik, rik, 2, 64, a)
                    m_ikk = [dve.do(lambda e, c=c: e.tensor_tensor(ikk[:, :, c, :], ik, bcast(rik, 2, 64), ALU.mult), a) for c in range(2)]
                    qn = q_nrm[:, :, 0:512]
                    k_raw, kn = kvn[:, :, 0:128], q_nrm[:, :, 512:640]
                    a = dve.do(lambda e: e.tensor_tensor(qn, q_raw[:], q_raw[:], ALU.mult), m["q"])
                    b = dve.do(lambda e: e.tensor_tensor(kn, k_raw, k_raw, ALU.mult))
                    for t in range(T):
                        c = dve.do(lambda e, t=t: e.tensor_reduce(rr[:, t * 10:t * 10 + 10], q_nrm[:, t, :].rearrange("p (g q) -> p g q", q=64), AX_X, ALU.add), a, b)
                    m_rr = inverse_root(rr[:, 0:20], rr[:, 0:20], 20, 64, c)
                    yield
                    i, ps, free = take_pair()
                    for t in range(T):
                        done = turn(ps[:, t * P:(t + 1) * P], ikk[:, t, :, :].rearrange("p c q -> p (c q)"), free, m_ikk, signal=t == 1)
                    m_ik = dve.do(lambda e, ps=ps: e.tensor_scalar(ikT[:], ps[:, 0:S], col("idx_k_norm"), None, ALU.mult), done)
                    give_pair(i, m_ik)
                    while "iq" not in m:
                        yield
                    yield
                    n_relu, relu_free, m_top = 0, [None, None], None
                    m_n = []
                    for t in range(T):
                        w = P * (t + 1)
                        a = None
                        for js in ([range(4)] if t == 0 else [range(0, 2), range(2, 4)]):
                            i, ps, free = take_pair()
                            for half in range(2):
                                for jj, j in enumerate(js):
                                    r = slice(64 * half, 64 * half + 64)
                                    done = mm(ps[:, half * 512 + jj * w:half * 512 + (jj + 1) * w], iqT[r, j, t * P:(t + 1) * P],
                                              ikT[r, 0:w], jj == 0, jj == len(js) - 1, free, m["iq"], m_ik,
                                              signal=half == 1 and jj == len(js) - 1)
                            rb = big[:, 1024 * (n_relu % 2):1024 * (n_relu % 2) + 1024]
                            m_scored = done
                            m_r = act.do(lambda e, rb=rb, ps=ps: e.activation(rb, ps[:, :], ACT.Relu), done, relu_free[n_relu % 2])
                            give_pair(i, m_r)
                            for half in range(2):
                                for jj, j in enumerate(js):
                                    head = 2 * j + half
                                    src, iw = rb[:, half * 512 + jj * w:half * 512 + (jj + 1) * w], kvn[:, t, 320 + head:321 + head]
                                    if a is None:
                                        a = dve.do(lambda e, src=src, iw=iw, t=t: e.tensor_scalar(work[t][:], src, iw, None, ALU.mult), m_r)
                                    else:
                                        a = dve.do(lambda e, src=src, iw=iw, t=t: e.scalar_tensor_tensor(
                                            work[t][:], src, iw, work[t][:], ALU.mult, ALU.add), m_r, a)
                            relu_free[n_relu % 2] = a
                            n_relu += 1
                            if t == 0:
                                for u in range(T):
                                    src = q_raw[:, u, :].rearrange("p (g j q) -> p g j q", g=2, j=4)
                                    dst = q_nrm[:, u, 0:512].rearrange("p (j g q) -> p g j q", g=2, j=4)
                                    r = rr[:, u * 10:u * 10 + 8].rearrange("p (g j) -> p g j", g=2)
                                    m_n.append(dve.do(lambda e, src=src, dst=dst, r=r: e.tensor_tensor(dst, src, bcast(r, 3, 64), ALU.mult), m_rr))
                                    src, r = kvn[:, u, 0:128].rearrange("p (g q) -> p g q", q=64), rr[:, u * 10 + 8:u * 10 + 10]
                                    dst = q_nrm[:, u, 512:640].rearrange("p (g q) -> p g q", q=64)
                                    m_n.append(dve.do(lambda e, src=src, dst=dst, r=r: e.tensor_tensor(dst, src, bcast(r, 2, 64), ALU.mult)))
                            yield
                        mask = chunked[:, P:2 * P] if t == 0 else chunked[:, :]
                        a = dve.do(lambda e, t=t, mask=mask: e.scalar_tensor_tensor(
                            work[t][:], work[t][:], (64 ** -0.5) * (8 ** -0.5), mask, ALU.mult, ALU.add), a, m_const)
                        for n in range(TOPK // 8):
                            a = dve.do(lambda e, t=t: e.max(top[:], work[t][:]), a, m_top)
                            a = m_top = dve.do(lambda e, t=t: e.match_replace(work[t][:], top[:], work[t][:], PICKED), a)
                            if t == 1 and n == 3:
                                yield
                        m[f"mask{t}"] = dve.do(lambda e, t=t: e.tensor_scalar(
                            work[t][:], work[t][:], (PICKED + UNPICKED) / 2, MASKED, ALU.is_gt, ALU.mult), a)
                        if t == 0:
                            i, ps, free = take_pair()
                            for j in range(4):
                                for u in range(T):
                                    done = turn(ps[:, j * S + u * P:j * S + (u + 1) * P], q_nrm[:, u, j * P:(j + 1) * P], free, m_n, signal=j == 3 and u == 1)
                            m["aq"] = act.do(lambda e, ps=ps: e.activation(qT[:].rearrange("p j s -> p (j s)"), ps[:, :], ACT.Copy, scale=col("q_norm")), done)
                            give_pair(i, m["aq"])
                            i, ps, free = take_pair()
                            for u in range(T):
                                done = turn(ps[:, u * P:(u + 1) * P], q_nrm[:, u, 512:640], free, signal=u == 1)
                            m["ak"] = act.do(lambda e, ps=ps: e.activation(kT[:], ps[:, 0:S], ACT.Copy, scale=col("k_norm")), done)
                            give_pair(i, m["ak"])
                            m_q_turned = done
                        else:
                            done = m_scored
                    yield
                    marks = {"q": m["aq"], "k": m["ak"], "v": m["kvn"], "mask0": m["mask0"], "mask1": [m["mask1"], a]}
                    ptv = q_nrm[:].rearrange("p t n -> p (t n)")
                    pe_free = [m_q_turned, done]
                    act.wait(pe_free)
                    dve.wait(pe_free)
                    yield from attention("a", scope, qT, lambda half, j: kT[64 * half:64 * half + 64, :],
                                         lambda st, half, j: kvn[:, st, 128 + 64 * half:192 + 64 * half],
                                         lambda t, g: [(0, 8 if t == 0 else 4, bcast(work[t][:], 1, 8 if t == 0 else 4))], marks,
                                         ya_hi[:].rearrange("p c s -> p (c s)"), ya_lo[:].rearrange("p c s -> p (c s)"),
                                         [q_raw[:].rearrange("p t n -> p (t n)").rearrange("p (h w) -> p h w", h=8), big[:].rearrange("p (h w) -> p h w", h=8)],
                                         [ptv[:, 0:384], ptv[:, 384:768], iqT[:, 0:2, :].rearrange("p j s -> p (j s)")[:, 0:384],
                                          iqT[:, 2:4, :].rearrange("p j s -> p (j s)")[:, 0:384]])
                    m["ya"] = marks["out"]

                def mlstm_chain():
                    order = (0, 2, 1, 3)
                    while "kvn" not in m:
                        yield
                    yield
                    i, ps, free = take_pair()
                    for t in range(T):
                        turn(ps[0:4, t * P:(t + 1) * P], kvn[:, t, 328:332], free, m["kvn"])
                        done = turn(ps[0:4, 512 + t * P:512 + (t + 1) * P], kvn[:, t, 332:336], signal=t == 1)
                    m_gi = dve.do(lambda e, ps=ps: e.tensor_scalar(gi, ps[0:4, 0:S], col("b_i", 0, 4), None, ALU.add), done, norm.marks[7, 1], xr_free)
                    a0 = dve.do(lambda e, ps=ps: e.tensor_scalar(gf, ps[0:4, 512:512 + S], col("b_f", 0, 4), None, ALU.add), done)
                    give_pair(i, m_gi, a0)
                    a = act.do(lambda e: e.activation(gt, gf, ACT.Abs), a0)
                    a = act.do(lambda e: e.activation(gt, gt, ACT.Exp, scale=-1.0), a)
                    a = act.do(lambda e: e.activation(gt, gt, ACT.Ln, bias=1.0), a)
                    yield
                    a = dve.do(lambda e: e.scalar_tensor_tensor(gt, gf, 0.0, gt, ALU.min, ALU.subtract), a)
                    b = dve.do(lambda e: e.memset(ones, 1.0))
                    m_F = dve.do(lambda e: e.tensor_tensor_scan(gf, ones, gt, 0.0, ALU.mult, ALU.add), a, b)
                    m_G = dve.do(lambda e: e.tensor_tensor(gi, gi, gf, ALU.subtract), m_F, m_gi)
                    yield
                    i, ps, free = take_pair()
                    for t in range(T):
                        m_turned = turn(ps[:, 4 * t:4 * t + 4], gf[:, t * P:(t + 1) * P], free, m_F, signal=t == 1)
                    m_ft = act.do(lambda e, ps=ps: e.copy(ft[:].rearrange("p t (half pair) -> p t half pair", half=2),
                                                          ps[:, 0:8].rearrange("p (t pair half) -> p t half pair", t=T, half=2)), m_turned, m_x)
                    give_pair(i, m_ft)
                    i, ps, free = take_pair()
                    for n, h in enumerate(order):
                        m_spread = mm(ps[:, n * S:(n + 1) * S], ident[0:4, h:h + 1].to_broadcast([4, P]), gi, n % 2 == 0, n % 2 == 1,
                                      free, m_G, signal=n == 3)
                    gps = ps[:, :].rearrange("p (h s) -> p h s", h=4)
                    m_d, m_e = [], []
                    for t in range(T):
                        w = P * (t + 1)
                        mask = causal[:, P:2 * P] if t == 0 else causal[:, :]
                        m_d.append(dve.do(lambda e, t=t, w=w, mask=mask, gps=gps: e.tensor_tensor(dm[t][:], gps[:, :, 0:w], bcast(mask, 1, 4), ALU.add), m_spread, m_par))
                    give_pair(i, m_d)
                    for t in range(T):
                        a = dve.do(lambda e, t=t: e.tensor_reduce(mt[:, t, :], dm[t][:], AX_X, ALU.max), m_d)
                        m_m = dve.do(lambda e, t=t: e.tensor_scalar(mt[:, t, :], mt[:, t, :], 0.0, None, ALU.max), a)
                        a = dve.do(lambda e, t=t: e.tensor_scalar(nmt[:, t, :], mt[:, t, :], -1.0, None, ALU.mult), m_m)
                        for h in range(4):
                            b = act.do(lambda e, t=t, h=h: e.activation(dm[t][:, h, :], dm[t][:, h, :], ACT.Exp, bias=nmt[:, t, h:h + 1]), a)
                        m_e.append(b)
                    a = dve.do(lambda e: e.tensor_tensor(ft[:], ft[:], mt[:], ALU.add), m_ft, m_m)
                    m_floor = act.do(lambda e: e.activation(ft[:], ft[:], ACT.Exp, scale=-1.0), a)
                    while "mx" not in m:
                        yield
                    yield
                    m_c = []
                    for c in range(4):
                        a = dve.do(lambda e, c=c: e.tensor_scalar(xc[:, c, :], xpad[:, c, 0:S], col("conv_w", c), col("conv_b", c), ALU.mult, ALU.add),
                                   m["mx"], m_zero)
                        for j in range(1, 4):
                            a = dve.do(lambda e, c=c, j=j: e.scalar_tensor_tensor(
                                xc[:, c, :], xpad[:, c, j:j + S], col("conv_w", 4 * j + c), xc[:, c, :], ALU.mult, ALU.add), a)
                        m_c.append(a)
                        if c % 2:
                            yield
                    a = act.do(lambda e: e.activation(sg, xc, ACT.Sigmoid), m_c, m_turned, m_spread)
                    m_xc = dve.do(lambda e: e.tensor_tensor(xc, xc, sg, ALU.mult), a)
                    yield
                    for w_m, dst, scale in ((w_mq, mq, 0.125), (w_mk, mk, 1.0)):
                        i, ps, free = take_pair()
                        for h in range(4):
                            half, pair = h % 2, h // 2
                            done = mm(ps[64 * half:64 * half + 64, pair * S:(pair + 1) * S], w_m[:, h, :], xc[:, h, :], pair == 0, pair == 1,
                                      free, m_xc, m_const, signal=h == 3)
                        m_qk = act.do(lambda e, dst=dst, ps=ps, scale=scale: e.activation(
                            dst[:].rearrange("p h s -> p (h s)"), ps[:, 0:512], ACT.Copy, scale=scale), done)
                        give_pair(i, m_qk)
                    yield
                    m_w = []
                    for t in range(T):
                        w = P * (t + 1)
                        i, ps, free = take_pair()
                        for n, h in enumerate(order):
                            half, pair = n // 2, n % 2
                            r = slice(64 * half, 64 * half + 64)
                            done = mm(ps[:, half * 512 + pair * w:half * 512 + (pair + 1) * w], mq[r, pair, t * P:(t + 1) * P], mk[r, pair, 0:w],
                                      pair == 0, pair == 1, free, m_qk, signal=n == 3)
                        for half in range(2):
                            src = ps[:, half * 512:half * 512 + 2 * w].rearrange("p (h s) -> p h s", h=2)
                            o = dm[t][:, 2 * half:2 * half + 2, :]
                            a = dve.do(lambda e, o=o, src=src: e.tensor_tensor(o, o, src, ALU.mult), done, m_e[t])
                        give_pair(i, a)
                        m_w.append(a)
                        m_den = dve.do(lambda e, t=t: e.tensor_reduce(den[:, t, :], dm[t][:], AX_X, ALU.add), a)
                    yield
                    a = act.do(lambda e: e.activation(den[:], den[:], ACT.Abs), m_den)
                    a = dve.do(lambda e: e.tensor_tensor(den[:], den[:], ft[:], ALU.max), a, m_floor)
                    m_den = dve.do(lambda e: e.reciprocal(den[:], den[:]), a)
                    while "mv" not in m:
                        yield
                    ih, ph, hfree = take_pair()
                    wt_free = [None, None]
                    for n, h in enumerate(order):
                        i, ps, free = take_pair()
                        turn(ps[:, 0:P], dm[0][:, n, :], free, m_w)
                        turn(ps[:, P:2 * P], dm[1][:, n, 0:P])
                        done = turn(ps[:, 2 * P:3 * P], dm[1][:, n, P:2 * P], signal=True)
                        b = n % 2
                        if b:
                            c = act.do(lambda e, b=b, ps=ps: e.copy(wt[b][:], ps[:, 0:384]), done, wt_free[b])
                        else:
                            c = dve.do(lambda e, b=b, ps=ps: e.tensor_copy(wt[b][:], ps[:, 0:384]), done, wt_free[b])
                        give_pair(i, c)
                        if n % 2:
                            yield
                        for nn in ((n - 1, n) if n % 2 else ()):
                            hh, bb = order[nn], nn % 2
                            cw = [prev_c, c][bb]
                            mm(ph[:, hh * P:(hh + 1) * P], wt[bb][:, 0:P], mv[:, 0, hh * P:(hh + 1) * P], nn == 0, nn == 3, cw, hfree, m["mv"])
                            mm(ph[:, 512 + hh * P:512 + (hh + 1) * P], wt[bb][:, P:2 * P], mv[:, 0, hh * P:(hh + 1) * P], nn == 0, False)
                            wt_free[bb] = mm(ph[:, 512 + hh * P:512 + (hh + 1) * P], wt[bb][:, 2 * P:3 * P], mv[:, 1, hh * P:(hh + 1) * P], False, nn == 3, signal=True)
                        prev_c = c
                    while "mo" not in m:
                        yield
                    m_mog = pool.do(lambda e: e.tensor_tensor(mo[:], mo[:], bcast(head_g[:], 1, T), ALU.mult), m["mo"], m_const)
                    hv, sv = (ap.rearrange("p c s -> p (c s)").rearrange("p (t q) -> p t q", t=T) for ap in (xc, sg))
                    h4 = lambda ap: ap.rearrange("p t (h q) -> p t h q", h=4)
                    a = []
                    for t in range(T):
                        dn = den[:, t, :].rearrange("p (half pair) -> p pair half", half=2)
                        o, src = xc.rearrange("p c s -> p (c s)")[:, t * 512:(t + 1) * 512], ph[:, t * 512:(t + 1) * 512]
                        a.append(dve.do(lambda e, o=o, src=src, dn=dn: e.tensor_tensor(
                            o.rearrange("p (pair half q) -> p pair half q", half=2, q=P), src.rearrange("p (pair half q) -> p pair half q", half=2, q=P),
                            bcast(dn, 3, P), ALU.mult), wt_free, m_den, m_qk))
                    give_pair(ih, a)
                    hm, s2 = xc.rearrange("p c s -> p (c s)"), sg.rearrange("p c s -> p (c s)")
                    g8 = lambda ap: ap.rearrange("p (g q) -> p g q", q=P)
                    a = dve.do(lambda e: e.tensor_tensor(s2, hm, hm, ALU.mult), a)
                    a = dve.do(lambda e: e.tensor_reduce(rh[:], g8(s2), AX_X, ALU.add), a)
                    m_rh = inverse_root(rh[:], rh[:], T * 4, P, a)
                    yield
                    a = dve.do(lambda e: e.tensor_tensor(g8(hm), g8(hm), bcast(rh[:], 2, P), ALU.mult), m_rh)
                    m_hm = dve.do(lambda e: e.tensor_tensor(hm, hm, flat(mo[:]), ALU.mult), a, m_mog)
                    yield
                    i, ps, free = take_pair()
                    for h in range(4):
                        for t in range(T):
                            done = turn(ps[:, h * S + t * P:h * S + (t + 1) * P], hm[:, t * 512 + h * P:t * 512 + (h + 1) * P], free, m_hm, signal=h == 3 and t == 1)
                    m["yb"] = split_whole(yb_hi[:].rearrange("p c s -> p (c s)"), yb_lo[:].rearrange("p c s -> p (c s)"), ps[:, :], done)
                    give_pair(i, m["yb"])
                    xr_free[0] = xr_free[1] = done

                B = lambda name, n0, nw, form, ev: Block(w_in, DC, n0, nw, h_hi, h_lo, norm.ready, form, ev)
                products([B("q", IN["q"], 512, "rows", evac("q", flat(q_raw[:])))], head=lambda: norm.turn(1))
                chain_a, chain_m = attention_chain(), mlstm_chain()
                side.extend([chain_a, chain_m])
                cols4 = lambda ap: ap.rearrange("p c s -> p (c s)")
                products([
                    B("kvn", IN["kv"], 336, "rows", evac("kvn", kvn[:], view=lambda ps: ps[:, :].rearrange("p (t n) -> p t n", t=T)[:, :, 0:336])),
                    B("iq", IN["iq"], 512, "cols", evac("iq", cols4(iqT[:]))),
                    B("mx", IN["mx"], 512, "cols", evac("mx", xpad[:, :, 3:3 + S], view=lambda ps: ps[:, :].rearrange("p (c s) -> p c s", c=4))),
                    B("mv", IN["mv"], 512, "rows", evac("mv", flat(mv[:]))),
                    B("mo", IN["mo"], 512, "rows", evac("mo", flat(mo[:]), ACT.Sigmoid))] +
                    [B(n_, IN[n_] + 512 * b, 512, "cols", evac((n_, b), cols4(g[:, 4 * b:4 * b + 4, :]), ACT.Sigmoid))
                     for n_, g in (("ga", ga), ("gb", gb)) for b in range(2)])
                drain(chain_a)

                def evac_gated(name, g):
                    def run(b, done, _):
                        h = b.n0 // 512
                        gv = cols4(g[:, 4 * h:4 * h + 4, :])
                        m[name, h] = dve.do(lambda e: e.tensor_tensor(gv, gv, b.ps[:, :], ALU.mult), done, m["g" + name, h])
                        give_pair(b.i, m[name, h])
                        if name == "b":
                            av = cols4(ga[:, 4 * h:4 * h + 4, :])
                            a = dve.do(lambda e: e.tensor_tensor(av, av, gv, ALU.add), m["a", h], m["b", h])
                            s_ = split_whole(cols4(h_hi[:, 4 * h:4 * h + 4, :]), cols4(h_lo[:, 4 * h:4 * h + 4, :]), av, a, m["gb", 1])
                            for c in range(4):
                                m_merged[4 * h + c] = s_
                    return run
                m_merged = {}
                products([Block(d["w_proj_a"], 4, 512 * b, 512, ya_hi, ya_lo, [m["ya"]] * 4, "cols", evac_gated("a", ga)) for b in range(2)])
                drain()
                products([Block(d["w_proj_b"], 4, 512 * b, 512, yb_hi, yb_lo, [m["yb"]] * 4, "cols", evac_gated("b", gb)) for b in range(2)])
                nxt = make_next()
                products(add_blocks(d["w_out"], DC, h_hi, h_lo, m_merged, 1.0, nxt), tail=nxt)
                return nxt

        def memory_blocks(hi, lo, ready, xk, xv):
            m_kv = {}

            def evac(n):
                def run(b, done, _):
                    if n < 2:
                        o, src = xk[:, 4 * n:4 * n + 4, :].rearrange("p c s -> p (c s)"), b.ps[:, :]
                    else:
                        o, src = xv[:, :, 512 * (n - 2):512 * (n - 1)], b.ps[:, :].rearrange("p (t n) -> p t n", t=T)
                    m_kv[n] = act.do(lambda e: e.copy(o, src), done)
                    give_pair(b.i, m_kv[n])
                return run
            return [Block(d["xa_wkv_2"], DC, 512 * n, 512, hi, lo, ready, "cols" if n < 2 else "rows", evac(n)) for n in range(4)], m_kv

        def mixer2(norm, y, kv, make_next):
            m_x = norm.m_xr[1]
            scope = ExitStack()
            with scope:
                alibi = sb(scope, "alibi", [P, 2, 2, 2, S])
                qT, kT = sb(scope, "qT2", [P, 4, S]), sb(scope, "kT2", [P, 4, S])
                v = sb(scope, "v2", [P, T, 512])
                sc = [sb(scope, f"sc2_{t}", [P, 8, P * (t + 1)]) for t in range(T)]
                pt = [sb(scope, f"pt2_{i}", [P, 384]) for i in range(4)]
                L = 16 + S
                win = [sb(scope, "win0", [P, 4, L]), y[:].rearrange("p t n -> p (t n)")[:, 0:4 * L].rearrange("p (g s) -> p g s", g=4)]
                pin, inv = (xr[:, n_, :].rearrange("p (g s) -> p g s", g=4) for n_ in range(2))
                pw = sb(scope, "pw", [P, 4, P])
                m_alibi = pool.dma(alibi[:].rearrange("p a b c s -> p (a b c s)"), d["consts"][:, 640:2688], s_small["alibi"], used, m_x)
                m_zero = pool.do(lambda e: e.memset(win[0][:, :, 0:16], 0.0))
                m = {}

                def evac(name, out_ap):
                    def run(b, done, _):
                        m[name] = act.do(lambda e: e.copy(out_ap, b.ps[:, :]), done, m_x)
                        give_pair(b.i, m[name])
                    return run

                def evac_pool(b, done, _):
                    src = b.ps[:, :].rearrange("p (g s) -> p g s", g=4)
                    m1 = act.do(lambda e: e.copy(win[0][:, :, 16:L], src), done)
                    m["pin"] = [m1, act.do(lambda e: e.copy(pin, src), xr_free)]
                    give_pair(b.i, m["pin"])

                def pool_chain():
                    while "pin" not in m:
                        yield
                    m_inv = pool.dma(inv.rearrange("p g s -> p (g s)"), d["consts"][:, 2688:3712], s_small["mix2"], used, xr_free)
                    m_inv = pool.dma(pw[:], d["pool_w_2"].rearrange("g c n -> c g n"), s_small["mix2"], used)
                    last = [m["pin"], m_zero]
                    m_sums = []
                    for g in range(4):
                        src, dst = win[g % 2], win[(g + 1) % 2]
                        sh, first = 2 ** g, (1, 4, 8, 16)[g]
                        last = [pool.do(lambda e, src=src, dst=dst, sh=sh, first=first, g=g: e.tensor_tensor(
                            dst[:, g:4, first:L], src[:, g:4, first:L], src[:, g:4, first - sh:L - sh], ALU.add), *last)]
                        m_sums.append(last)
                    yield
                    for g in range(4):
                        dst = win[(g + 1) % 2]
                        a = pool.do(lambda e, dst=dst, g=g: e.tensor_tensor(inv[:, g, :], dst[:, g, 16:L], inv[:, g, :], ALU.mult), m_sums[g], m_inv)
                        m_dev = pool.do(lambda e, g=g: e.tensor_tensor(pin[:, g, :], inv[:, g, :], pin[:, g, :], ALU.subtract), a, m["pin"])
                    yield
                    while "passed" not in m:
                        yield
                    i, ps, free = take_pair()
                    for g in range(4):
                        done = mm(ps[:, g * S:(g + 1) * S], pw[:, g, :], pin[:, g, :], g % 2 == 0, g % 2 == 1, free, m_dev, m_inv, signal=g == 3)
                    xr_free[0] = xr_free[1] = done
                    ms = split_gained(h_hi[:, 4:8, :], h_lo[:, 4:8, :], ps, [col("pool_scale_2", g) for g in range(4)], [done, done])
                    for g in range(4):
                        m_cat[4 + g] = ms[g]
                    give_pair(i, *ms)

                def attention_chain():
                    while "k" not in m:
                        yield
                    marks = {"q": m["q"], "k": m["k"], "v": m["v"], "mask0": m_alibi, "mask1": m_alibi}

                    def mask_ops(t, g):
                        if t == 1:
                            return [(0, 4, alibi[:, g].rearrange("p b c s -> p (b c) s"))]
                        return [(half * 4 + gg * 2, half * 4 + gg * 2 + 2, alibi[:, gg, half, :, P:2 * P]) for half in range(2) for gg in range(2)]
                    yield from attention("m", scope, qT, lambda half, j: kT[64 * half:64 * half + 64, j, :],
                                         lambda st, half, j: v[:, st, (2 * j + half) * 64:(2 * j + half) * 64 + 64], mask_ops, marks,
                                         h_hi[:, 0:4, :].rearrange("p c s -> p (c s)"), h_lo[:, 0:4, :].rearrange("p c s -> p (c s)"), sc, [p_[:] for p_ in pt])
                    for c in range(4):
                        m_cat[c] = marks["out"]

                m_cat = {}
                blocks, m_kv = kv
                cols4 = lambda ap: ap.rearrange("p c s -> p (c s)")
                products(blocks[0:1])
                side.extend([attention_chain(), pool_chain()])
                B = lambda b, form, ev: Block(w_in2, DC, 512 * b, 512, h_hi, h_lo, norm.ready, form, ev)
                products([B(2, "rows", evac("v", cols4(v[:])))], head=lambda: norm.turn(1))
                products([B(0, "cols", evac("q", cols4(qT[:]))), B(1, "cols", evac("k", cols4(kT[:]))), B(3, "cols", evac_pool)])
                m["passed"] = True
                products(blocks[1:2])
                while 4 not in m_cat:
                    tick()
                nxt = make_next()
                out_blocks = post_blocks(d["w_out_2"], DC, h_hi, h_lo, m_cat, y, "mix_post_g_2", s_small["post1"], 1.0, nxt, m_cat[7])
                steps = by_chunks(out_blocks, (4, 0))
                products(out_blocks, steps=steps[0:1])
                products(out_blocks, steps=steps[1:], tail=nxt)
                return nxt

        def cross(norm, y, xk, xv, kv, make_next):
            scope = ExitStack()
            with scope:
                xq = sb(scope, "xq", [P, DC, S])
                pr = sb(scope, "pr", [P, T, 4, S])
                nmax = sb(scope, "nmax_x", [P, T, 4])
                tot = sb(scope, "tot_x", [P, T, 4])
                pt = [sb(scope, f"ptx{i}", [P, 512]) for i in range(4)]
                blocks, m_kv = kv
                m_q = []

                def evac_q(b, done, _):
                    c = b.n0 // P
                    m_q.append(act.do(lambda e: e.copy(xq[:, c:c + 4, :].rearrange("p c s -> p (c s)"), b.ps[:, :]), done))
                    give_pair(b.i, m_q[-1])

                def attention_chain():
                    m_p, turned, pt_free = {}, {}, [None] * 4

                    def scores(hp):
                        i, ps, free = take_pair()
                        m_e = []
                        for t in range(T):
                            for n in range(2):
                                for c in range(2):
                                    ch = 2 * (2 * hp + n) + c
                                    done = mm(ps[:, t * 512 + n * S:t * 512 + (n + 1) * S], xq[:, ch, t * P:(t + 1) * P], xk[:, ch, :],
                                              n == 0 and c == 0, n == 1 and c == 1, free, m_q[hp], m_kv[hp], signal=n == 1 and c == 1)
                            pv_ = ps[:, t * 512:(t + 1) * 512].rearrange("p (h s) -> p h s", h=2)
                            nm, tt = nmax[:, t, 2 * hp:2 * hp + 2], tot[:, t, 2 * hp:2 * hp + 2]
                            a = dve.do(lambda e, nm=nm, pv_=pv_: e.tensor_reduce(nm, pv_, AX_X, ALU.max, negate=True), done)
                            a = dve.do(lambda e, nm=nm: e.tensor_scalar(nm, nm, 1.0 / 16, None, ALU.mult), a)
                            for n in range(2):
                                h = 2 * hp + n
                                b = act.do(lambda e, t=t, h=h, n=n, pv_=pv_: e.activation(pr[:, t, h, :], pv_[:, n, :], ACT.Exp, bias=nmax[:, t, h:h + 1],
                                           scale=1.0 / 16, accum_out=tot[:, t, h:h + 1]), a)
                            m_e.append(b)
                            b = dve.do(lambda e, tt=tt: e.reciprocal(tt, tt), b)
                            m_p[hp, t] = dve.do(lambda e, t=t, tt=tt: e.tensor_tensor(
                                pr[:, t, 2 * hp:2 * hp + 2], pr[:, t, 2 * hp:2 * hp + 2], bcast(tt, 2, S), ALU.mult), b)
                        give_pair(i, m_e)

                    def turn_heads(hp):
                        i, ps, free = take_pair()
                        for n in range(2):
                            h = 2 * hp + n
                            for mt in range(2):
                                for t in range(T):
                                    o = n * 512 + mt * S + t * P
                                    done = turn(ps[:, o:o + P], pr[:, t, h, mt * P:(mt + 1) * P], free, m_p[hp, t], signal=mt == 1 and t == 1)
                            src = ps[:, n * 512:(n + 1) * 512]
                            turned[h] = act.do(lambda e, h=h, src=src: e.copy(pt[h][:], src), done)
                        give_pair(i, turned[2 * hp], turned[2 * hp + 1])

                    def weigh(hp):
                        io, po, ofree = take_pair()
                        for n in range(2):
                            h = 2 * hp + n
                            for dd in range(2):
                                o = po[:, (2 * n + dd) * S:(2 * n + dd + 1) * S]
                                for mt in range(2):
                                    done = mm(o, xv[:, mt, (2 * h + dd) * P:(2 * h + dd + 1) * P], pt[h][:, mt * S:(mt + 1) * S],
                                              dd == 0 and mt == 0, dd == 1 and mt == 1, turned[h], ofree, m_kv[2 + hp], signal=dd == 1 and mt == 1)
                        c4 = slice(4 * hp, 4 * hp + 4)
                        s_ = split_whole(h_hi[:, c4, :].rearrange("p c s -> p (c s)"), h_lo[:, c4, :].rearrange("p c s -> p (c s)"), po[:, :], done)
                        give_pair(io, s_)
                        for c in range(4):
                            m_o[4 * hp + c] = s_

                    while len(m_q) < 1:
                        yield
                    scores(0)
                    yield
                    while len(m_q) < 2:
                        yield
                    scores(1)
                    yield
                    turn_heads(0)
                    yield
                    weigh(0)
                    turn_heads(1)
                    yield
                    weigh(1)

                m_o = {}
                products(blocks[2:3], then=lambda: norm.turn(1))
                side.append(attention_chain())
                products([Block(d["xa_wq_2"], DC, 512 * b, 512, h_hi, h_lo, norm.ready, "cols", evac_q) for b in range(2)])
                products(blocks[3:4])
                while 0 not in m_o:
                    tick()
                nxt = make_next()
                out_blocks = post_blocks(d["xa_wo_2"], DC, h_hi, h_lo, m_o, y, "xa_post_g_2", s_small["post2"], 1.0, nxt, m_q)
                steps = by_chunks(out_blocks, (0, 4))
                products(out_blocks, steps=steps[0:1])
                products(out_blocks, steps=steps[1:], tail=nxt)
                return nxt

        def next_norm(gain):
            return lambda: Norm(x, gain, h_hi, h_lo)

        n = Norm(x, "ffn1_norm", h_hi, h_lo, m_first_gain)
        for t in range(T):
            for half in range(2):
                n.part(t, half, m_x[t])
            n.stats(t)
            if t == 0:
                n.turn(0)
                queue_splits(1)
        n = ffn(0, d["ffn1_w_gate"], d["ffn1_w_up"], d["ffn1_w_down"], n, next_norm("mix_norm"))
        debug(0, n)
        n = mixer1(n, next_norm("ffn2_norm"))
        debug(1, n)
        n = ffn(1, d["ffn2_w_gate"], d["ffn2_w_up"], d["ffn2_w_down"], n, next_norm("ffn1_pre_g_2"))
        debug(2, n)
        second = ExitStack()
        with second:
            y = sb(second, "y", [P, T, D])
            xk, xv = sb(second, "xk", [P, DC, S]), sb(second, "xv", [P, T, D])
            gain_buf.append(sb(second, "gain", [P, D]))
            memory = ExitStack()
            with memory:
                mem_hi, mem_lo = sb(memory, "mem_hi", [P, DC, S], F32R), sb(memory, "mem_lo", [P, DC, S], F32R)
                for t in range(T):
                    m_mem = pool.dma(y[:, t, :], d["mem_2"][t * P:(t + 1) * P, :], s_small["mem"], used, n.m_xr[0])
                got = {}

                def norm_memory():
                    for _ in range(6):
                        yield
                    mem = got["mem"] = Norm(y, "mem_g_2", mem_hi, mem_lo)
                    for t in range(T):
                        for half in range(2):
                            mem.part(t, half, m_mem)
                    yield
                    for t in range(T):
                        mem.stats(t)
                        yield
                    for t in range(T):
                        mem.turn(t)
                        yield
                side.append(norm_memory())
                n = ffn(2, d["ffn1_w_gate_2"], d["ffn1_w_up_2"], d["ffn1_w_down_2"], n, next_norm("mix_pre_g_2"),
                        (y, "ffn1_post_g_2", s_small["post0"]))
                debug(3, n)
                kv = memory_blocks(mem_hi, mem_lo, got["mem"].ready, xk, xv)
                n = mixer2(n, y, kv, next_norm("xa_pre_g_2"))
                debug(4, n)
                n = cross(n, y, xk, xv, kv, next_norm("ffn2_pre_g_2"))
            debug(5, n)
            ffn(3, d["ffn2_w_gate_2"], d["ffn2_w_up_2"], d["ffn2_w_down_2"], n, Finish, (y, "ffn2_post_g_2", s_small["post3"]))
        sp.wait((s_out, used[id(s_out)]))
        assert state["next"] == len(plan)

        blk = ctx.enter_context(nc.Block())
        blk.tensor(pe.run)
        blk.scalar(act.run)
        blk.vector(dve.run)
        blk.gpsimd(pool.run)
        blk.sync(sp.run)


_MATS = ["ffn1_w_gate", "ffn1_w_up", "ffn1_w_down", "w_in", "w_mq", "w_mk", "w_proj_a", "w_proj_b", "w_out",
         "ffn2_w_gate", "ffn2_w_up", "ffn2_w_down", "ffn1_w_gate_2", "ffn1_w_up_2", "ffn1_w_down_2", "w_in_2",
         "pool_w_2", "w_out_2", "xa_wq_2", "xa_wkv_2", "xa_wo_2", "ffn2_w_gate_2", "ffn2_w_up_2", "ffn2_w_down_2",
         "x", "mem_2"]
_ROWS = ["ffn1_norm", "mix_norm", "ffn2_norm", "ffn1_pre_g_2", "mix_pre_g_2", "mem_g_2", "xa_pre_g_2", "ffn2_pre_g_2",
         "m_head_norm", "ffn1_post_g_2", "mix_post_g_2", "xa_post_g_2", "ffn2_post_g_2"]


def kernel(**inputs):
    import concourse.bacc as bacc
    from concourse.bass_utils import run_bass_kernel_spmd

    nc = bacc.Bacc("TRN2", target_bir_lowering=False, num_devices=1)
    arrays, d = {}, {}

    def declare(name, a):
        a = np.ascontiguousarray(a)
        arrays["in_" + name] = a
        d[name] = nc.dram_tensor("in_" + name, a.shape, mybir.dt.from_np(a.dtype), kind="ExternalInput").ap()

    for name in _MATS:
        declare(name, np.asarray(inputs[name])[0])
    for name in _ROWS:
        declare(name, np.asarray(inputs[name])[0])
    par = np.zeros((P, N_PARAMS), np.float32)
    for name, (a, b) in PARAM_COLS.items():
        v = np.asarray(inputs[name])[0]
        if name in ("q_norm", "k_norm", "idx_k_norm"):
            par[0:64, a], par[64:128, a] = v, v
        elif name in ("b_i", "b_f"):
            par[0:4, a] = v
        else:
            par[:, a:b] = v.reshape(b - a, P).T
    declare("params", par)
    declare("consts", shape_constants())
    out = nc.dram_tensor("out", (S, D), F32, kind="ExternalOutput").ap()
    dbg = nc.dram_tensor("dbg", (6, S, D), F32, kind="ExternalOutput").ap() if DEBUG else None
    build(nc, d, out, dbg)
    r = run_bass_kernel_spmd(nc, [arrays], core_ids=[0])
    got = r.results[0]["out"].reshape(1, S, D)
    if DEBUG:
        return (got, r.results[0]["dbg"])
    return got
```

```python
from contextlib import ExitStack

import concourse.bass as bass
import concourse.mybir as mybir
import numpy as np

F32 = mybir.dt.float32
F32R = mybir.dt.float32r
ACT = mybir.ActivationFunctionType
ALU = mybir.AluOpType
AX_X = mybir.AxisListType.X

P = 128
S = 256
T = S // P
D = 1024
DC = D // P
EPS = 1e-6
MASKED = -1e30
UNPICKED = -3e38
PICKED = -3.4e38
TOPK = S // 4
UNIT = 1024
STAGES = 6
SPLITS = 6


class Engine:

    def __init__(self, sem):
        self.sem, self.count, self.items, self.known = sem, 0, [], {}

    def wait(self, *marks):
        for m in marks:
            if m is None:
                continue
            if isinstance(m, list):
                self.wait(*m)
                continue
            sem, value = m
            if self.known.get(id(sem), 0) < value:
                self.known[id(sem)] = value
                self.items.append(lambda e, sem=sem, value=value: e.wait_ge(sem, value))

    def do(self, emit, *waits, signal=True):
        self.wait(*waits)
        if not signal:
            self.items.append(emit)
            return None
        self.count += 1
        self.items.append(lambda e: emit(e).then_inc(self.sem, 1))
        return (self.sem, self.count)

    def dma(self, out, in_, sem, used, *waits):
        self.wait(*waits)
        used[id(sem)] = used.get(id(sem), 0) + 16
        self.items.append(lambda e: e.dma_start(out, in_).then_inc(sem, 16))
        return (sem, used[id(sem)])

    def run(self, e):
        for item in self.items:
            item(e)


def bcast(ap, axis, n):
    a = ap.unsqueeze(axis)
    shape = list(a.shape)
    shape[axis] = n
    return a.to_broadcast(shape)


PARAM_COLS = {}


def param_columns():
    at = 0
    for name, n in (("q_norm", 1), ("k_norm", 1),
                    ("idx_k_norm", 1), ("conv_w", 16), ("conv_b", 4), ("pool_scale_2", 4), ("b_i", 1), ("b_f", 1)):
        PARAM_COLS[name] = (at, at + n)
        at += n
    return at


N_PARAMS = param_columns()
CONST_COLS = {"ident": (0, 128), "causal": (128, 384), "chunked": (384, 640), "alibi": (640, 2688),
              "inv_count": (2688, 3712)}
N_CONSTS = 3712


def shape_constants():
    c = np.zeros((P, N_CONSTS), np.float32)
    r = np.arange(P)[:, None]
    col = np.arange(P)[None, :]
    c[:, 0:128] = np.eye(P)
    causal = np.concatenate([np.zeros((P, P)), np.where(col <= r, 0.0, MASKED)], 1)
    c[:, 128:384] = causal
    c[:, 512:640] = np.where(col < (r // 64 + 1) * 64, 0.0, UNPICKED)
    dist = np.arange(S)[None, :] - (r + P)
    for group in range(2):
        for half in range(2):
            for jj in range(2):
                head = 2 * (2 * group + jj) + half
                at = 640 + ((group * 2 + half) * 2 + jj) * S
                slope = np.float32(2.0 ** (-8.0 * (head + 1) / 8))
                c[:, at:at + S] = np.where(dist <= 0, slope * dist, MASKED)
    for g, w in enumerate((2, 4, 8, 16)):
        c[:, 2688 + g * S:2688 + (g + 1) * S] = 1.0 / np.minimum(np.arange(S) + 1, w)
    return c


def build(nc, d, out):
    ctx = ExitStack()
    with ctx:
        def sb(scope, name, shape, dt=F32):
            return scope.enter_context(nc.sbuf_tensor(name, shape, dt))

        def sem(name):
            return ctx.enter_context(nc.semaphore(name))

        pe, act, dve, pool, sp = (Engine(sem("s_" + n)) for n in ("pe", "act", "dve", "pool", "sp"))
        used = {}
        s_stage = [sem(f"s_stage{i}") for i in range(STAGES)]
        s_x, s_par, s_out = [sem("s_x0"), sem("s_x1")], sem("s_par"), sem("s_out")
        s_small = {n: sem("s_" + n) for n in ("mix1", "alibi", "pooling", "mem", "post0", "post1", "post2", "post3")}
        s_gain, s_ident = sem("s_gain"), sem("s_ident")

        x = sb(ctx, "x", [P, T, D])
        xr = sb(ctx, "xr", [P, T, D])
        h_hi = sb(ctx, "h_hi", [P, DC, S], F32R)
        h_lo = sb(ctx, "h_lo", [P, DC, S], F32R)
        stage = [sb(ctx, f"stage{i}", [P, UNIT]) for i in range(STAGES)]
        w_hi = [sb(ctx, f"w_hi{i}", [P, UNIT], F32R) for i in range(SPLITS)]
        w_lo = [sb(ctx, f"w_lo{i}", [P, UNIT], F32R) for i in range(SPLITS)]
        par = sb(ctx, "par", [P, N_PARAMS])
        ident = sb(ctx, "ident", [P, P])
        causal = sb(ctx, "causal", [P, 2 * P])
        stat = sb(ctx, "stat", [P, T, 4])
        post_stat = sb(ctx, "post_stat", [P, T, 4])
        pre_gain = sb(ctx, "pre_gain", [P, D])
        half_pow = sb(ctx, "half_pow", [P, 32])
        pairs = [ctx.enter_context(nc.psum_tensor(f"pair{i}", [P, 1024], F32)) for i in range(4)]
        pair_free = [(i, []) for i in range(4)]

        def take_pair():
            i, waits = pair_free.pop(0)
            return i, pairs[i], waits

        def give_pair(i, *marks):
            pair_free.append((i, list(marks)))

        def col(name, c=0, rows=P):
            a = PARAM_COLS[name][0] + c
            return par[0:rows, a:a + 1]

        def const(name):
            return d["consts"][:, slice(*CONST_COLS[name])]

        m_x = [sp.dma(x[:, 0, :], d["x"][0:P, :], s_x[0], used)]
        m_ident = sp.dma(ident[:], const("ident"), s_ident, used)
        m_pow = pool.do(lambda e: e.memset(half_pow[:], -0.5))
        m_first_gain = pool.dma(pre_gain[:], d["ffn1_norm"].partition_broadcast(P), s_gain, used)
        pool.dma(par[:], d["params"], s_par, used)
        m_par = pool.dma(causal[:], const("causal"), s_par, used)

        plan = []

        def unit_chunks(K, nw):
            return min(K, UNIT // nw)

        def halves(first):
            return [(b, k) for h in (first, 1 - first) for b in range(2) for k in range(4 * h, 4 * h + 4, unit_chunks(DC, 512))]

        def plan_block(w, K, n0, nw, rows=None, share=False, ks=None):
            kc = unit_chunks(K, nw)
            for k0 in range(0, K, kc) if ks is None else [ks]:
                k1 = min(K, k0 + kc)
                if rows:
                    srcs = rows(k0, k1, n0, nw)
                else:
                    v = w.rearrange("(k p) n -> p k n", p=P)
                    srcs = [(slice(0, P), slice(0, nw), v[:, k0:k1, n0:n0 + nw])]
                plan.append((w, k0, k1, n0, nw, srcs, share and k0 % 4 == 0))

        state = {"next": 0, "hi": 0, "lo": 0, "loaded": 0}
        m_load, m_hi, m_lo, m_used = {}, {}, {}, {}

        def load_unit(u):
            _, k0, k1, _, nw, srcs, _ = plan[u]
            dst = stage[u % STAGES][:, 0:(k1 - k0) * nw].rearrange("p (k n) -> p k n", n=nw)
            held = [m_hi[u - STAGES], m_lo[u - STAGES]] if u >= STAGES else []
            for parts, cols, src in srcs:
                m_load[u] = sp.dma(dst[parts, :, cols], src, s_stage[u % STAGES], used, *held)

        def split_parts(u):
            _, k0, k1, _, nw, _, _ = plan[u]
            n = (k1 - k0) * nw
            held = m_used[u - SPLITS] if u >= SPLITS else None
            return stage[u % STAGES][:, 0:n], w_hi[u % SPLITS][:, 0:n], w_lo[u % SPLITS][:, 0:n], held

        def make_lo(u, engine):
            src, hi, lo, held = split_parts(u)
            m_lo[u] = engine.do(lambda e: e.tensor_tensor(lo, src, hi.bitcast(F32), ALU.subtract), m_hi[u], held)

        def queue_hi(most=SPLITS):
            end = min(state["hi"] + most, len(plan))
            while state["hi"] < end and (state["hi"] < SPLITS or state["hi"] - SPLITS in m_used):
                u = state["hi"]
                src, hi, _, held = split_parts(u)
                m_hi[u] = act.do(lambda e, hi=hi, src=src: e.copy(hi, src), m_load[u], held)
                if plan[u][6]:
                    make_lo(u, pool)
                state["hi"] += 1

        def queue_lo(most=SPLITS):
            while state["lo"] < state["hi"] and (most or plan[state["lo"]][6]):
                if not plan[state["lo"]][6]:
                    make_lo(state["lo"], dve)
                    most -= 1
                state["lo"] += 1
                if state["loaded"] < len(plan):
                    load_unit(state["loaded"])
                    state["loaded"] += 1

        def queue_splits(most=SPLITS):
            queue_hi(most)
            queue_lo()

        def take_unit(w, k0, n0):
            u = state["next"]
            assert plan[u][0] is w and plan[u][1] == k0 and plan[u][3] == n0, (u, k0, n0)
            assert u < state["lo"]
            state["next"] += 1
            return u

        class Block:

            def __init__(self, w, K, n0, nw, hi, lo, ready, form, evac):
                self.w, self.K, self.n0, self.nw, self.hi, self.lo, self.form, self.evac = w, K, n0, nw, hi, lo, form, evac
                self.ready = ready if callable(ready) else (lambda k, t: ready[k])
                self.begun, self.ps, self.left = set(), None, [K] * T
                self.kc = unit_chunks(K, nw)
                self.units = [(k0, min(K, k0 + self.kc)) for k0 in range(0, K, self.kc)]

            def complete(self, t):
                return self.left[t] == 0

            def take(self, k0):
                if self.ps is None:
                    self.i, self.ps, free = take_pair()
                    pe.wait(free)
                return take_unit(self.w, k0, self.n0)

            def multiply(self, u, k0, k1, ts):
                nw, form = self.nw, self.form
                w_h = w_hi[u % SPLITS][:, 0:(k1 - k0) * nw].rearrange("p (k n) -> p k n", n=nw)
                w_l = w_lo[u % SPLITS][:, 0:(k1 - k0) * nw].rearrange("p (k n) -> p k n", n=nw)
                pe.wait(m_hi[u], m_lo[u])
                c0, c1 = ts[0] * P, (ts[-1] + 1) * P
                groups = list(ts) if form == "rows" else list(range(nw // P))
                for t in ts:
                    self.left[t] -= k1 - k0
                for k in range(k0, k1):
                    for t in ts:
                        pe.wait(self.ready(k, t))
                    for g in groups:
                        if form == "rows":
                            o, bank = self.ps[:, g * 512:g * 512 + nw], g
                            a_h, a_l = self.hi[:, k, g * P:(g + 1) * P], self.lo[:, k, g * P:(g + 1) * P]
                            ops = [(a_h, w_h[:, k - k0, :]), (a_l, w_h[:, k - k0, :]), (a_h, w_l[:, k - k0, :])]
                        else:
                            o, bank = self.ps[:, g * S + c0:g * S + c1], g // 2
                            b_h, b_l = w_h[:, k - k0, g * P:(g + 1) * P], w_l[:, k - k0, g * P:(g + 1) * P]
                            ops = [(b_h, self.hi[:, k, c0:c1]), (b_h, self.lo[:, k, c0:c1]), (b_l, self.hi[:, k, c0:c1])]
                        for j, (l, r) in enumerate(ops):
                            first = bank not in self.begun
                            self.begun.add(bank)
                            done = pe.do(lambda e, o=o, l=l, r=r, first=first, stop=(self.left[ts[-1]] == 0 and k == k1 - 1 and j == 2):
                                         e.matmul(o, l, r, start=first, stop=stop, skip_group_check=True),
                                         signal=k == k1 - 1 and g == groups[-1] and j == 2)
                return done

        side = []

        def side_work(gen, wait=2):
            side.append([gen, wait])

        def tick(every=False):
            for entry in list(side):
                entry[1] -= 1
                if entry[1] <= 0 or every:
                    try:
                        entry[1] = next(entry[0]) or 2
                    except StopIteration:
                        side.remove(entry)

        def drain(*gens):
            while any(not gens or g in gens for g, _ in side):
                tick(every=True)

        def after_unit(lo=True):
            queue_hi()
            tick()
            if lo:
                queue_lo()

        def drain(*gens):
            while any(g in side for g in gens) if gens else side:
                tick(every=True)

        def in_halves(blocks, first):
            return [(blocks[b], k0, k1) for b, k in halves(first) for k0, k1 in blocks[b].units if k0 == k]

        def products(blocks, head=None, tail=None, then=None, steps=None, late=0):
            steps = steps or [(b, k0, k1) for b in blocks for k0, k1 in b.units]
            n_head = min(SPLITS, len(steps)) if head else 0
            n_tail = min(SPLITS, len(steps)) if tail else 0
            assert n_head + n_tail <= len(steps)
            queue_splits()
            taken = []
            for n, (b, k0, k1) in enumerate(steps[:n_head]):
                taken.append(b.take(k0))
                b.multiply(taken[n], k0, k1, [0])
                if n == min(4, n_head - 1):
                    head()
            for n, (b, k0, k1) in enumerate(steps[:n_head]):
                m_used[taken[n]] = done = b.multiply(taken[n], k0, k1, [1])
                if b.complete(1):
                    b.evac(b, done, None)
                after_unit()
            for b, k0, k1 in steps[n_head:len(steps) - n_tail]:
                u = b.take(k0)
                m_used[u] = done = b.multiply(u, k0, k1, [0, 1])
                if then and (b, k0) == steps[-1][:2]:
                    then()
                if b.complete(0):
                    b.evac(b, done, None)
                after_unit(lo=not then or (b, k0) == steps[-1][:2])
            if not tail:
                return
            drain()
            last = steps[len(steps) - n_tail:]
            taken = []
            for n, (b, k0, k1) in enumerate(last):
                taken.append(b.take(k0))
                done = b.multiply(taken[n], k0, k1, [0])
                if b.complete(0):
                    b.evac(b, done, 0)
            tail.stats(0)
            for n, (b, k0, k1) in enumerate(last):
                if n == n_tail - 2 + late:
                    tail.turn(0)
                m_used[taken[n]] = done = b.multiply(taken[n], k0, k1, [1])
                if n < 2 or n >= n_tail - 2:
                    queue_hi(1)
                if n == 0 or n >= n_tail - 2:
                    queue_lo(1)
                if b.complete(1):
                    b.evac(b, done, 1)
            tail.stats(1)
            queue_splits()

        def mm(o, l, r, start, stop, *waits, signal=False):
            return pe.do(lambda e: e.matmul(o, l, r, start=start, stop=stop, skip_group_check=True), *waits, signal=signal)

        def turn(o, i_, *waits, signal=False):
            n = i_.shape[0]
            return pe.do(lambda e: e.transpose(o, i_, ident[0:n, 0:n]), *waits, signal=signal)

        def inverse_root(r, ss, n, width, *waits):
            a = pool.do(lambda e: e.tensor_scalar(r, ss, 1.0 / width, EPS, ALU.mult, ALU.add), *waits)
            return pool.do(lambda e: e.tensor_tensor(r, r, half_pow[:, 0:n], ALU.pow), a, m_pow)

        def split_whole(hi, lo, src, *waits):
            a = act.do(lambda e: e.copy(hi, src), *waits)
            b = dve.do(lambda e: e.tensor_tensor(lo, src, hi.bitcast(F32), ALU.subtract), a, *waits)
            return [a, b]

        def split_gained(hi, lo, ps, gains, done, *waits):
            marks = []
            for bank in range(2):
                cs = (2 * bank, 2 * bank + 1)
                for c in cs:
                    a = act.do(lambda e, c=c: e.activation(hi[:, c, :], ps[:, c * S:(c + 1) * S], ACT.Copy, scale=gains[c]), done[bank], *waits)
                for c in cs:
                    b = dve.do(lambda e, c=c: e.scalar_tensor_tensor(
                        lo[:, c, :], ps[:, c * S:(c + 1) * S], gains[c], hi[:, c, :].bitcast(F32), ALU.mult, ALU.subtract), a, *waits)
                    marks.append([a, b])
            return marks

        gain_buf = []
        xr_free = [[], []]
        gain_free = [[]]

        class Norm:

            def __init__(self, src, gain, hi, lo, m_gain=None):
                self.src, self.hi, self.lo = src, hi, lo
                self.m_src = [[None, None], [None, None]]
                self.m_part = [[None, None], [None, None]]
                self.m_xr, self.marks = [None] * T, {}
                self.m_gain = m_gain or pool.dma(pre_gain[:], d[gain].partition_broadcast(P), s_gain, used, gain_free[0])

            def part(self, t, half, *marks):
                cols = slice(512 * half, 512 * half + 512)
                self.m_src[t][half] = list(marks)
                self.m_part[t][half] = act.do(lambda e: e.activation(
                    xr[:, t, cols], self.src[:, t, cols], ACT.Square, accum_out=stat[:, t, half:half + 1]), list(marks), xr_free[t])

            def stats(self, t):
                ss0, ss1, ms, r = (stat[:, t, n:n + 1] for n in range(4))
                a = dve.do(lambda e: e.tensor_scalar(ms, ss0, 1.0 / D, EPS, ALU.mult, ALU.add), self.m_part[t][0])
                a = dve.do(lambda e: e.scalar_tensor_tensor(ms, ss1, 1.0 / D, ms, ALU.mult, ALU.add), self.m_part[t][1], a)
                a = pool.do(lambda e: e.tensor_tensor(r, ms, half_pow[:, 0:1], ALU.pow), a, m_pow)
                if t == 1 and self.src is x:
                    queue_lo(1)
                self.m_xr[t] = []
                for half in range(2):
                    cols = slice(512 * half, 512 * half + 512)
                    self.m_xr[t].append(dve.do(lambda e, cols=cols: e.scalar_tensor_tensor(
                        xr[:, t, cols], self.src[:, t, cols], r, pre_gain[:, cols], ALU.mult, ALU.mult),
                        a, self.m_gain, self.m_src[t][half]))
                if t == T - 1:
                    gain_free[0] = self.m_xr[t]

            def turn(self, t):
                i, ps, free = take_pair()
                for bank in range(2):
                    for c in range(4):
                        k = 4 * bank + c
                        done = turn(ps[:, k * P:(k + 1) * P], xr[:, t, k * P:(k + 1) * P], free, self.m_xr[t][bank], m_ident, signal=c == 3)
                    ks, cols = slice(4 * bank, 4 * bank + 4), slice(t * P, (t + 1) * P)
                    src = ps[:, bank * 512:(bank + 1) * 512].rearrange("p (k s) -> p k s", k=4)
                    m = split_whole(self.hi[:, ks, cols], self.lo[:, ks, cols], src, done)
                    for c in range(4):
                        self.marks[4 * bank + c, t] = m
                xr_free[t] = done
                give_pair(i, m, self.marks[0, t])

            def ready(self, k, t):
                return self.marks[k, t]

        class Finish:

            def __init__(self):
                pass

            def part(self, t, half, *marks):
                cols = slice(512 * half, 512 * half + 512)
                sp.dma(out[t * P:(t + 1) * P, cols], x[:, t, cols], s_out, used, list(marks))

            def stats(self, t):
                pass

            def turn(self, t):
                pass

        FF = d["ffn1_w_gate"].shape[1]
        FC = FF // P
        ff_blocks = [(n, min(512, FF - n)) for n in range(0, FF, 512)]
        IN = {"q": 0, "kv": 512, "iq": 768, "ik_iw": 1280, "mx": 1352, "mv": 1864, "mi_mf": 2376, "mo": 2384,
              "ga": 2896, "gb": 3920}
        w_in, w_in2 = d["w_in"], d["w_in_2"]

        tails = []

        def ffn_plan(gate, up, down):
            for n, nw in ff_blocks:
                plan_block(gate, DC, n, nw)
                plan_block(up, DC, n, nw)
            for n in range(0, D, 512):
                plan_block(down, FC, n, 512)
            tails.append(len(plan))

        def narrow_rows(k0, k1, n0, nw):
            v = w_in.rearrange("(k p) n -> p k n", p=P)
            return [(slice(0, P), slice(0, 256), v[:, k0:k1, IN["kv"]:IN["kv"] + 256]),
                    (slice(0, P), slice(256, 328), v[:, k0:k1, IN["ik_iw"]:IN["ik_iw"] + 72]),
                    (slice(0, P), slice(328, 336), v[:, k0:k1, IN["mi_mf"]:IN["mi_mf"] + 8])]

        def proj_a_rows(k0, k1, n0, nw):
            v = d["w_proj_a"].rearrange("(g j q) n -> g q j n", g=2, j=4)
            return [(slice(64 * g, 64 * g + 64), slice(0, nw), v[g, :, k0:k1, n0:n0 + nw]) for g in range(2)]

        ffn_plan(d["ffn1_w_gate"], d["ffn1_w_up"], d["ffn1_w_down"])
        plan_block(w_in, DC, IN["q"], 512)
        plan_block(w_in, DC, IN["kv"], 336, narrow_rows)
        plan_block(w_in, DC, IN["iq"], 512)
        for n in ("mx", "mv", "mo"):
            plan_block(w_in, DC, IN[n], 512, share=True)
        for n in ("ga", "gb"):
            for b in range(2):
                plan_block(w_in, DC, IN[n] + 512 * b, 512, share=True)
        for b in range(2):
            plan_block(d["w_proj_a"], 4, 512 * b, 512, proj_a_rows)
        for b in range(2):
            plan_block(d["w_proj_b"], 4, 512 * b, 512)
        for b, k in halves(0):
            plan_block(d["w_out"], DC, 512 * b, 512, ks=k)
        tails.append(len(plan))
        ffn_plan(d["ffn2_w_gate"], d["ffn2_w_up"], d["ffn2_w_down"])
        ffn_plan(d["ffn1_w_gate_2"], d["ffn1_w_up_2"], d["ffn1_w_down_2"])
        for k in (0, 2):
            plan_block(d["xa_wkv_2"], DC, 0, 512, ks=k)
        for b in (2, 0, 1, 3):
            plan_block(w_in2, DC, 512 * b, 512, share=b not in (0, 2))
        for k in (4, 6):
            plan_block(d["xa_wkv_2"], DC, 0, 512, ks=k)
        plan_block(d["xa_wkv_2"], DC, 512, 512)
        for b, k in halves(1):
            plan_block(d["w_out_2"], DC, 512 * b, 512, ks=k)
        tails.append(len(plan))
        plan_block(d["xa_wkv_2"], DC, 1024, 512)
        for b in range(2):
            plan_block(d["xa_wq_2"], DC, 512 * b, 512)
        plan_block(d["xa_wkv_2"], DC, 1536, 512)
        for b, k in halves(0):
            plan_block(d["xa_wo_2"], DC, 512 * b, 512, ks=k)
        tails.append(len(plan))
        ffn_plan(d["ffn2_w_gate_2"], d["ffn2_w_up_2"], d["ffn2_w_down_2"])
        for u0 in tails[:-1]:
            plan[u0 + 1] = plan[u0 + 1][:6] + (True,)
        for u in range(STAGES):
            load_unit(u)
            if u == 1:
                m_x.append(sp.dma(x[:, 1, :], d["x"][P:2 * P, :], s_x[1], used))
        state["loaded"] = STAGES

        def post_blocks(w, K, a_hi, a_lo, ready, y, gain_name, s_g, weight, nxt, m_gain_free):
            gb = gain_buf[0]
            m_gb = pool.dma(gb[:], d[gain_name].partition_broadcast(P), s_g, used, m_gain_free)
            if weight != 1.0:
                m_gb = pool.do(lambda e: e.tensor_scalar(gb[:], gb[:], weight, None, ALU.mult), m_gb)
            m_y, m_ss = {}, {}

            def evac(half):
                def run(b, done, t_only):
                    cols = slice(512 * half, 512 * half + 512)
                    for t in ([t_only] if t_only is not None else range(T)):
                        src = b.ps[:, t * 512:(t + 1) * 512]
                        ss0, ss1, ms, r = (post_stat[:, t, n:n + 1] for n in range(4))
                        m_ss[t, half] = act.do(lambda e, src=src, t=t: e.activation(
                            xr[:, t, cols], src, ACT.Square, accum_out=post_stat[:, t, half:half + 1]), done, xr_free[t])
                        if half == 0:
                            dve.do(lambda e, ms=ms, ss0=ss0: e.tensor_scalar(ms, ss0, 1.0 / D, EPS, ALU.mult, ALU.add), m_ss[t, 0])
                        else:
                            a = dve.do(lambda e, ms=ms, ss1=ss1: e.scalar_tensor_tensor(ms, ss1, 1.0 / D, ms, ALU.mult, ALU.add), m_ss[t, 1], m_y[t, 0])
                            a = pool.do(lambda e, ms=ms, r=r: e.tensor_tensor(r, ms, half_pow[:, 0:1], ALU.pow), a, m_pow)
                        m_y[t, half] = dve.do(lambda e, src=src, t=t: e.tensor_tensor(y[:, t, cols], src, gb[:, cols], ALU.mult), m_ss[t, half], m_gb)
                        if half == 0:
                            continue
                        for h in range(2):
                            c2 = slice(512 * h, 512 * h + 512)
                            m = dve.do(lambda e, t=t, r=r, c2=c2: e.scalar_tensor_tensor(
                                x[:, t, c2], y[:, t, c2], r, x[:, t, c2], ALU.mult, ALU.add), a, m_y[t, h])
                            if t_only == 1:
                                queue_hi(1)
                            nxt.part(t, h, m)
                    if t_only != 0:
                        give_pair(b.i, m_y[0, half], m_y[1, half])
                return run
            return [Block(w, K, 512 * h, 512, a_hi, a_lo, ready, "rows", evac(h)) for h in range(2)]

        def add_blocks(w, K, a_hi, a_lo, ready, weight, nxt):
            def evac(half):
                def run(b, done, t_only):
                    for t in ([t_only] if t_only is not None else range(T)):
                        xt, src = x[:, t, 512 * half:512 * half + 512], b.ps[:, t * 512:(t + 1) * 512]
                        m = dve.do(lambda e, xt=xt, src=src: e.scalar_tensor_tensor(xt, src, weight, xt, ALU.mult, ALU.add), done)
                        if t_only == 1:
                            queue_hi(2)
                        nxt.part(t, half, m)
                    if t_only != 0:
                        give_pair(b.i, m)
                return run
            return [Block(w, K, 512 * h, 512, a_hi, a_lo, ready, "rows", evac(h)) for h in range(2)]

        def ffn(n_ffn, gate, up, down, norm, make_next, post=None, late=0):
            scope = ExitStack()
            with scope:
                f_hi = sb(scope, f"f_hi{n_ffn}", [P, FC, S], F32R)
                f_lo = sb(scope, f"f_lo{n_ffn}", [P, FC, S], F32R)
                act_buf = [sb(scope, f"act_buf{n_ffn}_{i}", [P, 1024]) for i in range(2)]
                buf_free = [None, None]
                m_silu, m_f = {}, {}

                def turn_rows(s_, k, a):
                    yield
                    i, ps, free = take_pair()
                    for c in range(4):
                        for t in range(T):
                            done = turn(ps[:, c * S + t * P:c * S + (t + 1) * P], s_[:, t * 512 + c * P:t * 512 + (c + 1) * P],
                                        free, a, signal=c == 3 and t == 1)
                    m = split_whole(f_hi[:, k:k + 4, :].rearrange("p k s -> p (k s)"), f_lo[:, k:k + 4, :].rearrange("p k s -> p (k s)"),
                                    ps[:, :], done)
                    give_pair(i, m)
                    buf_free[0] = done
                    for c in range(4):
                        m_f[k + c] = m

                def evac_gate(b, done, _):
                    n = b.n0 // 512
                    w = b.nw // P * S
                    s_, ps = act_buf[n % 2][:, 0:w], b.ps[:, 0:w]
                    a = act.do(lambda e: e.activation(s_, ps, ACT.Sigmoid), done, buf_free[n % 2])
                    m_silu[n] = dve.do(lambda e: e.tensor_tensor(s_, s_, ps, ALU.mult), a)
                    give_pair(b.i, m_silu[n])

                def evac_up(b, done, _):
                    n, k = b.n0 // 512, b.n0 // P
                    w = b.nw // P * S
                    s_, ps = act_buf[n % 2][:, 0:w], b.ps[:, 0:w]
                    a = dve.do(lambda e: e.tensor_tensor(s_, s_, ps, ALU.mult), m_silu[n], done)
                    give_pair(b.i, a)
                    if b.form == "rows":
                        side_work(turn_rows(s_, k, a))
                        return
                    hi = f_hi[:, k:k + b.nw // P, :].rearrange("p k s -> p (k s)")
                    lo = f_lo[:, k:k + b.nw // P, :].rearrange("p k s -> p (k s)")
                    buf_free[n % 2] = split_whole(hi, lo, s_, a)
                    for c in range(b.nw // P):
                        m_f[k + c] = buf_free[n % 2]

                up_blocks = []
                for n, nw in ff_blocks:
                    form = "rows" if n == 0 else "cols"
                    up_blocks.append(Block(gate, DC, n, nw, h_hi, h_lo, norm.ready, form, evac_gate))
                    up_blocks.append(Block(up, DC, n, nw, h_hi, h_lo, norm.ready, form, evac_up))
                products(up_blocks, head=lambda: norm.turn(1))
                nxt = make_next()
                if post:
                    down_blocks = post_blocks(down, FC, f_hi, f_lo, m_f, post[0], post[1], post[2], 0.5, nxt, norm.marks[7, 1])
                else:
                    down_blocks = add_blocks(down, FC, f_hi, f_lo, m_f, 0.5, nxt)
                products(down_blocks, tail=nxt, late=late)
                return nxt

        def attention(name, scope, qT, kT_of, v_of, mask_ops, marks, o_hi, o_lo, sc, pt):
            nmax = sb(scope, f"nmax_{name}", [P, T, 8])
            tot = sb(scope, f"tot_{name}", [P, T, 8])
            m_p = []
            for t in range(T):
                w = P * (t + 1)
                groups = [range(4)] if t == 0 else [range(0, 2), range(2, 4)]
                for g, js in enumerate(groups):
                    n = len(js)
                    i, ps, free = take_pair()
                    for half in range(2):
                        for jj, j in enumerate(js):
                            o = ps[:, half * 512 + jj * w:half * 512 + (jj + 1) * w]
                            r = slice(64 * half, 64 * half + 64)
                            done = mm(o, qT[r, j, t * P:(t + 1) * P], kT_of(half, j)[:, 0:w], jj == 0, jj == n - 1,
                                      free, marks["q"], marks["k"], signal=half == 1 and jj == n - 1)
                    dst = sc[t][:, g * 4:g * 4 + 2 * n, :]
                    src = ps[:, :].rearrange("p (h w) -> p h w", w=w)
                    m_s = []
                    for lo_, hi_, mask in mask_ops(t, g):
                        m_s.append(dve.do(lambda e, dst=dst, src=src, lo_=lo_, hi_=hi_, mask=mask: e.scalar_tensor_tensor(
                            dst[:, lo_:hi_, :], src[:, lo_:hi_, :], 0.125, mask, ALU.mult, ALU.add), done, marks[f"mask{t}"]))
                    give_pair(i, *m_s)
                    h0 = g * 4
                    nm = nmax[:, t, h0:h0 + 2 * n]
                    a = dve.do(lambda e, nm=nm, dst=dst: e.tensor_reduce(nm, dst, AX_X, ALU.max, negate=True), m_s)
                    for h in range(2 * n):
                        b = act.do(lambda e, h=h, dst=dst, t=t, h0=h0: e.activation(
                            dst[:, h, :], dst[:, h, :], ACT.Exp, bias=nmax[:, t, h0 + h:h0 + h + 1],
                            accum_out=tot[:, t, h0 + h:h0 + h + 1]), a)
                    tt = tot[:, t, h0:h0 + 2 * n]
                    b = dve.do(lambda e, tt=tt: e.reciprocal(tt, tt), b)
                    m_p.append(dve.do(lambda e, dst=dst, tt=tt, n=n, w=w: e.tensor_tensor(dst, dst, bcast(tt, 2, w), ALU.mult), b))
                    yield
            pt_free, turned = [None] * 4, {}
            io, po, ofree = take_pair()
            begun = set()
            for j in range(5):
                if j < 4:
                    i, ps, free = take_pair()
                    at0, at1 = (j, 4 + j), ((j // 2) * 4 + j % 2, (j // 2) * 4 + 2 + j % 2)
                    for half in range(2):
                        o = half * 512
                        turn(ps[:, o:o + P], sc[0][:, at0[half], :], free, m_p[0], m_p[1 + j // 2])
                        turn(ps[:, o + P:o + 2 * P], sc[1][:, at1[half], 0:P])
                        done = turn(ps[:, o + 2 * P:o + 3 * P], sc[1][:, at1[half], P:2 * P], signal=True)
                        b, src = 2 * (j % 2) + half, ps[:, o:o + 384]
                        turned[j, half] = act.do(lambda e, b=b, src=src: e.copy(pt[b], src), done, pt_free[b])
                    give_pair(i, turned[j, 0], turned[j, 1])
                for half in range(2 if j else 0):
                    q, b = j - 1, 2 * ((j - 1) % 2) + half
                    o = po[64 * half:64 * half + 64, q * S:(q + 1) * S]
                    key = (q // 2, half)
                    mm(o, v_of(0, half, q), pt[b][:, 0:S], key not in begun, False, turned[q, half], ofree, marks["v"])
                    begun.add(key)
                    pt_free[b] = mm(o[:, P:S], v_of(1, half, q), pt[b][:, S:384], False, True, signal=True)
                if j < 4:
                    yield 1
            a = act.do(lambda e: e.copy(o_hi, po[:, :]), pt_free)
            b = dve.do(lambda e: e.tensor_tensor(o_lo, po[:, :], o_hi.bitcast(F32), ALU.subtract), a)
            give_pair(io, a, b)
            marks["out"] = [a, b]

        def mixer1(norm, make_next):
            m_x = norm.m_xr[1]
            scope = ExitStack()
            with scope:
                ya_hi, ya_lo = sb(scope, "ya_hi", [P, 4, S], F32R), sb(scope, "ya_lo", [P, 4, S], F32R)
                yb_hi, yb_lo = sb(scope, "yb_hi", [P, 4, S], F32R), sb(scope, "yb_lo", [P, 4, S], F32R)
                xpad = sb(scope, "xpad", [P, 4, S + 3])
                mv, mo = sb(scope, "mv", [P, T, 512]), sb(scope, "mo", [P, T, 512])
                kvn = sb(scope, "kvn", [P, T, 336])
                ga, gb = sb(scope, "ga", [P, DC, S]), sb(scope, "gb", [P, DC, S])
                w_mq, w_mk = sb(scope, "w_mq", [P, 4, 64]), sb(scope, "w_mk", [P, 4, 64])
                head_g = sb(scope, "head_g", [P, 512])
                chunked = sb(scope, "chunked", [P, 2 * P])
                q_raw = sb(scope, "q_raw", [P, T, 512])
                q_nrm = sb(scope, "q_nrm", [P, T, 640])
                rr = sb(scope, "rr", [P, 22])
                ikk = sb(scope, "ikk", [P, T, 2, 64])
                qT, kT, ikT = sb(scope, "qT", [P, 4, S]), sb(scope, "kT", [P, S]), sb(scope, "ikT", [P, S])
                iqT = sb(scope, "iqT", [P, 4, S])
                work = [sb(scope, f"work{t}", [P, P * (t + 1)]) for t in range(T)]
                top = sb(scope, "top", [P, 8])
                big = sb(scope, "big", [P, 2 * 1024])
                mq, mk = sb(scope, "mq", [P, 2, S]), sb(scope, "mk", [P, 2, S])
                dm = [sb(scope, f"dm{t}", [P, 4, P * (t + 1)]) for t in range(T)]
                mt, nmt, ft, den = (sb(scope, n_, [P, T, 4]) for n_ in ("mt", "nmt", "ft", "den"))
                wt = [sb(scope, f"wt{i}", [P, 384]) for i in range(2)]
                rh = sb(scope, "rh", [P, T * 4])
                xc, sg = xr[:, 0, :].rearrange("p (c s) -> p c s", c=4), xr[:, 1, :].rearrange("p (c s) -> p c s", c=4)
                gi, gf, gt, ones = (xr[0:4, 1, n_ * S:(n_ + 1) * S] for n_ in range(4))
                s_m = s_small["mix1"]
                pool.dma(chunked[:], const("chunked"), s_m, used, m_x)
                pool.dma(head_g[:], d["m_head_norm"].partition_broadcast(P), s_m, used)
                pool.dma(w_mq[:], d["w_mq"].rearrange("h c q -> c h q"), s_m, used)
                m_const = pool.dma(w_mk[:], d["w_mk"].rearrange("h c q -> c h q"), s_m, used)
                m_zero = pool.do(lambda e: e.memset(xpad[:, :, 0:3], 0.0))
                m = {}
                flat = lambda ap: ap.rearrange("p t n -> p (t n)")

                def evac(name, out_ap, func=ACT.Copy, view=lambda ps: ps[:, :]):
                    def run(b, done, _):
                        m[name] = act.do(lambda e: e.activation(out_ap, view(b.ps), func), done, m_x)
                        give_pair(b.i, m[name])
                    return run

                def attention_chain():
                    while "kvn" not in m:
                        yield
                    rik, sq_ik, ik = rr[:, 20:22], ikk[:, :, 0, :], kvn[:, :, 256:320]
                    a = dve.do(lambda e: e.tensor_tensor(sq_ik, ik, ik, ALU.mult), m["kvn"])
                    a = dve.do(lambda e: e.tensor_reduce(rik, sq_ik, AX_X, ALU.add), a)
                    a = inverse_root(rik, rik, 2, 64, a)
                    m_ikk = [dve.do(lambda e, c=c: e.tensor_tensor(ikk[:, :, c, :], ik, bcast(rik, 2, 64), ALU.mult), a) for c in range(2)]
                    qn = q_nrm[:, :, 0:512]
                    k_raw, kn = kvn[:, :, 0:128], q_nrm[:, :, 512:640]
                    a = dve.do(lambda e: e.tensor_tensor(qn, q_raw[:], q_raw[:], ALU.mult), m["q"])
                    b = dve.do(lambda e: e.tensor_tensor(kn, k_raw, k_raw, ALU.mult))
                    for t in range(T):
                        c = dve.do(lambda e, t=t: e.tensor_reduce(rr[:, t * 10:t * 10 + 10], q_nrm[:, t, :].rearrange("p (g q) -> p g q", q=64), AX_X, ALU.add), a, b)
                    m_rr = inverse_root(rr[:, 0:20], rr[:, 0:20], 20, 64, c)
                    yield
                    i, ps, free = take_pair()
                    for t in range(T):
                        done = turn(ps[:, t * P:(t + 1) * P], ikk[:, t, :, :].rearrange("p c q -> p (c q)"), free, m_ikk, signal=t == 1)
                    m_ik = dve.do(lambda e, ps=ps: e.tensor_scalar(ikT[:], ps[:, 0:S], col("idx_k_norm"), None, ALU.mult), done)
                    give_pair(i, m_ik)
                    m_n = []
                    for u in range(T):
                        src = q_raw[:, u, :].rearrange("p (g j q) -> p g j q", g=2, j=4)
                        dst = q_nrm[:, u, 0:512].rearrange("p (j g q) -> p g j q", g=2, j=4)
                        r = rr[:, u * 10:u * 10 + 8].rearrange("p (g j) -> p g j", g=2)
                        m_n.append(dve.do(lambda e, src=src, dst=dst, r=r: e.tensor_tensor(dst, src, bcast(r, 3, 64), ALU.mult), m_rr))
                        src, r = kvn[:, u, 0:128].rearrange("p (g q) -> p g q", q=64), rr[:, u * 10 + 8:u * 10 + 10]
                        dst = q_nrm[:, u, 512:640].rearrange("p (g q) -> p g q", q=64)
                        m_n.append(dve.do(lambda e, src=src, dst=dst, r=r: e.tensor_tensor(dst, src, bcast(r, 2, 64), ALU.mult)))
                    while "iq" not in m:
                        yield
                    yield
                    n_relu, relu_free, m_top = 0, [None, None], None
                    for t in range(T):
                        w = P * (t + 1)
                        a = None
                        for js in ([range(4)] if t == 0 else [range(0, 2), range(2, 4)]):
                            i, ps, free = take_pair()
                            for half in range(2):
                                for jj, j in enumerate(js):
                                    r = slice(64 * half, 64 * half + 64)
                                    done = mm(ps[:, half * 512 + jj * w:half * 512 + (jj + 1) * w], iqT[r, j, t * P:(t + 1) * P],
                                              ikT[r, 0:w], jj == 0, jj == len(js) - 1, free, m["iq"], m_ik,
                                              signal=half == 1 and jj == len(js) - 1)
                            rb = big[:, 1024 * (n_relu % 2):1024 * (n_relu % 2) + 1024]
                            m_scored = done
                            m_r = act.do(lambda e, rb=rb, ps=ps: e.activation(rb, ps[:, :], ACT.Relu), done, relu_free[n_relu % 2])
                            give_pair(i, m_r)
                            for half in range(2):
                                for jj, j in enumerate(js):
                                    head = 2 * j + half
                                    src, iw = rb[:, half * 512 + jj * w:half * 512 + (jj + 1) * w], kvn[:, t, 320 + head:321 + head]
                                    if a is None:
                                        a = dve.do(lambda e, src=src, iw=iw, t=t: e.tensor_scalar(work[t][:], src, iw, None, ALU.mult), m_r)
                                    else:
                                        a = dve.do(lambda e, src=src, iw=iw, t=t: e.scalar_tensor_tensor(
                                            work[t][:], src, iw, work[t][:], ALU.mult, ALU.add), m_r, a)
                            relu_free[n_relu % 2] = a
                            n_relu += 1
                            yield
                        mask = chunked[:, P:2 * P] if t == 0 else chunked[:, :]
                        a = dve.do(lambda e, t=t, mask=mask: e.scalar_tensor_tensor(
                            work[t][:], work[t][:], (64 ** -0.5) * (8 ** -0.5), mask, ALU.mult, ALU.add), a, m_const)
                        for n in range(TOPK // 8):
                            a = dve.do(lambda e, t=t: e.max(top[:], work[t][:]), a, m_top)
                            a = m_top = dve.do(lambda e, t=t: e.match_replace(work[t][:], top[:], work[t][:], PICKED), a)
                            if t == 1 and n == 3:
                                yield
                        m[f"mask{t}"] = dve.do(lambda e, t=t: e.tensor_scalar(
                            work[t][:], work[t][:], (PICKED + UNPICKED) / 2, MASKED, ALU.is_gt, ALU.mult), a)
                        if t == 0:
                            i, ps, free = take_pair()
                            for j in range(4):
                                for u in range(T):
                                    done = turn(ps[:, j * S + u * P:j * S + (u + 1) * P], q_nrm[:, u, j * P:(j + 1) * P], free, m_n, signal=j == 3 and u == 1)
                            m["aq"] = act.do(lambda e, ps=ps: e.activation(qT[:].rearrange("p j s -> p (j s)"), ps[:, :], ACT.Copy, scale=col("q_norm")), done)
                            give_pair(i, m["aq"])
                            i, ps, free = take_pair()
                            for u in range(T):
                                done = turn(ps[:, u * P:(u + 1) * P], q_nrm[:, u, 512:640], free, signal=u == 1)
                            m["ak"] = act.do(lambda e, ps=ps: e.activation(kT[:], ps[:, 0:S], ACT.Copy, scale=col("k_norm")), done)
                            give_pair(i, m["ak"])
                            m_q_turned = done
                    yield
                    marks = {"q": m["aq"], "k": m["ak"], "v": m["kvn"], "mask0": m["mask0"], "mask1": [m["mask1"], a]}
                    ptv = q_nrm[:].rearrange("p t n -> p (t n)")
                    pe_free = [m_q_turned, m_scored]
                    act.wait(pe_free)
                    dve.wait(pe_free)
                    yield from attention("a", scope, qT, lambda half, j: kT[64 * half:64 * half + 64, :],
                                         lambda st, half, j: kvn[:, st, 128 + 64 * half:192 + 64 * half],
                                         lambda t, g: [(0, 8 if t == 0 else 4, bcast(work[t][:], 1, 8 if t == 0 else 4))], marks,
                                         ya_hi[:].rearrange("p c s -> p (c s)"), ya_lo[:].rearrange("p c s -> p (c s)"),
                                         [q_raw[:].rearrange("p t n -> p (t n)").rearrange("p (h w) -> p h w", h=8), big[:].rearrange("p (h w) -> p h w", h=8)],
                                         [ptv[:, 0:384], ptv[:, 384:768], iqT[:, 0:2, :].rearrange("p j s -> p (j s)")[:, 0:384],
                                          iqT[:, 2:4, :].rearrange("p j s -> p (j s)")[:, 0:384]])
                    m["ya"] = marks["out"]

                def mlstm_chain():
                    order = (0, 2, 1, 3)
                    while "kvn" not in m:
                        yield
                    yield
                    i, ps, free = take_pair()
                    for t in range(T):
                        turn(ps[0:4, t * P:(t + 1) * P], kvn[:, t, 328:332], free, m["kvn"])
                        done = turn(ps[0:4, 512 + t * P:512 + (t + 1) * P], kvn[:, t, 332:336], signal=t == 1)
                    m_gi = dve.do(lambda e, ps=ps: e.tensor_scalar(gi, ps[0:4, 0:S], col("b_i", 0, 4), None, ALU.add), done, norm.marks[7, 1], xr_free)
                    a0 = dve.do(lambda e, ps=ps: e.tensor_scalar(gf, ps[0:4, 512:512 + S], col("b_f", 0, 4), None, ALU.add), done)
                    give_pair(i, m_gi, a0)
                    a = act.do(lambda e: e.activation(gt, gf, ACT.Abs), a0)
                    a = act.do(lambda e: e.activation(gt, gt, ACT.Exp, scale=-1.0), a)
                    a = act.do(lambda e: e.activation(gt, gt, ACT.Ln, bias=1.0), a)
                    yield
                    a = dve.do(lambda e: e.scalar_tensor_tensor(gt, gf, 0.0, gt, ALU.min, ALU.subtract), a)
                    b = dve.do(lambda e: e.memset(ones, 1.0))
                    m_F = dve.do(lambda e: e.tensor_tensor_scan(gf, ones, gt, 0.0, ALU.mult, ALU.add), a, b)
                    m_G = dve.do(lambda e: e.tensor_tensor(gi, gi, gf, ALU.subtract), m_F, m_gi)
                    yield
                    i, ps, free = take_pair()
                    for t in range(T):
                        m_turned = turn(ps[:, 4 * t:4 * t + 4], gf[:, t * P:(t + 1) * P], free, m_F, signal=t == 1)
                    m_ft = act.do(lambda e, ps=ps: e.copy(ft[:].rearrange("p t (half pair) -> p t half pair", half=2),
                                                          ps[:, 0:8].rearrange("p (t pair half) -> p t half pair", t=T, half=2)), m_turned, m_x)
                    give_pair(i, m_ft)
                    i, ps, free = take_pair()
                    for n, h in enumerate(order):
                        m_spread = mm(ps[:, n * S:(n + 1) * S], ident[0:4, h:h + 1].to_broadcast([4, P]), gi, n % 2 == 0, n % 2 == 1,
                                      free, m_G, signal=n == 3)
                    gps = ps[:, :].rearrange("p (h s) -> p h s", h=4)
                    m_d, m_e = [], []
                    for t in range(T):
                        w = P * (t + 1)
                        mask = causal[:, P:2 * P] if t == 0 else causal[:, :]
                        m_d.append(dve.do(lambda e, t=t, w=w, mask=mask, gps=gps: e.tensor_tensor(dm[t][:], gps[:, :, 0:w], bcast(mask, 1, 4), ALU.add), m_spread, m_par))
                    give_pair(i, m_d)
                    for t in range(T):
                        a = dve.do(lambda e, t=t: e.tensor_reduce(mt[:, t, :], dm[t][:], AX_X, ALU.max), m_d)
                        m_m = dve.do(lambda e, t=t: e.tensor_scalar(mt[:, t, :], mt[:, t, :], 0.0, None, ALU.max), a)
                        a = dve.do(lambda e, t=t: e.tensor_scalar(nmt[:, t, :], mt[:, t, :], -1.0, None, ALU.mult), m_m)
                        for h in range(4):
                            b = act.do(lambda e, t=t, h=h: e.activation(dm[t][:, h, :], dm[t][:, h, :], ACT.Exp, bias=nmt[:, t, h:h + 1]), a)
                        m_e.append(b)
                    a = dve.do(lambda e: e.tensor_tensor(ft[:], ft[:], mt[:], ALU.add), m_ft, m_m)
                    m_floor = act.do(lambda e: e.activation(ft[:], ft[:], ACT.Exp, scale=-1.0), a)
                    while "mx" not in m:
                        yield
                    yield
                    m_c = []
                    for c in range(4):
                        a = dve.do(lambda e, c=c: e.tensor_scalar(xc[:, c, :], xpad[:, c, 0:S], col("conv_w", c), col("conv_b", c), ALU.mult, ALU.add),
                                   m["mx"], m_zero)
                        for j in range(1, 4):
                            a = dve.do(lambda e, c=c, j=j: e.scalar_tensor_tensor(
                                xc[:, c, :], xpad[:, c, j:j + S], col("conv_w", 4 * j + c), xc[:, c, :], ALU.mult, ALU.add), a)
                        m_c.append(a)
                        if c % 2:
                            yield
                    a = act.do(lambda e: e.activation(sg, xc, ACT.Sigmoid), m_c, m_turned, m_spread)
                    m_xc = dve.do(lambda e: e.tensor_tensor(xc, xc, sg, ALU.mult), a)
                    yield 4
                    for w_m, dst, scale in ((w_mq, mq, 0.125), (w_mk, mk, 1.0)):
                        i, ps, free = take_pair()
                        for h in range(4):
                            half, pair = h % 2, h // 2
                            done = mm(ps[64 * half:64 * half + 64, pair * S:(pair + 1) * S], w_m[:, h, :], xc[:, h, :], pair == 0, pair == 1,
                                      free, m_xc, m_const, signal=h == 3)
                        m_qk = act.do(lambda e, dst=dst, ps=ps, scale=scale: e.activation(
                            dst[:].rearrange("p h s -> p (h s)"), ps[:, 0:512], ACT.Copy, scale=scale), done)
                        give_pair(i, m_qk)
                    yield
                    m_w = []
                    for t in range(T):
                        w = P * (t + 1)
                        i, ps, free = take_pair()
                        for n, h in enumerate(order):
                            half, pair = n // 2, n % 2
                            r = slice(64 * half, 64 * half + 64)
                            done = mm(ps[:, half * 512 + pair * w:half * 512 + (pair + 1) * w], mq[r, pair, t * P:(t + 1) * P], mk[r, pair, 0:w],
                                      pair == 0, pair == 1, free, m_qk, signal=n == 3)
                        for half in range(2):
                            src = ps[:, half * 512:half * 512 + 2 * w].rearrange("p (h s) -> p h s", h=2)
                            o = dm[t][:, 2 * half:2 * half + 2, :]
                            a = dve.do(lambda e, o=o, src=src: e.tensor_tensor(o, o, src, ALU.mult), done, m_e[t])
                        give_pair(i, a)
                        m_w.append(a)
                        if t == 0:
                            yield
                        m_den = dve.do(lambda e, t=t: e.tensor_reduce(den[:, t, :], dm[t][:], AX_X, ALU.add), a)
                    yield
                    a = act.do(lambda e: e.activation(den[:], den[:], ACT.Abs), m_den)
                    a = dve.do(lambda e: e.tensor_tensor(den[:], den[:], ft[:], ALU.max), a, m_floor)
                    m_den = dve.do(lambda e: e.reciprocal(den[:], den[:]), a)
                    while "mv" not in m:
                        yield
                    ih, ph, hfree = take_pair()
                    wt_free = [None, None]
                    for n, h in enumerate(order):
                        i, ps, free = take_pair()
                        turn(ps[:, 0:P], dm[0][:, n, :], free, m_w)
                        turn(ps[:, P:2 * P], dm[1][:, n, 0:P])
                        done = turn(ps[:, 2 * P:3 * P], dm[1][:, n, P:2 * P], signal=True)
                        b = n % 2
                        if b:
                            c = act.do(lambda e, b=b, ps=ps: e.copy(wt[b][:], ps[:, 0:384]), done, wt_free[b])
                        else:
                            c = dve.do(lambda e, b=b, ps=ps: e.tensor_copy(wt[b][:], ps[:, 0:384]), done, wt_free[b])
                        give_pair(i, c)
                        if n % 2:
                            yield
                        for nn in ((n - 1, n) if n % 2 else ()):
                            hh, bb = order[nn], nn % 2
                            cw = [prev_c, c][bb]
                            mm(ph[:, hh * P:(hh + 1) * P], wt[bb][:, 0:P], mv[:, 0, hh * P:(hh + 1) * P], nn == 0, nn == 3, cw, hfree, m["mv"])
                            mm(ph[:, 512 + hh * P:512 + (hh + 1) * P], wt[bb][:, P:2 * P], mv[:, 0, hh * P:(hh + 1) * P], nn == 0, False)
                            wt_free[bb] = mm(ph[:, 512 + hh * P:512 + (hh + 1) * P], wt[bb][:, 2 * P:3 * P], mv[:, 1, hh * P:(hh + 1) * P], False, nn == 3, signal=True)
                        prev_c = c
                    while "mo" not in m:
                        yield
                    m_mog = pool.do(lambda e: e.tensor_tensor(mo[:], mo[:], bcast(head_g[:], 1, T), ALU.mult), m["mo"], m_const)
                    hv, sv = (ap.rearrange("p c s -> p (c s)").rearrange("p (t q) -> p t q", t=T) for ap in (xc, sg))
                    h4 = lambda ap: ap.rearrange("p t (h q) -> p t h q", h=4)
                    a = []
                    for t in range(T):
                        dn = den[:, t, :].rearrange("p (half pair) -> p pair half", half=2)
                        o, src = xc.rearrange("p c s -> p (c s)")[:, t * 512:(t + 1) * 512], ph[:, t * 512:(t + 1) * 512]
                        a.append(dve.do(lambda e, o=o, src=src, dn=dn: e.tensor_tensor(
                            o.rearrange("p (pair half q) -> p pair half q", half=2, q=P), src.rearrange("p (pair half q) -> p pair half q", half=2, q=P),
                            bcast(dn, 3, P), ALU.mult), wt_free, m_den, m_qk))
                    give_pair(ih, a)
                    hm, s2 = xc.rearrange("p c s -> p (c s)"), sg.rearrange("p c s -> p (c s)")
                    g8 = lambda ap: ap.rearrange("p (g q) -> p g q", q=P)
                    a = dve.do(lambda e: e.tensor_tensor(s2, hm, hm, ALU.mult), a)
                    a = dve.do(lambda e: e.tensor_reduce(rh[:], g8(s2), AX_X, ALU.add), a)
                    m_rh = inverse_root(rh[:], rh[:], T * 4, P, a)
                    yield
                    a = dve.do(lambda e: e.tensor_tensor(g8(hm), g8(hm), bcast(rh[:], 2, P), ALU.mult), m_rh)
                    m_hm = dve.do(lambda e: e.tensor_tensor(hm, hm, flat(mo[:]), ALU.mult), a, m_mog)
                    yield
                    i, ps, free = take_pair()
                    for h in range(4):
                        for t in range(T):
                            done = turn(ps[:, h * S + t * P:h * S + (t + 1) * P], hm[:, t * 512 + h * P:t * 512 + (h + 1) * P], free, m_hm, signal=h == 3 and t == 1)
                    m["yb"] = split_whole(yb_hi[:].rearrange("p c s -> p (c s)"), yb_lo[:].rearrange("p c s -> p (c s)"), ps[:, :], done)
                    give_pair(i, m["yb"])
                    xr_free[0] = xr_free[1] = done

                B = lambda name, n0, nw, form, ev: Block(w_in, DC, n0, nw, h_hi, h_lo, norm.ready, form, ev)
                products([B("q", IN["q"], 512, "rows", evac("q", flat(q_raw[:])))], head=lambda: norm.turn(1))
                chain_a, chain_m = attention_chain(), mlstm_chain()
                side_work(chain_a)
                side_work(chain_m, 1)
                cols4 = lambda ap: ap.rearrange("p c s -> p (c s)")
                products([
                    B("kvn", IN["kv"], 336, "rows", evac("kvn", kvn[:], view=lambda ps: ps[:, :].rearrange("p (t n) -> p t n", t=T)[:, :, 0:336])),
                    B("iq", IN["iq"], 512, "cols", evac("iq", cols4(iqT[:]))),
                    B("mx", IN["mx"], 512, "cols", evac("mx", xpad[:, :, 3:3 + S], view=lambda ps: ps[:, :].rearrange("p (c s) -> p c s", c=4))),
                    B("mv", IN["mv"], 512, "rows", evac("mv", flat(mv[:]))),
                    B("mo", IN["mo"], 512, "rows", evac("mo", flat(mo[:]), ACT.Sigmoid))] +
                    [B(n_, IN[n_] + 512 * b, 512, "cols", evac((n_, b), cols4(g[:, 4 * b:4 * b + 4, :]), ACT.Sigmoid))
                     for n_, g in (("ga", ga), ("gb", gb)) for b in range(2)])
                drain(chain_a)

                def evac_gated(name, g):
                    def run(b, done, _):
                        h = b.n0 // 512
                        gv = cols4(g[:, 4 * h:4 * h + 4, :])
                        m[name, h] = dve.do(lambda e: e.tensor_tensor(gv, gv, b.ps[:, :], ALU.mult), done, m["g" + name, h])
                        give_pair(b.i, m[name, h])
                        if name == "b":
                            av = cols4(ga[:, 4 * h:4 * h + 4, :])
                            a = dve.do(lambda e: e.tensor_tensor(av, av, gv, ALU.add), m["a", h], m["b", h])
                            s_ = split_whole(cols4(h_hi[:, 4 * h:4 * h + 4, :]), cols4(h_lo[:, 4 * h:4 * h + 4, :]), av, a, m["gb", 1])
                            for c in range(4):
                                m_merged[4 * h + c] = s_
                    return run
                m_merged = {}
                products([Block(d["w_proj_a"], 4, 512 * b, 512, ya_hi, ya_lo, [m["ya"]] * 4, "cols", evac_gated("a", ga)) for b in range(2)])
                drain()
                products([Block(d["w_proj_b"], 4, 512 * b, 512, yb_hi, yb_lo, [m["yb"]] * 4, "cols", evac_gated("b", gb)) for b in range(2)])
                nxt = make_next()
                out_blocks = add_blocks(d["w_out"], DC, h_hi, h_lo, m_merged, 1.0, nxt)
                products(out_blocks, steps=in_halves(out_blocks, 0), tail=nxt)
                return nxt

        def memory_blocks(hi, lo, ready, xk, xv):
            m_kv = {}

            def evac(n):
                def run(b, done, _):
                    if n < 2:
                        o, src = xk[:, 4 * n:4 * n + 4, :].rearrange("p c s -> p (c s)"), b.ps[:, :]
                    else:
                        o, src = xv[:, :, 512 * (n - 2):512 * (n - 1)], b.ps[:, :].rearrange("p (t n) -> p t n", t=T)
                    m_kv[n] = act.do(lambda e: e.copy(o, src), done)
                    give_pair(b.i, m_kv[n])
                return run
            return [Block(d["xa_wkv_2"], DC, 512 * n, 512, hi, lo, ready, "cols" if n < 2 else "rows", evac(n)) for n in range(4)], m_kv

        def mixer2(norm, y, kv, make_next):
            m_x = norm.m_xr[1]
            scope = ExitStack()
            with scope:
                alibi = sb(scope, "alibi", [P, 2, 2, 2, S])
                qT, kT = sb(scope, "qT2", [P, 4, S]), sb(scope, "kT2", [P, 4, S])
                v = sb(scope, "v2", [P, T, 512])
                sc = [sb(scope, f"sc2_{t}", [P, 8, P * (t + 1)]) for t in range(T)]
                pt = [sb(scope, f"pt2_{i}", [P, 384]) for i in range(4)]
                L = 16 + S
                win = [sb(scope, "win0", [P, 4, L]), y[:].rearrange("p t n -> p (t n)")[:, 0:4 * L].rearrange("p (g s) -> p g s", g=4)]
                pin, inv = (xr[:, n_, :].rearrange("p (g s) -> p g s", g=4) for n_ in range(2))
                pw = sb(scope, "pw", [P, 4, P])
                m_alibi = pool.dma(alibi[:].rearrange("p a b c s -> p (a b c s)"), const("alibi"), s_small["alibi"], used, m_x)
                m_zero = pool.do(lambda e: e.memset(win[0][:, :, 0:16], 0.0))
                m = {}

                def evac(name, out_ap):
                    def run(b, done, _):
                        m[name] = act.do(lambda e: e.copy(out_ap, b.ps[:, :]), done, m_x)
                        give_pair(b.i, m[name])
                    return run

                def evac_pool(b, done, _):
                    src = b.ps[:, :].rearrange("p (g s) -> p g s", g=4)
                    m1 = act.do(lambda e: e.copy(win[0][:, :, 16:L], src), done)
                    m["pin"] = [m1, act.do(lambda e: e.copy(pin, src), xr_free)]
                    give_pair(b.i, m["pin"])

                def pool_chain():
                    while "pin" not in m:
                        yield
                    m_inv = pool.dma(inv.rearrange("p g s -> p (g s)"), const("inv_count"), s_small["pooling"], used, xr_free)
                    m_inv = pool.dma(pw[:], d["pool_w_2"].rearrange("g c n -> c g n"), s_small["pooling"], used)
                    last = [m["pin"], m_zero]
                    m_sums = []
                    for g in range(4):
                        src, dst = win[g % 2], win[(g + 1) % 2]
                        sh, first = 2 ** g, (1, 4, 8, 16)[g]
                        last = [pool.do(lambda e, src=src, dst=dst, sh=sh, first=first, g=g: e.tensor_tensor(
                            dst[:, g:4, first:L], src[:, g:4, first:L], src[:, g:4, first - sh:L - sh], ALU.add), *last)]
                        m_sums.append(last)
                    yield
                    for g in range(4):
                        dst = win[(g + 1) % 2]
                        a = pool.do(lambda e, dst=dst, g=g: e.tensor_tensor(inv[:, g, :], dst[:, g, 16:L], inv[:, g, :], ALU.mult), m_sums[g], m_inv)
                        m_dev = pool.do(lambda e, g=g: e.tensor_tensor(pin[:, g, :], inv[:, g, :], pin[:, g, :], ALU.subtract), a, m["pin"])
                    yield
                    while "passed" not in m:
                        yield
                    i, ps, free = take_pair()
                    for g in range(4):
                        done = mm(ps[:, g * S:(g + 1) * S], pw[:, g, :], pin[:, g, :], g % 2 == 0, g % 2 == 1, free, m_dev, m_inv, signal=g == 3)
                    xr_free[0] = xr_free[1] = done
                    ms = split_gained(h_hi[:, 4:8, :], h_lo[:, 4:8, :], ps, [col("pool_scale_2", g) for g in range(4)], [done, done])
                    for g in range(4):
                        m_cat[4 + g] = ms[g]
                    give_pair(i, *ms)

                def attention_chain():
                    while "k" not in m:
                        yield 1
                    yield 1
                    marks = {"q": m["q"], "k": m["k"], "v": m["v"], "mask0": m_alibi, "mask1": m_alibi}

                    def mask_ops(t, g):
                        if t == 1:
                            return [(0, 4, alibi[:, g].rearrange("p b c s -> p (b c) s"))]
                        return [(half * 4 + gg * 2, half * 4 + gg * 2 + 2, alibi[:, gg, half, :, P:2 * P]) for half in range(2) for gg in range(2)]
                    yield from attention("m", scope, qT, lambda half, j: kT[64 * half:64 * half + 64, j, :],
                                         lambda st, half, j: v[:, st, (2 * j + half) * 64:(2 * j + half) * 64 + 64], mask_ops, marks,
                                         h_hi[:, 0:4, :].rearrange("p c s -> p (c s)"), h_lo[:, 0:4, :].rearrange("p c s -> p (c s)"), sc, [p_[:] for p_ in pt])
                    for c in range(4):
                        m_cat[c] = marks["out"]

                m_cat = {}
                blocks, m_kv = kv
                cols4 = lambda ap: ap.rearrange("p c s -> p (c s)")
                keys = [(b, k0, k1) for b in blocks[0:2] for k0, k1 in b.units]
                products(blocks[0:1], steps=keys[0:2])
                side_work(attention_chain())
                side_work(pool_chain(), 1)
                B = lambda b, form, ev: Block(w_in2, DC, 512 * b, 512, h_hi, h_lo, norm.ready, form, ev)
                products([B(2, "rows", evac("v", cols4(v[:])))], head=lambda: norm.turn(1))
                products([B(0, "cols", evac("q", cols4(qT[:]))), B(1, "cols", evac("k", cols4(kT[:]))), B(3, "cols", evac_pool)])
                m["passed"] = True
                products(blocks[0:2], steps=keys[2:])
                while 4 not in m_cat:
                    tick(every=True)
                nxt = make_next()
                out_blocks = post_blocks(d["w_out_2"], DC, h_hi, h_lo, m_cat, y, "mix_post_g_2", s_small["post1"], 1.0, nxt, m_cat[7])
                steps = in_halves(out_blocks, 1)
                products(out_blocks, steps=steps[0:2])
                products(out_blocks, steps=steps[2:], tail=nxt, late=1)
                return nxt

        def cross(norm, y, xk, xv, kv, make_next):
            scope = ExitStack()
            with scope:
                xq = sb(scope, "xq", [P, DC, S])
                pr = sb(scope, "pr", [P, T, 4, S])
                nmax = sb(scope, "nmax_x", [P, T, 4])
                tot = sb(scope, "tot_x", [P, T, 4])
                pt = [sb(scope, f"ptx{i}", [P, 512]) for i in range(4)]
                blocks, m_kv = kv
                m_q = []

                def evac_q(b, done, _):
                    c = b.n0 // P
                    m_q.append(act.do(lambda e: e.copy(xq[:, c:c + 4, :].rearrange("p c s -> p (c s)"), b.ps[:, :]), done))
                    give_pair(b.i, m_q[-1])

                def attention_chain():
                    m_p, turned, pt_free = {}, {}, [None] * 4

                    def scores(hp):
                        i, ps, free = take_pair()
                        m_e = []
                        for t in range(T):
                            for n in range(2):
                                for c in range(2):
                                    ch = 2 * (2 * hp + n) + c
                                    done = mm(ps[:, t * 512 + n * S:t * 512 + (n + 1) * S], xq[:, ch, t * P:(t + 1) * P], xk[:, ch, :],
                                              n == 0 and c == 0, n == 1 and c == 1, free, m_q[hp], m_kv[hp], signal=n == 1 and c == 1)
                            pv_ = ps[:, t * 512:(t + 1) * 512].rearrange("p (h s) -> p h s", h=2)
                            nm, tt = nmax[:, t, 2 * hp:2 * hp + 2], tot[:, t, 2 * hp:2 * hp + 2]
                            a = dve.do(lambda e, nm=nm, pv_=pv_: e.tensor_reduce(nm, pv_, AX_X, ALU.max, negate=True), done)
                            a = dve.do(lambda e, nm=nm: e.tensor_scalar(nm, nm, 1.0 / 16, None, ALU.mult), a)
                            for n in range(2):
                                h = 2 * hp + n
                                b = act.do(lambda e, t=t, h=h, n=n, pv_=pv_: e.activation(pr[:, t, h, :], pv_[:, n, :], ACT.Exp, bias=nmax[:, t, h:h + 1],
                                           scale=1.0 / 16, accum_out=tot[:, t, h:h + 1]), a)
                            m_e.append(b)
                            b = dve.do(lambda e, tt=tt: e.reciprocal(tt, tt), b)
                            m_p[hp, t] = dve.do(lambda e, t=t, tt=tt: e.tensor_tensor(
                                pr[:, t, 2 * hp:2 * hp + 2], pr[:, t, 2 * hp:2 * hp + 2], bcast(tt, 2, S), ALU.mult), b)
                        give_pair(i, m_e)

                    def turn_heads(hp):
                        i, ps, free = take_pair()
                        for n in range(2):
                            h = 2 * hp + n
                            for mt in range(2):
                                for t in range(T):
                                    o = n * 512 + mt * S + t * P
                                    done = turn(ps[:, o:o + P], pr[:, t, h, mt * P:(mt + 1) * P], free, m_p[hp, t], signal=mt == 1 and t == 1)
                            src = ps[:, n * 512:(n + 1) * 512]
                            turned[h] = act.do(lambda e, h=h, src=src: e.copy(pt[h][:], src), done)
                        give_pair(i, turned[2 * hp], turned[2 * hp + 1])

                    def weigh(hp):
                        io, po, ofree = take_pair()
                        for n in range(2):
                            h = 2 * hp + n
                            for dd in range(2):
                                o = po[:, (2 * n + dd) * S:(2 * n + dd + 1) * S]
                                for mt in range(2):
                                    done = mm(o, xv[:, mt, (2 * h + dd) * P:(2 * h + dd + 1) * P], pt[h][:, mt * S:(mt + 1) * S],
                                              dd == 0 and mt == 0, dd == 1 and mt == 1, turned[h], ofree, m_kv[2 + hp], signal=dd == 1 and mt == 1)
                        c4 = slice(4 * hp, 4 * hp + 4)
                        s_ = split_whole(h_hi[:, c4, :].rearrange("p c s -> p (c s)"), h_lo[:, c4, :].rearrange("p c s -> p (c s)"), po[:, :], done)
                        give_pair(io, s_)
                        for c in range(4):
                            m_o[4 * hp + c] = s_

                    for hp in range(2):
                        while len(m_q) < hp + 1:
                            yield 1
                        yield 1
                        scores(hp)
                        yield 1
                    yield 1
                    turn_heads(0)
                    yield
                    weigh(0)
                    turn_heads(1)
                    yield
                    weigh(1)

                m_o = {}
                products(blocks[2:3], then=lambda: norm.turn(1))
                side_work(attention_chain())
                products([Block(d["xa_wq_2"], DC, 512 * b, 512, h_hi, h_lo, norm.ready, "cols", evac_q) for b in range(2)])
                products(blocks[3:4])
                while 0 not in m_o:
                    tick(every=True)
                nxt = make_next()
                out_blocks = post_blocks(d["xa_wo_2"], DC, h_hi, h_lo, m_o, y, "xa_post_g_2", s_small["post2"], 1.0, nxt, m_q)
                steps = in_halves(out_blocks, 0)
                products(out_blocks, steps=steps[0:2])
                products(out_blocks, steps=steps[2:], tail=nxt)
                return nxt

        def next_norm(gain):
            return lambda: Norm(x, gain, h_hi, h_lo)

        n = Norm(x, "ffn1_norm", h_hi, h_lo, m_first_gain)
        for half in range(2):
            n.part(0, half, m_x[0])
        n.stats(0)
        queue_splits(1)
        n.turn(0)
        queue_splits(1)
        for half in range(2):
            n.part(1, half, m_x[1])
        n.stats(1)
        n = ffn(0, d["ffn1_w_gate"], d["ffn1_w_up"], d["ffn1_w_down"], n, next_norm("mix_norm"))
        n = mixer1(n, next_norm("ffn2_norm"))
        n = ffn(1, d["ffn2_w_gate"], d["ffn2_w_up"], d["ffn2_w_down"], n, next_norm("ffn1_pre_g_2"))
        second = ExitStack()
        with second:
            y = sb(second, "y", [P, T, D])
            xk, xv = sb(second, "xk", [P, DC, S]), sb(second, "xv", [P, T, D])
            gain_buf.append(sb(second, "gain", [P, D]))
            memory = ExitStack()
            with memory:
                mem_hi, mem_lo = sb(memory, "mem_hi", [P, DC, S], F32R), sb(memory, "mem_lo", [P, DC, S], F32R)
                for t in range(T):
                    m_mem = pool.dma(y[:, t, :], d["mem_2"][t * P:(t + 1) * P, :], s_small["mem"], used, n.m_xr[0])
                got = {}

                def norm_memory():
                    for _ in range(6):
                        yield
                    mem = got["mem"] = Norm(y, "mem_g_2", mem_hi, mem_lo)
                    for t in range(T):
                        for half in range(2):
                            mem.part(t, half, m_mem)
                    yield
                    for t in range(T):
                        mem.stats(t)
                        yield
                    for t in range(T):
                        mem.turn(t)
                        yield
                side_work(norm_memory())
                n = ffn(2, d["ffn1_w_gate_2"], d["ffn1_w_up_2"], d["ffn1_w_down_2"], n, next_norm("mix_pre_g_2"),
                        (y, "ffn1_post_g_2", s_small["post0"]), late=1)
                kv = memory_blocks(mem_hi, mem_lo, got["mem"].ready, xk, xv)
                n = mixer2(n, y, kv, next_norm("xa_pre_g_2"))
                n = cross(n, y, xk, xv, kv, next_norm("ffn2_pre_g_2"))
            ffn(3, d["ffn2_w_gate_2"], d["ffn2_w_up_2"], d["ffn2_w_down_2"], n, Finish, (y, "ffn2_post_g_2", s_small["post3"]))
        sp.wait((s_out, used[id(s_out)]))
        assert state["next"] == len(plan)

        blk = ctx.enter_context(nc.Block())
        blk.tensor(pe.run)
        blk.scalar(act.run)
        blk.vector(dve.run)
        blk.gpsimd(pool.run)
        blk.sync(sp.run)


_MATS = ["ffn1_w_gate", "ffn1_w_up", "ffn1_w_down", "w_in", "w_mq", "w_mk", "w_proj_a", "w_proj_b", "w_out",
         "ffn2_w_gate", "ffn2_w_up", "ffn2_w_down", "ffn1_w_gate_2", "ffn1_w_up_2", "ffn1_w_down_2", "w_in_2",
         "pool_w_2", "w_out_2", "xa_wq_2", "xa_wkv_2", "xa_wo_2", "ffn2_w_gate_2", "ffn2_w_up_2", "ffn2_w_down_2",
         "x", "mem_2"]
_ROWS = ["ffn1_norm", "mix_norm", "ffn2_norm", "ffn1_pre_g_2", "mix_pre_g_2", "mem_g_2", "xa_pre_g_2", "ffn2_pre_g_2",
         "m_head_norm", "ffn1_post_g_2", "mix_post_g_2", "xa_post_g_2", "ffn2_post_g_2"]


def kernel(**inputs):
    import concourse.bacc as bacc
    from concourse.bass_utils import run_bass_kernel_spmd

    nc = bacc.Bacc("TRN2", target_bir_lowering=False, num_devices=1)
    arrays, d = {}, {}

    def declare(name, a):
        a = np.ascontiguousarray(a)
        arrays["in_" + name] = a
        d[name] = nc.dram_tensor("in_" + name, a.shape, mybir.dt.from_np(a.dtype), kind="ExternalInput").ap()

    for name in _MATS:
        declare(name, np.asarray(inputs[name])[0])
    for name in _ROWS:
        declare(name, np.asarray(inputs[name])[0])
    par = np.zeros((P, N_PARAMS), np.float32)
    for name, (a, b) in PARAM_COLS.items():
        v = np.asarray(inputs[name])[0]
        if name in ("q_norm", "k_norm", "idx_k_norm"):
            par[0:64, a], par[64:128, a] = v, v
        elif name in ("b_i", "b_f"):
            par[0:4, a] = v
        else:
            par[:, a:b] = v.reshape(b - a, P).T
    declare("params", par)
    declare("consts", shape_constants())
    out = nc.dram_tensor("out", (S, D), F32, kind="ExternalOutput").ap()
    build(nc, d, out)
    r = run_bass_kernel_spmd(nc, [arrays], core_ids=[0])
    return r.results[0]["out"].reshape(1, S, D)
```
